# Optimizing a Trainium2 kernel written in Bass

```python
import jax, jax.numpy as jnp
from jax import lax
import numpy as np

D_MODEL = 1024
BATCH = 1
SEQ = 1024
DEPTH = 1
DEC_BATCH = 8
DEC_SEQ = 16
PAST_LEN = 256

CHUNK = 64
HGRN_BLOCK = CHUNK // 4
A_HEADS = 4
A_DK = 128
A_DV = 128
A_WIDTH = A_HEADS * A_DV
B_WIDTH = D_MODEL // 2
CONV_W = 3
D_FF = 2816
N_IN = 4 * A_WIDTH + 3 * B_WIDTH
EPS = 1e-6

kernel_name = 'hybrid_hgrn2_shortconv_convffn_stream_step'

def rmsnorm(x, g):
    xf = x.astype(jnp.float32)
    y = xf * lax.rsqrt(jnp.mean(xf * xf, axis=-1, keepdims=True) + EPS)
    return (y * g.astype(jnp.float32)).astype(x.dtype)

def causal_dwconv(u, buf, w):
    L = u.shape[1]
    full = jnp.concatenate([buf.astype(u.dtype), u], axis=1)
    y = full[:, 0:L] * w[0]
    for k in range(1, CONV_W):
        y = y + full[:, k:k + L] * w[k]
    return y, full[:, -(CONV_W - 1):]

def hgrn_lower_bounds(lb_logits):
    p = jax.nn.softmax(lb_logits.astype(jnp.float32), axis=0)
    g = jnp.cumsum(p, axis=0)
    return g - g[0:1]

def hgrn_block(S, q, k, v, logf):
    L = q.shape[1]
    b = jnp.cumsum(logf, axis=1)
    o_inter = jnp.einsum('blhk,bhkv->blhv', q * jnp.exp(b), S)
    causal = (jnp.arange(L)[:, None] >= jnp.arange(L)[None, :])[None, :, :, None, None]
    decay = jnp.exp(jnp.where(causal, b[:, :, None] - b[:, None, :], -jnp.inf))
    A = jnp.einsum('btshk,bthk->btsh', decay * k[:, None], q)
    o_intra = jnp.einsum('btsh,bshv->bthv', A, v)
    b_last = b[:, -1]
    kd = k * jnp.exp(b_last[:, None] - b)
    S_new = jnp.exp(b_last)[..., None] * S + jnp.einsum('blhk,blhv->bhkv', kd, v)
    return S_new, o_inter + o_intra

def hgrn_scan(S0, q, k, v, logf):
    B, T = q.shape[:2]
    nb = T // HGRN_BLOCK

    def to_blocks(a):
        return a.reshape(B, nb, HGRN_BLOCK, *a.shape[2:]).swapaxes(0, 1)

    def step(S, blk):
        return hgrn_block(S, *blk)

    S, o = lax.scan(step, S0, (to_blocks(q), to_blocks(k), to_blocks(v), to_blocks(logf)))
    return S, o.swapaxes(0, 1).reshape(B, T, *o.shape[3:])

def token_mixer(h, S0, conv_buf, lb, w_in, a_norm, w_pa, conv_w, w_pb, w_bgate, w_o):
    B, L, _ = h.shape
    a, bw = A_WIDTH, B_WIDTH
    q, f, i, g, bg, cg, xv = jnp.split(h @ w_in, [a, 2 * a, 3 * a, 4 * a, 4 * a + bw, 4 * a + 2 * bw], axis=-1)
    shp = (B, L, A_HEADS, A_DK)
    qa = jax.nn.silu(q.astype(jnp.float32)).reshape(shp)
    z = f.astype(jnp.float32).reshape(shp)
    lbh = lb.reshape(A_HEADS, A_DK)
    logf = jnp.logaddexp(jnp.log(lbh), jnp.log1p(-lbh) + jax.nn.log_sigmoid(z))
    ka = (1.0 - lbh) * jax.nn.sigmoid(-z)
    va = i.astype(jnp.float32).reshape(B, L, A_HEADS, A_DV)
    S0 = S0.astype(jnp.float32)
    if L > CHUNK:
        S, o = hgrn_scan(S0, qa, ka, va, logf)
    else:
        S, o = hgrn_block(S0, qa, ka, va, logf)
    o = rmsnorm(o, a_norm) * jax.nn.silu(g.astype(jnp.float32).reshape(B, L, A_HEADS, A_DV))
    y_a = o.reshape(B, L, A_WIDTH).astype(h.dtype) @ w_pa
    u, new_buf = causal_dwconv(cg * xv, conv_buf, conv_w)
    y_b = (bg * u) @ w_pb
    ga, gb = jnp.split(jax.nn.sigmoid(h @ w_bgate), 2, axis=-1)
    return (ga * y_a + gb * y_b) @ w_o, S, new_buf

def conv_ffn(h, buf, w_up, conv_w, w_down):
    gate, val = jnp.split(h @ w_up, 2, axis=-1)
    gate, new_buf = causal_dwconv(gate, buf, conv_w)
    return (jax.nn.silu(gate) * val) @ w_down, new_buf

def trunk(x, c, S_in, cb_in, fb_in, lbs, params):
    (w_ada, b_ada, g_pre_mix, g_post_mix, g_pre_ffn, g_post_ffn, w_in, a_norm, w_pa,
     conv_w, w_pb, w_bgate, w_o, w_up, ffn_conv_w, w_down) = params
    cs = jax.nn.silu(c)
    new_S, new_cb, new_fb = [], [], []
    for l in range(DEPTH):
        ada = cs @ w_ada[l] + b_ada[l]
        sh1, sc1, gt1, sh2, sc2, gt2 = jnp.split(ada[:, None, :], 6, axis=-1)
        h = rmsnorm(x, g_pre_mix[l]) * (1.0 + sc1) + sh1
        m, S, cb = token_mixer(h, S_in[l], cb_in[l], lbs[l], w_in[l], a_norm[l], w_pa[l],
                               conv_w[l], w_pb[l], w_bgate[l], w_o[l])
        x = x + gt1 * rmsnorm(m, g_post_mix[l])
        h = rmsnorm(x, g_pre_ffn[l]) * (1.0 + sc2) + sh2
        ff, fb = conv_ffn(h, fb_in[l], w_up[l], ffn_conv_w[l], w_down[l])
        x = x + gt2 * rmsnorm(ff, g_post_ffn[l])
        new_S.append(S)
        new_cb.append(cb)
        new_fb.append(fb)
    return x, jnp.stack(new_S).astype(x.dtype), jnp.stack(new_cb), jnp.stack(new_fb)

def setup_inputs(seed: int = 0) -> dict:
    key = jax.random.key(seed)
    ks = jax.random.split(key, 32)
    D = D_MODEL

    def nrm(k, shape, scale):
        return jax.random.normal(k, shape, jnp.float32) * scale

    return {
        'x_prompt': nrm(ks[0], (BATCH, SEQ, D), 1.0),
        'x_sample': nrm(ks[1], (DEC_BATCH, DEC_SEQ, D), 1.0),
        'state_hgrn': nrm(ks[2], (DEPTH, DEC_BATCH, A_HEADS, A_DK, A_DV), 0.5),
        'state_conv': nrm(ks[3], (DEPTH, DEC_BATCH, CONV_W - 1, B_WIDTH), 1.0),
        'state_ffn_conv': nrm(ks[4], (DEPTH, DEC_BATCH, CONV_W - 1, D_FF), 1.0),
        'c_prompt': nrm(ks[5], (BATCH, D), 1.0),
        'c_sample': nrm(ks[6], (DEC_BATCH, D), 1.0),
        'w_ada': nrm(ks[7], (DEPTH, D, 6 * D), 0.5 * D ** -0.5),
        'b_ada': nrm(ks[8], (DEPTH, 6 * D), 0.02),
        'g_pre_mix': 1.0 + nrm(ks[9], (DEPTH, D), 0.05),
        'g_post_mix': 1.0 + nrm(ks[10], (DEPTH, D), 0.05),
        'g_pre_ffn': 1.0 + nrm(ks[11], (DEPTH, D), 0.05),
        'g_post_ffn': 1.0 + nrm(ks[12], (DEPTH, D), 0.05),
        'w_in': nrm(ks[13], (DEPTH, D, N_IN), D ** -0.5),
        'hgrn_lb_logits': nrm(ks[14], (DEPTH, A_WIDTH), 1.0),
        'hgrn_norm': 1.0 + nrm(ks[15], (DEPTH, A_DV), 0.05),
        'w_pa': nrm(ks[16], (DEPTH, A_WIDTH, D), A_WIDTH ** -0.5),
        'conv_w': nrm(ks[17], (DEPTH, CONV_W, B_WIDTH), CONV_W ** -0.5),
        'w_pb': nrm(ks[18], (DEPTH, B_WIDTH, D), B_WIDTH ** -0.5),
        'w_bgate': nrm(ks[19], (DEPTH, D, 2 * D), D ** -0.5),
        'w_o': nrm(ks[20], (DEPTH, D, D), D ** -0.5),
        'w_up': nrm(ks[21], (DEPTH, D, 2 * D_FF), D ** -0.5),
        'ffn_conv_w': nrm(ks[22], (DEPTH, CONV_W, D_FF), CONV_W ** -0.5),
        'w_down': nrm(ks[23], (DEPTH, D_FF, D), D_FF ** -0.5),
    }

def reference(x_prompt, x_sample, state_hgrn, state_conv, state_ffn_conv, c_prompt, c_sample,
              w_ada, b_ada, g_pre_mix, g_post_mix, g_pre_ffn, g_post_ffn, w_in, hgrn_lb_logits,
              hgrn_norm, w_pa, conv_w, w_pb, w_bgate, w_o, w_up, ffn_conv_w, w_down):
    params = (w_ada, b_ada, g_pre_mix, g_post_mix, g_pre_ffn, g_post_ffn, w_in, hgrn_norm, w_pa,
              conv_w, w_pb, w_bgate, w_o, w_up, ffn_conv_w, w_down)
    lbs = hgrn_lower_bounds(hgrn_lb_logits)
    B = x_prompt.shape[0]
    dt = x_prompt.dtype
    S0 = jnp.zeros((DEPTH, B, A_HEADS, A_DK, A_DV), jnp.float32)
    cb0 = jnp.zeros((DEPTH, B, CONV_W - 1, B_WIDTH), dt)
    fb0 = jnp.zeros((DEPTH, B, CONV_W - 1, D_FF), dt)
    y_prompt, s_hgrn_p, s_conv_p, s_ffn_p = trunk(x_prompt, c_prompt, S0, cb0, fb0, lbs, params)
    y_sample, s_hgrn_s, s_conv_s, s_ffn_s = trunk(x_sample, c_sample, state_hgrn, state_conv,
                                                  state_ffn_conv, lbs, params)
    return (y_prompt, y_sample, s_hgrn_p, s_conv_p, s_ffn_p, s_hgrn_s, s_conv_s, s_ffn_s)


_drawn_inputs = setup_inputs


def setup_inputs(seed=0):
    import zlib

    import numpy as np

    out = dict(_drawn_inputs(seed))
    spreads = {}
    factors = {'state_hgrn': 8.0, 'g_post_mix': 3.64, 'g_post_ffn': 4.1, 'hgrn_norm': 5.395}
    for name, (base, spread) in spreads.items():
        noise = np.random.default_rng([zlib.crc32(name.encode()), seed]).standard_normal(out[name].shape)
        drawn = base * np.exp(spread * noise) if base else spread * noise
        out[name] = __import__('jax').numpy.asarray(drawn.astype(out[name].dtype))
    for name, factor in factors.items():
        out[name] = (out[name] * factor).astype(out[name].dtype)
    return out
```

```python
from contextlib import ExitStack

import concourse.bass as bass
from concourse import mybir

P = 128
F32 = mybir.dt.float32
F32R = mybir.dt.float32r
U32 = mybir.dt.uint32
ALU = mybir.AluOpType
ACT = mybir.ActivationFunctionType
NEG_HUGE = -3.0e38
LN_FLOOR = 2.0 ** -63
EPS = 1e-6


class Link:

    def __init__(self, eng, sem, base=0):
        self.eng, self.sem, self.base, self.n = eng, sem, base, 0

    def __call__(self, ins):
        self.n += 1
        ins.then_inc(self.sem, 1)
        self.eng.wait_ge(self.sem, self.base + self.n)


def build_trunk(nc, io):
    NP_, D = io["x_prompt"].shape[1:]
    NB, LS = io["x_sample"].shape[:2]
    DFF = io["w_down"].shape[1]
    AW = io["w_pa"].shape[1]
    BW = io["w_pb"].shape[1]
    H = AW // P
    T = NP_ + NB * LS
    KD = D // P
    KF = DFF // P
    KB = BW // P
    NT = T // P
    NPT = NP_ // P
    NG, G = 3, T // 3
    C = NB + 1
    HALF = D // 2
    assert NB * LS == P and G <= 512 and io["state_hgrn"].shape[0] == 1 and KF % 2 == 0
    assert NG * G == T and 2 * G <= NP_ < 3 * G and H == KB == 4 and H * P == 512
    REST = NP_ - 2 * G

    w_in, w_bgate, w_up = io["w_in"][0], io["w_bgate"][0], io["w_up"][0]

    gate_scratch = nc.dram_tensor("gate_rows_scratch", (2, C, D), F32, kind="Internal").ap()
    x1_scratch = nc.dram_tensor("x_after_mixer_scratch", (T, D), F32, kind="Internal").ap()

    top = ExitStack()
    sems, parts = {}, [1]

    def sem(name):
        if name not in sems:
            sems[name] = nc.alloc_semaphore(f"{name}_part{parts[0]}")
        return sems[name]

    def new_semaphores():
        nc.clear_and_free_semaphores(list(sems.values()))
        sems.clear()
        parts[0] += 1
        nc.all_engine_barrier()

    def hold(sp, name, value):
        sp.wait_ge(sem(name), value)
        sp.sem_inc(sem("sp_passed"), 1)

    def sb(ctx, name, shape, dt=F32):
        return ctx.enter_context(nc.sbuf_tensor(name, shape, dt))

    def pb(ctx, name, shape):
        return ctx.enter_context(nc.psum_tensor(name, shape, F32))

    def f32(ap):
        return ap.bitcast(F32)

    PASSES = ((0, 0), (0, 1), (1, 0))
    SLOTS = 2

    def give_slots(eng, names):
        for name in names:
            eng.sem_inc(sem(name), SLOTS)

    def pairs(eng, count, body):
        with eng.Fori(0, count // 2, 1) as i:
            for s in range(2):
                body(i, s)

    class WeightStream:

        def __init__(self, ctx, name, psum=None):
            self.name = name
            self.raw = sb(ctx, name + "_raw", [P, 2, KD * P])
            self.halves = sb(ctx, name + "_halves", [P, 2, 2, KD * P], F32R)
            self.psum = psum

        def start(self, eng):
            give_slots(eng, [self.name + x for x in ("_lo", "_mm")])
            for s in range(2):
                eng.sem_inc(sem(f"{self.name}_pfree{s}"), 1)

        def load(self, sp, u, s, src):
            k = src.shape[0] // P
            hold(sp, self.name + "_lo", u * 2 + s + 1)
            sp.dma_start(self.raw[:, s, 0:k * P].rearrange("p (k m) -> p k m", m=P),
                         src.rearrange("(k p) m -> p k m", p=P)).then_inc(sem(f"{self.name}_in{s}"), 16)

        def split(self, pool, u, s, k):
            n = u * 2 + s
            raw, hi, lo = self.raw[:, s, :k * P], self.halves[:, s, 0, :k * P], self.halves[:, s, 1, :k * P]
            pool.wait_ge(sem(f"{self.name}_in{s}"), u * 16 + 16)
            pool.wait_ge(sem(self.name + "_mm"), n + 1)
            pool.tensor_tensor(hi, raw, ones[:, 0:1].to_broadcast([P, k * P]), ALU.mult).then_inc(sem(self.name + "_hi"), 1)
            pool.wait_ge(sem(self.name + "_hi"), n + 1)
            pool.tensor_tensor(lo, raw, f32(hi), ALU.subtract).then_inc(sem(self.name + "_lo"), 1)

        def product(self, pe, u, s, k, moving, out=None):
            n = u * 2 + s
            out = self.psum[s] if out is None else out
            pe.wait_ge(sem(self.name + "_lo"), n + 3)
            pe.wait_ge(sem(f"{self.name}_pfree{s}"), u + 1)
            for g in range(NG):
                for j, (a, b) in enumerate(PASSES):
                    for kt in range(k):
                        last = pe.matmul(out[:, g, 0:G], self.halves[:, s, a, kt * P:(kt + 1) * P],
                                         moving[:, b, kt, g * G:(g + 1) * G],
                                         start=(j == 0 and kt == 0), stop=(j == 2 and kt == k - 1))
            last.then_inc(sem(self.name + "_mm"), 1)

        def arrived(self, eng, u, s):
            eng.wait_ge(sem(self.name + "_mm"), u * 2 + s + 3)

    def groups(ps):
        return ps[:, :, 0:G]

    def by_group(ap):
        return ap.rearrange("p (g t) -> p g t", t=G)

    with top:
        ident = sb(top, "ident", [P, P])
        ones = sb(top, "ones", [P, P])
        eps = sb(top, "eps", [P, 1])
        cols = sb(top, "param_cols", [P, 6 * P])
        scale1 = sb(top, "scale1", [P, KD, C])
        shift1 = sb(top, "shift1", [P, KD, C])
        scale2 = sb(top, "scale2", [P, KD, C])
        shift2 = sb(top, "shift2", [P, KD, C])
        log_lb = sb(top, "log_lower_bound", [P, H])
        log_1mlb = sb(top, "log_one_minus_lb", [P, H])
        new_conv = sb(top, "new_conv", [P, 2 * NB * KB + 2 * KB])
        new_ffn = sb(top, "new_ffn", [P, 2 * NB * KF + 2 * KF])
        h = sb(top, "h", [P, 2, KD, T], F32R)
        M = sb(top, "middle", [P, KD, T])

        def modulate(dve, name, u, s, pT, full, scale, shift, sample=False):
            t = u * 2 + s
            buf = full[:, s % full.shape[1], :].rearrange("p (k t) -> p k t", t=P)
            src = pT[:, s].rearrange("p a (k t) -> p (a k) t", t=P)
            if sample:
                view = lambda ap: ap.rearrange("p k (b l) -> p k b l", l=LS)
                sc, sh = (m[:, :, 1:C].unsqueeze(3).to_broadcast([P, KD, NB, LS]) for m in (scale, shift))
            else:
                view = lambda ap: ap
                sc, sh = (m[:, :, 0:1].to_broadcast([P, KD, P]) for m in (scale, shift))
            dve.wait_ge(sem(name + "_xT"), t + 3)
            dve.wait_ge(sem(name + "_lo"), t + (2 if full.shape[1] == 1 else 1))
            dve.tensor_tensor(view(buf), view(src), sc, ALU.mult).then_inc(sem(name + "_pT"), 1)
            dve.wait_ge(sem(name + "_pT"), t + 3)
            dve.tensor_tensor(view(buf), view(buf), sh, ALU.add).then_inc(sem(name + "_h"), 1)

        def halves_of_h(pool, name, u, s, full):
            t = u * 2 + s
            tok = bass.ds(t * P, P)
            buf = full[:, s % full.shape[1], :].rearrange("p (k t) -> p k t", t=P)
            pool.wait_ge(sem(name + "_h"), t + 1)
            pool.tensor_tensor(h[:, 0, :, tok], buf, ones[:, 0:1].unsqueeze(1).to_broadcast([P, KD, P]), ALU.mult) \
                .then_inc(sem(name + "_hi"), 1)
            pool.wait_ge(sem(name + "_hi"), t + 1)
            pool.tensor_tensor(h[:, 1, :, tok], buf, f32(h[:, 0, :, tok]), ALU.subtract).then_inc(sem(name + "_lo"), 1)

        def conv3(dve, link, U, Us, y, w):
            ys = y[:, NP_:].rearrange("p (b t) -> p b t", t=LS)
            for out, u, n in ((y[:, 0:NP_], U[:, :], NP_), (ys, Us[:, :, :], LS)):
                tap = lambda d: u[..., d:d + n]
                link(dve.tensor_scalar(out, tap(0), w[0], None, ALU.mult))
                link(dve.scalar_tensor_tensor(out, tap(1), w[1], out, ALU.mult, ALU.add))
                link(dve.scalar_tensor_tensor(out, tap(2), w[2], out, ALU.mult, ALU.add))

        def transposes(pe, name, u, s, xn, pT):
            t = u * 2 + s
            pe.wait_ge(sem(name + "_xn"), t + 1)
            pe.wait_ge(sem(name + "_pT"), t + 1)
            for k in range(KD):
                last = pe.transpose(pT[:, s, k // 4, (k % 4) * P:(k % 4 + 1) * P], xn[:, s % xn.shape[1], k * P:(k + 1) * P],
                                    ident[:, :])
            last.then_inc(sem(name + "_xT"), 1)

        o_bada, o_fcw, o_gmix = 0, 6 * KD, 6 * KD + 3 * KF
        o_gffn = P
        o_cw = o_gffn + KD
        o_an = o_cw + 3 * KB
        o_lb = o_an + 1
        o_c = o_lb + H
        o_fst = 2 * P
        n_fst = 2 * NB * KF
        o_cst = 5 * P
        n_cst = 2 * NB * KB
        stack_rows = [o_gmix + KD, o_c + C * KD - P, P, P, n_fst - 2 * P, n_cst]
        assert max(stack_rows) <= P

        def state_ffn_cols(f):
            return cols[:, o_fst:o_fst + n_fst].rearrange("p (bw f) -> p f bw", f=KF)[:, f]

        ctx = ExitStack()
        with ctx:
            rows = sb(ctx, "param_rows", [P, 6, P])
            cs = sb(ctx, "silu_c", [P, C * KD])
            wada = (sb(ctx, "w_ada_section", [P, KD, D])[:, :, :], M[:, :, 0:D])
            brow = sb(ctx, "gate_bias_row", [C, 2, D])
            gpost = sb(ctx, "gate_post_row", [C, 2, D])
            grow = sb(ctx, "gate_row", [C, 2, D])
            tiny = sb(ctx, "lb_steps", [P, 8, H])
            xt = sb(ctx, "x_tile", [P, 2, D])
            xn = sb(ctx, "x_normed", [P, 2, D])
            junk = sb(ctx, "squares", [P, D])
            stat = sb(ctx, "stat", [P, 2, 4])
            hf = sb(ctx, "h_full", [P, 2, D])
            pcol = pb(ctx, "p_cols", [P, 2, 512])
            pada = pb(ctx, "p_ada", [P, 2, 512])
            pT = pb(ctx, "p_xT", [P, 2, 2, 512])
            SECTIONS = [1, 0, 4, 3, 2, 5]
            FM = 4
            cs_k = cs[:, :].rearrange("p (c k) -> p k c", k=KD)
            xp_dram = io["x_prompt"][0]
            xs_dram = io["x_sample"].rearrange("b l d -> (b l) d")
            N_ROWS_IN = 13

            with nc.Block() as block:
                @block.sync
                def _(sp):
                    give_slots(sp, ["in_xT", "in_pT", "in_lo"])

                    def rows_in(stack, r, src):
                        sp.dma_start(rows[r:r + src.shape[0], stack, :], src).then_inc(sem("rows_in"), 16)

                    rows_in(1, o_c - P, io["c_prompt"].rearrange("b (k p) -> (b k) p", p=P))
                    rows_in(1, o_c - P + KD, io["c_sample"].rearrange("b (k p) -> (b k) p", p=P))
                    rows_in(1, 0, io["g_pre_ffn"].rearrange("a (k p) -> (a k) p", p=P))
                    rows_in(1, o_cw - P, io["conv_w"].rearrange("a w (k p) -> (a w k) p", p=P))
                    rows_in(1, o_an - P, io["hgrn_norm"])
                    rows_in(1, o_lb - P, io["hgrn_lb_logits"].rearrange("a (k p) -> (a k) p", p=P))
                    rows_in(0, o_bada, io["b_ada"].rearrange("a (k p) -> (a k) p", p=P))
                    rows_in(0, o_fcw, io["ffn_conv_w"].rearrange("a w (k p) -> (a w k) p", p=P))
                    rows_in(0, o_gmix, io["g_pre_mix"].rearrange("a (k p) -> (a k) p", p=P))
                    fst = io["state_ffn_conv"].rearrange("a b w (k p) -> (a b w k) p", p=P)
                    for n in range(3):
                        rows_in(2 + n, 0, fst[n * P:min((n + 1) * P, n_fst), :])
                    rows_in(5, 0, io["state_conv"].rearrange("a b w (k p) -> (a b w k) p", p=P))
                    for n, s in enumerate(SECTIONS):
                        if n >= 2:
                            sp.wait_ge(sem("ada_mm"), n - 1)
                        sp.dma_start(wada[n % 2], io["w_ada"][0, :, s * D:(s + 1) * D]
                                     .rearrange("(k p) n -> p k n", p=P)).then_inc(sem(f"wada_in{n % 2}"), 16)
                    for n in range(2):
                        sp.wait_ge(sem("grow_ready"), n + 1)
                        sp.dma_start(gate_scratch[n], grow[:, n, :]).then_inc(sem("grow_out"), 16)
                    sp.wait_ge(sem("grow_out"), 32)

                @block.gpsimd
                def _(pool):
                    pool.memset(ident[:, :], 0.0).then_inc(sem("ident_zero"), 1)
                    pool.memset(ones[:, :], 1.0).then_inc(sem("consts"), 1)
                    pool.memset(eps[:, :], EPS).then_inc(sem("consts"), 1)
                    pool.wait_ge(sem("ident_zero"), 1)
                    pool.affine_select(out=ident[:, :], in_=ident[:, :], compare_op=ALU.not_equal, fill=1.0,
                                       base=0, pattern=[[-1, P]], channel_multiplier=1).then_inc(sem("ident"), 1)
                    pairs(pool, NPT, lambda u, s: halves_of_h(pool, "in", u, s, hf))
                    halves_of_h(pool, "in", NPT // 2, 0, hf)

                @block.scalar
                def _(act):
                    for n in range(2):
                        act.dma_start(brow[:, n, :], io["b_ada"][:, (2 + 3 * n) * D:(3 + 3 * n) * D]
                                      .to_broadcast([C, D])).then_inc(sem("brow_in"), 16)
                        act.dma_start(gpost[:, n, :], (io["g_post_mix"], io["g_post_ffn"])[n]
                                      .to_broadcast([C, D])).then_inc(sem("brow_in"), 16)
                    act.dma_start(xt[:, 0], xp_dram[0:P, :]).then_inc(sem("x_in0"), 16)
                    act.wait_ge(sem("cols"), 6)
                    act.activation(cs[:, :], cols[:, o_c:o_c + C * KD], ACT.Silu).then_inc(sem("cs"), 1)
                    act.wait_ge(sem("lb_shifted"), 1)
                    act.activation(tiny[:, 1], tiny[:, 0], ACT.Exp).then_inc(sem("lb_exp"), 1)
                    act.wait_ge(sem("lb_ready"), 1)
                    act.activation(log_1mlb[:, :], tiny[:, 5], ACT.Ln).then_inc(sem("lb_logs"), 1)
                    act.activation(tiny[:, 7], tiny[:, 6], ACT.Ln).then_inc(sem("lb_logs"), 1)
                    act.wait_ge(sem("consts"), 2)

                    def norm(u, s, following):
                        t = u * 2 + s
                        if following is not None:
                            act.wait_ge(sem("in_xn"), t)
                            act.dma_start(xt[:, 1 - s], following).then_inc(sem(f"x_in{1 - s}"), 16)
                        act.wait_ge(sem(f"x_in{s}"), u * 16 + 16)
                        link = Link(act, sem("in_norm"), t * 3)
                        link(act.activation(junk[:, :], xt[:, s], ACT.Square, accum_out=stat[:, s, 0:1]))
                        link(act.activation(stat[:, s, 1:2], stat[:, s, 0:1], ACT.Ln, scale=1.0 / D, bias=eps[:, :]))
                        link(act.activation(stat[:, s, 2:3], stat[:, s, 1:2], ACT.Exp, scale=-0.5))
                        act.wait_ge(sem("in_xT"), t + 1)
                        act.activation(xn[:, s], xt[:, s], ACT.Copy, scale=stat[:, s, 2:3]).then_inc(sem("in_xn"), 1)

                    with act.Fori(0, NPT // 2 - 1, 1) as i:
                        for s in range(2):
                            norm(i, s, xp_dram[bass.ds((i * 2 + s + 1) * P, P), :])
                    norm(NPT // 2 - 1, 0, xp_dram[(NPT - 1) * P:, :])
                    norm(NPT // 2 - 1, 1, xs_dram)
                    norm(NPT // 2, 0, None)

                @block.vector
                def _(dve):
                    dve.wait_ge(sem("rows_T"), 1)
                    for n, r in enumerate(stack_rows):
                        dve.tensor_copy(cols[:, n * P:n * P + r], pcol[:, n // 4, (n % 4) * P:(n % 4) * P + r]) \
                            .then_inc(sem("cols"), 1)
                    dve.wait_ge(sem("cols"), 6)
                    lg = cols[:, o_lb:o_lb + H]
                    link = Link(dve, sem("lb_step"))
                    dve.tensor_tensor(tiny[:, 0], lg, lg, ALU.subtract).then_inc(sem("lb_shifted"), 1)
                    dve.wait_ge(sem("lb_exp"), 1)
                    link(dve.reciprocal(tiny[:, 2], tiny[:, 1]))
                    link(dve.tensor_tensor(tiny[:, 3], tiny[:, 1], tiny[:, 2], ALU.mult))
                    link(dve.tensor_tensor(tiny[:, 4], tiny[:, 3], tiny[:, 3], ALU.subtract))
                    link(dve.tensor_scalar(tiny[:, 5], tiny[:, 4], -1.0, 1.0, ALU.mult, ALU.add))
                    link(dve.tensor_scalar(tiny[:, 6], tiny[:, 4], LN_FLOOR, None, ALU.max))
                    dve.tensor_scalar(log_lb[:, :], tiny[:, 4], 0.0, NEG_HUGE, ALU.is_le, ALU.mult) \
                        .then_inc(sem("lb_ready"), 1)
                    dve.wait_ge(sem("lb_ready"), 1)
                    dve.wait_ge(sem("lb_logs"), 2)
                    dve.tensor_tensor(log_lb[:, :], log_lb[:, :], tiny[:, 7], ALU.add).then_inc(sem("lb_ready"), 1)

                    bada = cols[:, o_bada:o_bada + 6 * KD].rearrange("p (s k) -> p s k", k=KD)

                    def ada(n):
                        dst = (scale1, shift1, scale2, shift2)[n]
                        gain = cols[:, o_gmix:o_gmix + KD] if n == 0 else cols[:, o_gffn:o_gffn + KD]
                        dve.wait_ge(sem("ada_mm"), n + 1)
                        dve.tensor_tensor(dst[:, :, :], pada[:, n % 2, 0:KD * C].rearrange("p (k c) -> p k c", c=C),
                                          bada[:, SECTIONS[n], :].unsqueeze(2).to_broadcast([P, KD, C]), ALU.add) \
                            .then_inc(sem("ada_free"), 1)
                        dve.wait_ge(sem("ada_free"), n + 1)
                        if n % 2 == 0:
                            dve.scalar_tensor_tensor(dst[:, :, :], dst[:, :, :], 1.0,
                                                     gain.unsqueeze(2).to_broadcast([P, KD, C]), ALU.add, ALU.mult) \
                                .then_inc(sem("ada_gain"), 1)
                            dve.wait_ge(sem("ada_gain"), n // 2 + 1)

                    ada(0)
                    ada(1)
                    pairs(dve, NPT, lambda u, s: modulate(dve, "in", u, s, pT, hf, scale1, shift1))
                    modulate(dve, "in", NPT // 2, 0, pT, hf, scale1, shift1, sample=True)
                    ada(2)
                    ada(3)
                    dve.wait_ge(sem("brow_in"), 64)
                    for n in range(2):
                        dve.wait_ge(sem("ada_mm"), FM + n + 1)
                        dve.tensor_tensor(grow[:, n, :], pada[0:C, :, :].rearrange("p a b -> p (a b)"),
                                          brow[:, n, :], ALU.add).then_inc(sem("ada_free"), 1)
                        dve.wait_ge(sem("ada_free"), FM + n + 1)
                        dve.tensor_tensor(grow[:, n, :], grow[:, n, :], gpost[:, n, :], ALU.mult) \
                            .then_inc(sem("grow_ready"), 1)

                @block.tensor
                def _(pe):
                    pe.wait_ge(sem("ident"), 1)
                    pe.wait_ge(sem("rows_in"), 16 * N_ROWS_IN)
                    for n, r in enumerate(stack_rows):
                        last = pe.transpose(pcol[:, n // 4, (n % 4) * P:(n % 4) * P + r], rows[0:r, n, :],
                                            ident[0:r, 0:r])
                    last.then_inc(sem("rows_T"), 1)
                    pe.wait_ge(sem("cs"), 1)

                    def ada_columns(n):
                        pe.wait_ge(sem(f"wada_in{n % 2}"), 16 * (n // 2 + 1))
                        if n >= 2:
                            pe.wait_ge(sem("ada_free"), n - 1)
                        for j in range(KD):
                            for k in range(KD):
                                last = pe.matmul(pada[:, n % 2, j * C:(j + 1) * C], wada[n % 2][:, k, j * P:(j + 1) * P],
                                                 cs_k[:, k, :], start=(k == 0), stop=(k == KD - 1))
                        last.then_inc(sem("ada_mm"), 1)

                    ada_columns(0)
                    ada_columns(1)
                    pairs(pe, NPT, lambda u, s: transposes(pe, "in", u, s, xn, pT))
                    transposes(pe, "in", NPT // 2, 0, xn, pT)
                    ada_columns(2)
                    ada_columns(3)
                    for n in range(2):
                        pe.wait_ge(sem(f"wada_in{n}"), 16 * (FM // 2 + 1))
                        pe.wait_ge(sem("ada_free"), FM + n)
                        for half in range(2):
                            for k in range(KD):
                                last = pe.matmul(pada[0:C, half, :], cs_k[:, k, :],
                                                 wada[(FM + n) % 2][:, k, half * HALF:(half + 1) * HALF],
                                                 start=(k == 0), stop=(k == KD - 1))
                        last.then_inc(sem("ada_mm"), 1)

        q_ctx = ExitStack()
        Q = sb(q_ctx, "q", [P, H, T])
        K, LF = M[:, 0:H, :], M[:, H:2 * H, :]
        act_ctx = ExitStack()
        with act_ctx:
            V = sb(act_ctx, "v", [P, H, T])

            ctx = ExitStack()
            with ctx:
                ps = [pb(ctx, f"p_proj{s}", [P, NG, 512]) for s in range(2)]
                ws = WeightStream(ctx, "wqfi", ps)
                ft = [sb(ctx, f"f_step{n}", [P, T]) for n in range(4)]

                with nc.Block() as block:
                    @block.sync
                    def _(sp):
                        ws.start(sp)
                        pairs(sp, 3 * H, lambda u, s: ws.load(sp, u, s, w_in[:, bass.ds((u * 2 + s) * P, P)]))

                    @block.gpsimd
                    def _(pool):
                        pairs(pool, 3 * H, lambda u, s: ws.split(pool, u, s, KD))

                    @block.tensor
                    def _(pe):
                        pairs(pe, 3 * H, lambda u, s: ws.product(pe, u, s, KD, h))

                    @block.scalar
                    def _(act):
                        def silu_q(u, s):
                            ws.arrived(act, u, s)
                            act.activation(Q[:, bass.ds(u * 2 + s, 1), :].rearrange("p a (g t) -> p (a g) t", t=G), groups(ps[s]),
                                           ACT.Silu).then_inc(sem(f"wqfi_pfree{s}"), 1)

                        def copy_v(u, s):
                            ws.arrived(act, u + H, s)
                            act.activation(V[:, bass.ds(u * 2 + s, 1), :].rearrange("p a (g t) -> p (a g) t", t=G), groups(ps[s]),
                                           ACT.Copy).then_inc(sem(f"wqfi_pfree{s}"), 1)

                        pairs(act, H, silu_q)
                        link = Link(act, sem("f_act"))
                        for hd in range(H):
                            ws.arrived(act, (H + hd) // 2, hd % 2)
                            if hd:
                                act.wait_ge(sem("f_kexp"), hd)
                            link(act.activation(by_group(ft[1][:, :]), groups(ps[hd % 2]), ACT.Abs))
                            link(act.activation(ft[1][:, :], ft[1][:, :], ACT.Exp, scale=-1.0))
                            act.activation(ft[1][:, :], ft[1][:, :], ACT.Ln, bias=1.0).then_inc(sem("f_softplus"), 1)
                            act.wait_ge(sem("f_kexp"), hd + 1)
                            act.activation(K[:, hd, :], ft[2][:, :], ACT.Exp, scale=-1.0, bias=log_1mlb[:, hd:hd + 1]) \
                                .then_inc(sem("f_k"), 1)
                            act.wait_ge(sem("f_c"), hd + 1)
                            if hd:
                                act.wait_ge(sem("f_done"), hd)
                            link(act.activation(ft[3][:, :], ft[0][:, :], ACT.Abs, scale=-1.0, bias=log_lb[:, hd:hd + 1]))
                            link(act.activation(ft[3][:, :], ft[3][:, :], ACT.Exp, scale=-1.0))
                            act.activation(ft[3][:, :], ft[3][:, :], ACT.Ln, bias=1.0).then_inc(sem("f_lse"), 1)
                        pairs(act, H, copy_v)

                    @block.vector
                    def _(dve):
                        link = Link(dve, sem("f_dve"))
                        for hd in range(H):
                            z = groups(ps[hd % 2])
                            step = [by_group(f[:, :]) for f in ft]
                            lb = log_lb[:, hd:hd + 1]
                            ws.arrived(dve, (H + hd) // 2, hd % 2)
                            dve.wait_ge(sem("f_softplus"), hd + 1)
                            link(dve.scalar_tensor_tensor(step[0], z, 0.0, step[1], ALU.min, ALU.subtract))
                            if hd:
                                dve.wait_ge(sem("f_k"), hd)
                            dve.scalar_tensor_tensor(step[2], z, 0.0, step[1], ALU.max, ALU.add).then_inc(sem("f_kexp"), 1)
                            dve.wait_ge(sem("f_kexp"), hd + 1)
                            dve.sem_inc(sem(f"wqfi_pfree{hd % 2}"), 1)
                            dve.tensor_scalar(ft[0][:, :], ft[0][:, :], log_1mlb[:, hd:hd + 1], None, ALU.add) \
                                .then_inc(sem("f_c"), 1)
                            dve.wait_ge(sem("f_lse"), hd + 1)
                            dve.scalar_tensor_tensor(LF[:, hd, :], ft[0][:, :], lb, ft[3][:, :], ALU.max, ALU.add) \
                                .then_inc(sem("f_done"), 1)
                            dve.wait_ge(sem("f_done"), hd + 1)

            ctx = ExitStack()
            with ctx:
                HW = H * P
                R = sb(ctx, "decay_in", [P, HW])
                L = sb(ctx, "decay_out", [P, HW])
                Qc = sb(ctx, "q_chunk", [P, HW])
                Kc = sb(ctx, "k_chunk", [P, HW])
                Vc = sb(ctx, "v_chunk", [P, HW])
                Er = sb(ctx, "exp_in", [P, 2, HW // 2])
                El = sb(ctx, "exp_out", [P, 2, HW // 2])
                Ql = sb(ctx, "q_level", [P, 2, HW // 2])
                Kl = sb(ctx, "k_level", [P, 2, HW])
                Qb = sb(ctx, "q_decayed", [P, HW])
                Kd = sb(ctx, "k_decayed", [P, HW])
                vt = sb(ctx, "v_tokens", [P, HW])
                kdt = sb(ctx, "kd_tokens", [P, HW])
                A = sb(ctx, "attention", [P, HW])
                S = sb(ctx, "state", [P, HW])
                rs = sb(ctx, "readout_rstd", [P, HW])
                LEVELS = P.bit_length() - 1
                SLEVELS = LS.bit_length() - 1
                masks = sb(ctx, "level_masks", [P, LEVELS, P // 2])
                pl = [pb(ctx, f"p_level{n}", [P, 512]) for n in range(2)]
                pd = pb(ctx, "p_diagonal", [P, 512])
                pt = pb(ctx, "p_tokens", [P, 512])
                po = pb(ctx, "p_readout", [P, 512])
                pm = pb(ctx, "p_meansq", [P, 512])
                pst = [pb(ctx, f"p_state{n}", [P, 512]) for n in range(2)]
                a_norm = cols[:, o_an:o_an + 1]

                def heads(ap):
                    return ap.rearrange("p (h t) -> p h t", h=H)

                def blocks(ap, l):
                    return ap.rearrange("p (n two t) -> p n two t", two=2, t=1 << l)

                def chunk_act(act, x, c, tok, levels):
                    act.wait_ge(sem(x + "on"), c)
                    act.wait_ge(sem(x + "state"), c * H)
                    for dst, src in ((R, LF), (Qc, Q), (Kc, K), (Vc, V)):
                        act.activation(heads(dst[:, :]), src[:, :, tok], ACT.Copy).then_inc(sem(x + "in"), 1)
                    act.wait_ge(sem(x + "in"), c * 4 + 4)
                    for l in range(levels):
                        if l == 0:
                            act.wait_ge(sem(x + "L0"), c + 1)
                        else:
                            act.wait_ge(sem(x + "upd"), c * 2 * levels + 2 * l)
                        if l >= 2:
                            act.wait_ge(sem(x + "prod"), c * 2 * levels + 2 * (l - 1))
                        act.activation(Er[:, l % 2, :].rearrange("p (n t) -> p n t", t=1 << l),
                                       blocks(R[:, :], l)[:, :, 1, :], ACT.Exp).then_inc(sem(x + "ex"), 1)
                        act.activation(El[:, l % 2, :].rearrange("p (n t) -> p n t", t=1 << l),
                                       blocks(L[:, :], l)[:, :, 0, :], ACT.Exp).then_inc(sem(x + "ex"), 1)
                        if l == 1:
                            act.wait_ge(sem(x + "vT"), c + 1)
                            act.activation(vt[:, :], pt[:, :], ACT.Copy).then_inc(sem(x + "vt"), 1)
                    act.wait_ge(sem(x + "upd"), c * 2 * levels + 2 * levels)
                    act.activation(R[:, :], R[:, :], ACT.Exp).then_inc(sem(x + "exf"), 1)
                    act.activation(L[:, :], L[:, :], ACT.Exp).then_inc(sem(x + "exf"), 1)
                    act.wait_ge(sem(x + "kdT"), c + 1)
                    act.activation(kdt[:, :], pt[:, :], ACT.Copy).then_inc(sem(x + "kdt"), 1)
                    act.wait_ge(sem(x + "o"), c + 1)
                    act.activation(Vc[:, :], po[:, :], ACT.Square).then_inc(sem(x + "sq"), 1)
                    act.wait_ge(sem(x + "ms"), c + 1)
                    act.activation(rs[:, :], pm[:, :], ACT.Ln, scale=1.0 / P, bias=eps[:, :]).then_inc(sem(x + "lnms"), 1)
                    act.wait_ge(sem(x + "lnms"), c + 1)
                    act.activation(rs[:, :], rs[:, :], ACT.Exp, scale=-0.5).then_inc(sem(x + "rs"), 1)

                def chunk_dve(dve, x, c, tok, levels, state_update):
                    L2 = 2 * levels
                    dve.wait_ge(sem(x + "kdt"), c)
                    dve.wait_ge(sem(x + "fin"), c * 2)
                    dve.memset(L[:, :], 0.0).then_inc(sem(x + "L0"), 1)

                    def take(l):
                        dve.wait_ge(sem(x + "lev"), c * levels + (l + 1))
                        dve.wait_ge(sem(x + "taken"), c * (levels + 1) + l)
                        dve.sem_inc(sem("dve_passed"), 1)
                        nb, hh = P >> (l + 1), 1 << l
                        out = blocks(A[:, :], l)[:, :, 1, :].rearrange("p (h n) t -> p h n t", h=H)
                        mask = masks[:, l, :].bitcast(U32).rearrange("p (n t) -> p n t", t=hh) \
                            .unsqueeze(1).to_broadcast([P, H, nb, hh])
                        dve.copy_predicated(out, mask, pl[l % 2][:, 0:HW // 2].rearrange("p (h n t) -> p h n t", h=H, t=hh)) \
                            .then_inc(sem(x + "taken"), 1)

                    for l in range(levels):
                        r, q = blocks(R[:, :], l), blocks(Qc[:, :], l)
                        lo, k = blocks(L[:, :], l), blocks(Kc[:, :], l)
                        n, hh = HW >> (l + 1), 1 << l
                        half = lambda ap: ap.rearrange("p (n t) -> p n t", t=hh)
                        dve.wait_ge(sem(x + "ex"), c * L2 + 2 * l + 2)
                        if l >= 2:
                            dve.wait_ge(sem(x + "lev"), c * levels + (l - 1))
                        dve.tensor_tensor(half(Ql[:, l % 2, :]), half(Er[:, l % 2, :]), q[:, :, 1, :], ALU.mult) \
                            .then_inc(sem(x + "prod"), 1)
                        dve.tensor_tensor(blocks(Kl[:, l % 2, :], l)[:, :, 0, :], half(El[:, l % 2, :]), k[:, :, 0, :],
                                          ALU.mult).then_inc(sem(x + "prod"), 1)
                        dve.tensor_tensor(lo[:, :, 0, :], lo[:, :, 0, :], r[:, :, 1, hh - 1:hh].to_broadcast([P, n, hh]),
                                          ALU.add).then_inc(sem(x + "upd"), 1)
                        dve.wait_ge(sem(x + "upd"), c * L2 + 2 * l + 1)
                        dve.tensor_tensor(r[:, :, 1, :], r[:, :, 1, :], r[:, :, 0, hh - 1:hh].to_broadcast([P, n, hh]),
                                          ALU.add).then_inc(sem(x + "upd"), 1)
                        dve.wait_ge(sem(x + "upd"), c * L2 + 2 * l + 2)
                        if l >= 1:
                            take(l - 1)
                    dve.wait_ge(sem(x + "exf"), c * 2 + 2)
                    dve.tensor_tensor(Kd[:, :], L[:, :], Kc[:, :], ALU.mult).then_inc(sem(x + "fin"), 1)
                    dve.tensor_tensor(Qb[:, :], R[:, :], Qc[:, :], ALU.mult).then_inc(sem(x + "fin"), 1)
                    take(levels - 1)
                    dve.wait_ge(sem(x + "diag"), c + 1)
                    dve.wait_ge(sem(x + "taken"), c * (levels + 1) + levels)
                    dve.sem_inc(sem("dve_passed"), 1)
                    dve.copy_predicated(heads(A[:, :]), ident[:, :].bitcast(U32).unsqueeze(1).to_broadcast([P, H, P]),
                                        heads(pd[:, :])).then_inc(sem(x + "taken"), 1)
                    state_update()
                    dve.wait_ge(sem(x + "rs"), c + 1)
                    dve.scalar_tensor_tensor(Q[:, :, tok], heads(po[:, :]), a_norm, heads(rs[:, :]), ALU.mult, ALU.mult) \
                        .then_inc(sem(x + "on"), 1)

                def head(ap, hd):
                    return ap[:, hd * P:(hd + 1) * P]

                def chunk_pe(pe, x, c, levels, inter, state_product):
                    pe.wait_ge(sem(x + "in"), c * 4 + 4)
                    for hd in range(H):
                        last = pe.transpose(head(pt, hd), head(Vc, hd), ident[:, :])
                    last.then_inc(sem(x + "vT"), 1)
                    for hd in range(H):
                        last = pe.matmul(head(pd, hd), head(Kc, hd), head(Qc, hd), start=True, stop=True)
                    last.then_inc(sem(x + "diag"), 1)
                    for l in range(levels):
                        pe.wait_ge(sem(x + "prod"), c * 2 * levels + 2 * l + 2)
                        if l >= 2:
                            pe.wait_ge(sem(x + "taken"), c * (levels + 1) + (l - 1))
                        for hd in range(H):
                            last = pe.matmul(pl[l % 2][:, hd * P // 2:(hd + 1) * P // 2], head(Kl[:, l % 2, :], hd),
                                             Ql[:, l % 2, hd * P // 2:(hd + 1) * P // 2], start=True, stop=True)
                        last.then_inc(sem(x + "lev"), 1)
                    pe.wait_ge(sem(x + "fin"), c * 2 + 1)
                    pe.wait_ge(sem(x + "vt"), c + 1)
                    for hd in range(H):
                        last = pe.transpose(head(pt, hd), head(Kd, hd), ident[:, :])
                    last.then_inc(sem(x + "kdT"), 1)
                    pe.wait_ge(sem(x + "fin"), c * 2 + 2)
                    pe.wait_ge(sem(x + "taken"), c * (levels + 1) + (levels + 1))
                    pe.wait_ge(sem(x + "state"), c * H)
                    for hd in range(H):
                        pe.matmul(head(po, hd), head(vt, hd), head(A, hd), start=True, stop=x == "s_")
                        last = inter(hd)
                    last.then_inc(sem(x + "o"), 1)
                    pe.wait_ge(sem(x + "kdt"), c + 1)
                    state_product()
                    pe.wait_ge(sem(x + "sq"), c + 1)
                    pe.matmul(pm[:, :], ones[:, :], Vc[:, :], start=True, stop=True).then_inc(sem(x + "ms"), 1)

                sctx = ExitStack()
                with sctx:
                    S0 = sb(sctx, "sample_states", [P, NB, HW])
                    kdm = sb(sctx, "kd_of_stream", [P, HW])
                    in_stream = sb(sctx, "in_stream", [P, NB])
                    with nc.Block() as block:
                        @block.sync
                        def _(sp):
                            for b in range(NB):
                                sp.dma_start(heads(S0[:, b, :]), io["state_hgrn"][0, b].rearrange("h k v -> k h v")) \
                                    .then_inc(sem("s_S0"), 16)
                            for b in range(NB):
                                sp.wait_ge(sem("s_state"), b + 1)
                                sp.dma_start(io["hgrn_sample"][0, b].rearrange("h k v -> k h v"), heads(S0[:, b, :])).then_inc(sem("s_state_out"), 16)
                            sp.wait_ge(sem("s_state_out"), 16 * NB)

                        @block.gpsimd
                        def _(pool):
                            pool.memset(masks[:, :, :], 1.0).then_inc(sem("mask"), 1)
                            pool.memset(in_stream[:, :], 1.0).then_inc(sem("mask"), 1)
                            pool.memset(Kl[:, :, :], 0.0).then_inc(sem("mask"), 1)
                            pool.memset(A[:, :], 0.0).then_inc(sem("mask"), 1)
                            pool.memset(S[:, :], 0.0).then_inc(sem("mask"), 1)
                            pool.wait_ge(sem("mask"), 5)
                            link = Link(pool, sem("mask"), 5)
                            for l in range(LEVELS):
                                nb, hh = P >> (l + 1), 1 << l
                                m = masks[:, l, :].rearrange("p (n t) -> p n t", t=hh)
                                link(pool.affine_select(out=m, in_=m, compare_op=ALU.is_ge, fill=0.0, base=0,
                                                        pattern=[[-2 * hh, nb], [0, hh]], channel_multiplier=1))
                                link(pool.affine_select(out=m, in_=m, compare_op=ALU.is_ge, fill=0.0, base=hh - 1,
                                                        pattern=[[2 * hh, nb], [0, hh]], channel_multiplier=-1))
                            link(pool.affine_select(out=in_stream[:, :], in_=in_stream[:, :], compare_op=ALU.is_ge,
                                                    fill=0.0, base=0, pattern=[[-LS, NB]], channel_multiplier=1))
                            link(pool.affine_select(out=in_stream[:, :], in_=in_stream[:, :], compare_op=ALU.is_ge,
                                                    fill=0.0, base=LS - 1, pattern=[[LS, NB]], channel_multiplier=-1))
                            pool.memset(rs[:, 0:1], 0.0).then_inc(sem("masks_ready"), 1)

                        tok = slice(NPT * P, T)

                        @block.scalar
                        def _(act):
                            act.wait_ge(sem("masks_ready"), 1)
                            chunk_act(act, "s_", 0, tok, SLEVELS)

                        @block.vector
                        def _(dve):
                            def states():
                                dve.wait_ge(sem("s_kdt"), 1)
                                dve.wait_ge(sem("s_S0"), 16 * NB)
                                dve.wait_ge(sem("s_o"), 1)
                                ends = R[:, :].rearrange("p (h b t) -> p b h t", h=H, t=LS)[:, :, :, LS - 1:LS]
                                for b in range(NB):
                                    if b:
                                        dve.wait_ge(sem("s_mm"), b)
                                    dve.tensor_scalar(kdm[:, :], kdt[:, :], in_stream[:, b:b + 1], None, ALU.mult) \
                                        .then_inc(sem("s_kdm"), 1)
                                    s0 = heads(S0[:, b, :])
                                    dve.tensor_tensor(s0, s0, ends[:, b].to_broadcast([P, H, P]), ALU.mult) \
                                        .then_inc(sem("s_dec"), 1)
                                    dve.wait_ge(sem("s_dec"), b + 1)
                                    dve.wait_ge(sem("s_mm"), b + 1)
                                    dve.tensor_tensor(S0[:, b, :], S0[:, b, :], pst[b % 2][:, :], ALU.add) \
                                        .then_inc(sem("s_state"), 1)

                            dve.wait_ge(sem("masks_ready"), 1)
                            chunk_dve(dve, "s_", 0, tok, SLEVELS, states)

                        @block.tensor
                        def _(pe):
                            def inter(hd):
                                for b in range(NB):
                                    at = slice(hd * P + b * LS, hd * P + (b + 1) * LS)
                                    last = pe.matmul(po[:, at], head(S0[:, b, :], hd), Qb[:, at], start=False,
                                                     stop=(b == NB - 1), skip_group_check=True)
                                return last

                            def state_product():
                                for b in range(NB):
                                    pe.wait_ge(sem("s_kdm"), b + 1)
                                    if b >= 2:
                                        pe.wait_ge(sem("s_state"), b - 1)
                                    for hd in range(H):
                                        last = pe.matmul(head(pst[b % 2], hd), head(kdm, hd), head(vt, hd),
                                                         start=True, stop=True)
                                    last.then_inc(sem("s_mm"), 1)

                            pe.wait_ge(sem("s_S0"), 16 * NB)
                            chunk_pe(pe, "s_", 0, SLEVELS, inter, state_product)

                with nc.Block() as block:
                    @block.sync
                    def _(sp):
                        sp.wait_ge(sem("p_state"), H * NPT)
                        sp.dma_start(io["hgrn_prompt"][0, 0].rearrange("h k v -> k h v"), heads(S[:, :])) \
                            .then_inc(sem("p_state_out"), 16)
                        sp.wait_ge(sem("p_state_out"), 16)

                    @block.scalar
                    def _(act):
                        with act.Fori(0, NPT, 1) as c:
                            chunk_act(act, "p_", c, bass.ds(c * P, P), LEVELS)

                    @block.vector
                    def _(dve):
                        with dve.Fori(0, NPT, 1) as c:
                            def state():
                                dve.wait_ge(sem("p_st"), c + 1)
                                for hd in range(H):
                                    dve.scalar_tensor_tensor(head(S, hd), head(S, hd), R[:, (hd + 1) * P - 1:(hd + 1) * P],
                                                             head(pst[0], hd), ALU.mult, ALU.add).then_inc(sem("p_state"), 1)
                            chunk_dve(dve, "p_", c, bass.ds(c * P, P), LEVELS, state)

                    @block.tensor
                    def _(pe):
                        def inter(hd):
                            return pe.matmul(head(po, hd), head(S, hd), head(Qb, hd), start=False, stop=True)

                        with pe.Fori(0, NPT, 1) as c:
                            def state_product():
                                for hd in range(H):
                                    last = pe.matmul(head(pst[0], hd), head(kdt, hd), head(vt, hd), start=True, stop=True)
                                last.then_inc(sem("p_st"), 1)
                            chunk_pe(pe, "p_", c, LEVELS, inter, state_product)

        new_semaphores()

        ot_ctx = ExitStack()
        branch = sb(ot_ctx, "branch", [P, 2, H, T], F32R)
        ctx = ExitStack()
        with ctx:
            ps = [pb(ctx, f"p_gate{s}", [P, NG, 512]) for s in range(2)]
            ws = WeightStream(ctx, "wg", ps)
            sg = sb(ctx, "silu_g", [P, T])
            with nc.Block() as block:
                @block.sync
                def _(sp):
                    ws.start(sp)
                    pairs(sp, H, lambda u, s: ws.load(sp, u, s, w_in[:, bass.ds((u * 2 + s) * P + 3 * AW, P)]))

                @block.gpsimd
                def _(pool):
                    pairs(pool, H, lambda u, s: ws.split(pool, u, s, KD))

                @block.tensor
                def _(pe):
                    pairs(pe, H, lambda u, s: ws.product(pe, u, s, KD, h))

                @block.scalar
                def _(act):
                    def silu_g(u, s):
                        ws.arrived(act, u, s)
                        act.wait_ge(sem("ga_lo"), u * 2 + s)
                        act.activation(by_group(sg[:, :]), groups(ps[s]), ACT.Silu).then_inc(sem(f"wg_pfree{s}"), 1)
                        act.wait_ge(sem(f"wg_pfree{s}"), u + 2)
                        act.sem_inc(sem("ga_silu"), 1)
                    pairs(act, H, silu_g)

                @block.vector
                def _(dve):
                    def gate(u, s):
                        n = u * 2 + s
                        one = bass.ds(n, 1)
                        x = sg[:, :].unsqueeze(1)
                        dve.wait_ge(sem("ga_silu"), n + 1)
                        dve.tensor_tensor(branch[:, 0, one, :], x, Q[:, one, :], ALU.mult).then_inc(sem("ga_hi"), 1)
                        dve.tensor_tensor(x, x, Q[:, one, :], ALU.mult).then_inc(sem("ga_full"), 1)
                        dve.wait_ge(sem("ga_full"), n + 1)
                        dve.tensor_tensor(branch[:, 1, one, :], x, f32(branch[:, 0, one, :]), ALU.subtract) \
                            .then_inc(sem("ga_lo"), 1)
                    pairs(dve, H, gate)

        def mix(name, which, w_proj):
            ctx = ExitStack()
            with ctx:
                ps = [pb(ctx, f"p_{name}{s}", [P, NG, 512]) for s in range(2)]
                ws = WeightStream(ctx, name, ps)
                sg = sb(ctx, name + "_sigmoid", [P, T])
                y = sb(ctx, name + "_gated", [P, T])
                with nc.Block() as block:
                    @block.sync
                    def _(sp):
                        ws.start(sp)
                        with sp.Fori(0, KD, 1) as j:
                            ws.load(sp, j, 0, w_bgate[:, bass.ds(j * P + which * D, P)])
                            ws.load(sp, j, 1, w_proj[:, bass.ds(j * P, P)])

                    @block.gpsimd
                    def _(pool):
                        with pool.Fori(0, KD, 1) as j:
                            ws.split(pool, j, 0, KD)
                            ws.split(pool, j, 1, H)

                    @block.tensor
                    def _(pe):
                        with pe.Fori(0, KD, 1) as j:
                            ws.product(pe, j, 0, KD, h)
                            ws.product(pe, j, 1, H, branch)

                    @block.scalar
                    def _(act):
                        with act.Fori(0, KD, 1) as j:
                            ws.arrived(act, j, 0)
                            act.wait_ge(sem(name + "_pfree1"), j + 1)
                            act.activation(by_group(sg[:, :]), groups(ps[0]), ACT.Sigmoid) \
                                .then_inc(sem(name + "_pfree0"), 1)

                    @block.vector
                    def _(dve):
                        with dve.Fori(0, KD, 1) as j:
                            z = M[:, bass.ds(j, 1), :]
                            ws.arrived(dve, j, 1)
                            dve.wait_ge(sem(name + "_pfree0"), j + 2)
                            if which == 0:
                                dve.tensor_tensor(z.rearrange("p a (g t) -> p (a g) t", t=G), by_group(sg[:, :]),
                                                  groups(ps[1]), ALU.mult).then_inc(sem(name + "_pfree1"), 1)
                            else:
                                dve.wait_ge(sem(name + "_z"), j)
                                dve.tensor_tensor(by_group(y[:, :]), by_group(sg[:, :]), groups(ps[1]), ALU.mult) \
                                    .then_inc(sem(name + "_pfree1"), 1)
                                dve.wait_ge(sem(name + "_pfree1"), j + 2)
                                dve.tensor_tensor(z, z, y[:, :].unsqueeze(1), ALU.add).then_inc(sem(name + "_z"), 1)

        mix("mixa", 0, io["w_pa"][0])

        ctx = ExitStack()
        with ctx:
            ps = [pb(ctx, f"p_cvb{s}", [P, NG, 512]) for s in range(2)]
            ws = WeightStream(ctx, "wcvb", ps)
            U = sb(ctx, "conv_in", [P, 2 + NP_])
            Us = sb(ctx, "conv_in_samples", [P, NB, 2 + LS])
            cg, y, tf = Q[:, 0, :], Q[:, 1, :], Q[:, 2, :]
            FIRST_COL = (4 * AW + BW, 4 * AW + 2 * BW, 4 * AW)
            cw = cols[:, o_cw:o_cw + 3 * KB].rearrange("p (w j) -> p w j", j=KB)
            cst = cols[:, o_cst:o_cst + n_cst].rearrange("p (b w j) -> p b w j", w=2, j=KB)
            n_s = 2 * NB * KB
            ncs = new_conv[:, 0:n_s].rearrange("p (b w j) -> p b w j", w=2, j=KB)
            ncp = new_conv[:, n_s:].rearrange("p (w j) -> p w j", j=KB)

            with nc.Block() as block:
                @block.sync
                def _(sp):
                    ws.start(sp)
                    with sp.Fori(0, KB // 2, 1) as i:
                        for n in range(6):
                            ws.load(sp, i * 3 + n // 2, n % 2, w_in[:, bass.ds((i * 2 + n // 3) * P + FIRST_COL[n % 3], P)])

                @block.gpsimd
                def _(pool):
                    with pool.Fori(0, KB // 2, 1) as i:
                        for n in range(6):
                            ws.split(pool, i * 3 + n // 2, n % 2, KD)

                @block.tensor
                def _(pe):
                    with pe.Fori(0, KB // 2, 1) as i:
                        for n in range(6):
                            ws.product(pe, i * 3 + n // 2, n % 2, KD, h)

                @block.scalar
                def _(act):
                    for j in range(KB):
                        n = 3 * j
                        ws.arrived(act, n // 2, n % 2)
                        if j:
                            act.wait_ge(sem("cv_u"), 3 * j)
                        act.activation(by_group(cg), groups(ps[n % 2]), ACT.Copy).then_inc(sem("cv_c"), 1)
                        act.wait_ge(sem("cv_c"), j + 1)
                        act.sem_inc(sem(f"wcvb_pfree{n % 2}"), 1)

                @block.vector
                def _(dve):
                    link = Link(dve, sem("cv_dve"))
                    link(dve.memset(U[:, 0:2], 0.0))
                    for j in range(KB):
                        nv, nb_ = 3 * j + 1, 3 * j + 2
                        v, b = ps[nv % 2], ps[nb_ % 2]
                        link(dve.tensor_copy(Us[:, :, 0:2], cst[:, :, :, j]))
                        dve.wait_ge(sem("cv_c"), j + 1)
                        ws.arrived(dve, nv // 2, nv % 2)
                        dve.tensor_tensor(U[:, 2:2 + 2 * G].rearrange("p (g t) -> p g t", t=G), v[:, 0:2, 0:G],
                                          cg[:, 0:2 * G].rearrange("p (g t) -> p g t", t=G), ALU.mult).then_inc(sem("cv_u"), 1)
                        dve.tensor_tensor(U[:, 2 + 2 * G:], v[:, 2, 0:REST], cg[:, 2 * G:NP_], ALU.mult) \
                            .then_inc(sem("cv_u"), 1)
                        dve.tensor_tensor(Us[:, :, 2:], v[:, 2, REST:G].rearrange("p (b t) -> p b t", t=LS),
                                          cg[:, NP_:].rearrange("p (b t) -> p b t", t=LS), ALU.mult).then_inc(sem("cv_u"), 1)
                        dve.wait_ge(sem("cv_u"), 3 * j + 3)
                        dve.sem_inc(sem(f"wcvb_pfree{nv % 2}"), 1)
                        conv3(dve, link, U, Us, y, [cw[:, w, j:j + 1] for w in range(3)])
                        link(dve.tensor_copy(ncs[:, :, :, j], Us[:, :, LS:]))
                        link(dve.tensor_copy(ncp[:, :, j], U[:, NP_:]))
                        ws.arrived(dve, nb_ // 2, nb_ % 2)
                        link(dve.tensor_tensor(by_group(tf), groups(b), by_group(y), ALU.mult))
                        link(dve.tensor_tensor(by_group(branch[:, 0, j, :]), groups(b), by_group(y), ALU.mult))
                        dve.sem_inc(sem(f"wcvb_pfree{nb_ % 2}"), 1)
                        link(dve.tensor_tensor(branch[:, 1, j, :], tf, f32(branch[:, 0, j, :]), ALU.subtract))

        mix("mixb", 1, io["w_pb"][0])
        ot_ctx.close()
        q_ctx.close()

        def token_rows(name_p, name_s):
            prompt = io[name_p][0]
            return (lambda t: prompt[bass.ds(t * P, P), :]), io[name_s].rearrange("b l d -> (b l) d")

        def load_gate(sp, dst, n, sample, sem_name):
            if sample:
                for b in range(NB):
                    sp.dma_start(dst[b * LS:(b + 1) * LS, :], gate_scratch[n, b + 1:b + 2, :].to_broadcast([LS, D])) \
                        .then_inc(sem(sem_name), 16)
            else:
                sp.dma_start(dst[:, :], gate_scratch[n, 0:1, :].to_broadcast([P, D])).then_inc(sem(sem_name), 16)

        x_rows, x_sample_rows = token_rows("x_prompt", "x_sample")
        ctx = ExitStack()
        with ctx:
            wo = sb(ctx, "w_o_halves", [P, 2, KD, D], F32R)
            X = sb(ctx, "x_tile_mid", [P, 2, D])
            zh = sb(ctx, "z_tile", [P, 2, KD, P], F32R)
            xn = sb(ctx, "x1_normed", [P, 1, D])
            gate = sb(ctx, "gate_mix", [P, D])
            full = sb(ctx, "h_mid", [P, 1, D])
            stat = sb(ctx, "stat_mid", [P, 8])
            pm = pb(ctx, "p_m", [P, 2, 2, 512])
            pT = pb(ctx, "p_x1T", [P, 2, 2, 512])
            w_o = io["w_o"][0]

            with nc.Block() as block:
                @block.sync
                def _(sp):
                    give_slots(sp, ["mid_xT", "mid_pT", "mid_lo", "m_used"])
                    load_gate(sp, gate, 0, False, "gate_mix_in")
                    for k in range(KD):
                        if k >= 2:
                            sp.wait_ge(sem("wo_lo"), k - 1)
                        sp.dma_start(X[:, k % 2, :], w_o[k * P:(k + 1) * P, :]).then_inc(sem(f"wo_in{k % 2}"), 16)
                    sp.wait_ge(sem("wo_lo"), KD)

                    def load_x(u, s, src, normed):
                        if normed is not None:
                            hold(sp, "mid_xn", normed)
                        hold(sp, f"x1_out{s}", u * 16)
                        sp.dma_start(X[:, s, :], src).then_inc(sem(f"x_mid_in{s}"), 16)

                    def store(u, s, dst):
                        hold(sp, "x1", u * 2 + s + 1)
                        sp.dma_start(dst, X[:, s, :]).then_inc(sem(f"x1_out{s}"), 16)

                    load_x(0, 0, x_rows(0), None)
                    with sp.Fori(0, NPT // 2 - 1, 1) as i:
                        for s in range(2):
                            load_x(i + s, 1 - s, x_rows(i * 2 + s + 1), i * 2 + s)
                            store(i, s, x1_scratch[bass.ds((i * 2 + s) * P, P), :])
                    i = NPT // 2 - 1
                    load_x(i, 1, x_rows(NPT - 1), NPT - 2)
                    store(i, 0, x1_scratch[(NPT - 2) * P:(NPT - 1) * P, :])
                    load_x(NPT // 2, 0, x_sample_rows, NPT - 1)
                    store(i, 1, x1_scratch[(NPT - 1) * P:NPT * P, :])
                    sp.wait_ge(sem("x1"), NPT)
                    load_gate(sp, gate, 0, True, "gate_mix_s_in")
                    store(NPT // 2, 0, x1_scratch[NPT * P:, :])
                    sp.wait_ge(sem("x1_out0"), 16 * (NPT // 2 + 1))
                    sp.wait_ge(sem("x1_out1"), 16 * (NPT // 2))

                @block.gpsimd
                def _(pool):
                    pairs(pool, NPT, lambda u, s: halves_of_h(pool, "mid", u, s, full))
                    halves_of_h(pool, "mid", NPT // 2, 0, full)

                @block.scalar
                def _(act):
                    for k in range(KD):
                        act.wait_ge(sem(f"wo_in{k % 2}"), 16 * (k // 2 + 1))
                        act.activation(wo[:, 0, k, :], X[:, k % 2, :], ACT.Copy).then_inc(sem("wo_hi"), 1)

                    def z_hi(t):
                        act.wait_ge(sem("m_mm"), t)
                        act.activation(zh[:, 0, :, :], M[:, :, bass.ds(t * P, P)], ACT.Copy).then_inc(sem("z_hi"), 1)

                    def norms(u, s):
                        t = u * 2 + s
                        link = Link(act, sem("mid_norm"), t * 4)

                        def rstd(at):
                            link(act.activation(stat[:, at + 1:at + 2], stat[:, at:at + 1], ACT.Ln, scale=1.0 / D,
                                                bias=eps[:, :]))
                            act.activation(stat[:, at + 2:at + 3], stat[:, at + 1:at + 2], ACT.Exp, scale=-0.5) \
                                .then_inc(sem("mid_rstd"), 1)

                        act.wait_ge(sem("m_mm"), t + 1)
                        act.wait_ge(sem("mid_xT"), t + 2)
                        link(act.activation(xn[:, 0, :].rearrange("p (a n) -> p a n", a=2), pm[:, s], ACT.Square,
                                            accum_out=stat[:, 0:1]))
                        rstd(0)
                        act.wait_ge(sem("x1"), t + 1)
                        link(act.activation(xn[:, 0, :], X[:, s, :], ACT.Square, accum_out=stat[:, 4:5]))
                        rstd(4)
                        act.wait_ge(sem("mid_rstd"), t * 2 + 2)
                        act.activation(xn[:, 0, :], X[:, s, :], ACT.Copy, scale=stat[:, 6:7]).then_inc(sem("mid_xn"), 1)

                    z_hi(0)
                    with act.Fori(0, NPT // 2, 1) as i:
                        for s in range(2):
                            z_hi(i * 2 + s + 1)
                            norms(i, s)
                    norms(NPT // 2, 0)

                @block.vector
                def _(dve):
                    for k in range(KD):
                        dve.wait_ge(sem("wo_hi"), k + 1)
                        dve.tensor_tensor(wo[:, 1, k, :], X[:, k % 2, :], f32(wo[:, 0, k, :]), ALU.subtract) \
                            .then_inc(sem("wo_lo"), 1)

                    def z_lo(t):
                        dve.wait_ge(sem("z_hi"), t + 1)
                        dve.tensor_tensor(zh[:, 1, :, :], M[:, :, bass.ds(t * P, P)], f32(zh[:, 0, :, :]), ALU.subtract) \
                            .then_inc(sem("z_lo"), 1)

                    def residual(u, s, sample):
                        t = u * 2 + s
                        flat = lambda ap: ap.rearrange("p (a n) -> p a n", a=2)
                        dve.wait_ge(sem("mid_rstd"), t * 2 + 1)
                        dve.wait_ge(sem("mid_lo"), t + 2)
                        dve.wait_ge(sem("gate_mix_in"), 16)
                        if sample:
                            dve.wait_ge(sem("gate_mix_s_in"), 16 * NB)
                        dve.scalar_tensor_tensor(flat(full[:, 0, :]), pm[:, s], stat[:, 2:3], flat(gate[:, :]), ALU.mult,
                                                 ALU.mult).then_inc(sem("m_used"), 1)
                        dve.wait_ge(sem("m_used"), t + 3)
                        dve.wait_ge(sem(f"x_mid_in{s}"), u * 16 + 16)
                        dve.tensor_tensor(X[:, s, :], X[:, s, :], full[:, 0, :], ALU.add).then_inc(sem("x1"), 1)
                        dve.wait_ge(sem("x1"), t + 1)

                    z_lo(0)
                    with dve.Fori(0, NPT // 2, 1) as i:
                        for s in range(2):
                            z_lo(i * 2 + s + 1)
                            residual(i, s, False)
                            modulate(dve, "mid", i, s, pT, full, scale2, shift2)
                    residual(NPT // 2, 0, True)
                    modulate(dve, "mid", NPT // 2, 0, pT, full, scale2, shift2, sample=True)

                @block.tensor
                def _(pe):
                    def out_product(t, s):
                        pe.wait_ge(sem("z_lo"), t + 1)
                        pe.wait_ge(sem("m_used"), t + 1)
                        for half in range(2):
                            for j, (a, b) in enumerate(PASSES):
                                for k in range(KD):
                                    last = pe.matmul(pm[:, s, half, :], zh[:, a, k, :],
                                                     wo[:, b, k, half * HALF:(half + 1) * HALF],
                                                     start=(j == 0 and k == 0), stop=(j == 2 and k == KD - 1))
                        last.then_inc(sem("m_mm"), 1)

                    pe.wait_ge(sem("wo_lo"), KD)
                    out_product(0, 0)
                    with pe.Fori(0, NPT // 2, 1) as i:
                        for s in range(2):
                            out_product(i * 2 + s + 1, 1 - s)
                            transposes(pe, "mid", i, s, xn, pT)
                    transposes(pe, "mid", NPT // 2, 0, xn, pT)

        out_sum = M[:, :, :].rearrange("p k t -> p (k t)").rearrange("p (t a n) -> p t a n", a=2, n=HALF)
        ctx = ExitStack()
        with ctx:
            ps = [pb(ctx, f"p_up{s}", [P, NG, 512]) for s in range(2)]
            pdn = pb(ctx, "p_down", [P, 2, 512])
            ws = WeightStream(ctx, "wup", ps)
            wd_raw = sb(ctx, "w_down_raw", [P, 2, D])
            wd = sb(ctx, "w_down_halves", [P, 2, 2, D], F32R)
            ff = sb(ctx, "mlp_hidden", [P, 2, 2, T], F32R)
            U = sb(ctx, "gate_in", [P, 2 + NP_])
            Us = sb(ctx, "gate_in_samples", [P, NB, 2 + LS])
            y = sb(ctx, "gate_conv", [P, T])
            fw = sb(ctx, "ffn_taps", [P, 3])
            TURNS, DOWNS = KF // 2, NT * 2
            w_gate, w_val, w_dn = w_up[:, 0:DFF], w_up[:, DFF:], io["w_down"][0]
            fcw = cols[:, o_fcw:o_fcw + 3 * KF].rearrange("p (w f) -> p w f", f=KF)
            fst = cols[:, o_fst:o_fst + n_fst].rearrange("p (b w f) -> p b w f", w=2, f=KF)
            nfs = new_ffn[:, 0:n_fst].rearrange("p (b w f) -> p b w f", w=2, f=KF)
            nfp = new_ffn[:, n_fst:].rearrange("p (w f) -> p w f", f=KF)

            with nc.Block() as block:
                @block.sync
                def _(sp):
                    ws.start(sp)
                    give_slots(sp, ["down_free"])
                    with sp.Fori(0, TURNS, 1) as g:
                        for f in range(2):
                            col = bass.ds((g * 2 + f) * P, P)
                            ws.load(sp, g * 2 + f, 0, w_gate[:, col])
                            ws.load(sp, g * 2 + f, 1, w_val[:, col])
                        hold(sp, "wd_lo", g)
                        sp.dma_start(wd_raw[:, :, :], w_dn[bass.ds(g * (2 * P), 2 * P), :]
                                     .rearrange("(f p) n -> p f n", p=P)).then_inc(sem("wd_in"), 16)

                @block.gpsimd
                def _(pool):
                    pool.memset(out_sum[:, :, :, :], 0.0).then_inc(sem("sum_zero"), 1)
                    with pool.Fori(0, TURNS, 1) as g:
                        for n in range(4):
                            ws.split(pool, g * 2 + n // 2, n % 2, KD)
                        hi, lo = wd[:, 0, :, :], wd[:, 1, :, :]
                        pool.wait_ge(sem("wd_in"), g * 16 + 16)
                        pool.wait_ge(sem("down_mm"), g * DOWNS)
                        pool.tensor_tensor(hi, wd_raw[:, :, :], ones[:, 0:1].unsqueeze(1).to_broadcast([P, 2, D]),
                                           ALU.mult).then_inc(sem("wd_hi"), 1)
                        pool.wait_ge(sem("wd_hi"), g + 1)
                        pool.tensor_tensor(lo, wd_raw[:, :, :], f32(hi), ALU.subtract).then_inc(sem("wd_lo"), 1)

                @block.tensor
                def _(pe):
                    def up(g, f):
                        ws.product(pe, g * 2 + f, 0, KD, h)
                        ws.product(pe, g * 2 + f, 1, KD, h)

                    def down(g):
                        pe.wait_ge(sem("ff_lo"), g * 2 + 2)
                        pe.wait_ge(sem("wd_lo"), g + 1)
                        for n in range(DOWNS):
                            t, half = n // 2, n % 2
                            pe.wait_ge(sem("down_free"), g * DOWNS + (n + 1))
                            for j, (a, b) in enumerate(PASSES):
                                for f in range(2):
                                    last = pe.matmul(pdn[:, half, :], ff[:, a, f, t * P:(t + 1) * P],
                                                     wd[:, b, f, half * HALF:(half + 1) * HALF],
                                                     start=(j == 0 and f == 0), stop=(j == 2 and f == 1))
                            last.then_inc(sem("down_mm"), 1)

                    up(0, 0)
                    up(0, 1)
                    with pe.Fori(1, TURNS, 1) as g:
                        up(g, 0)
                        down(g - 1)
                        up(g, 1)
                    down(TURNS - 1)

                @block.scalar
                def _(act):
                    def hidden(g, f):
                        n = g * 2 + f
                        gate = ps[0]
                        ws.arrived(act, n, 0)
                        act.wait_ge(sem("conv_read"), n)
                        act.activation(U[:, 2:2 + 2 * G].rearrange("p (g t) -> p g t", t=G), gate[:, 0:2, 0:G], ACT.Copy) \
                            .then_inc(sem("gate_rows"), 1)
                        act.activation(U[:, 2 + 2 * G:], gate[:, 2, 0:REST], ACT.Copy).then_inc(sem("gate_rows"), 1)
                        act.activation(Us[:, :, 2:], gate[:, 2, REST:G].rearrange("p (b t) -> p b t", t=LS), ACT.Copy) \
                            .then_inc(sem("wup_pfree0"), 1)
                        act.wait_ge(sem("conv_read"), n + 1)
                        act.activation(y[:, :], y[:, :], ACT.Silu).then_inc(sem("gate_silu"), 1)
                        act.wait_ge(sem("ff_full"), n + 1)
                        act.wait_ge(sem("down_mm"), g * DOWNS)
                        act.activation(ff[:, 0, f, :], y[:, :], ACT.Copy).then_inc(sem("ff_hi"), 1)

                    with act.Fori(0, TURNS, 1) as g:
                        hidden(g, 0)
                        hidden(g, 1)

                @block.vector
                def _(dve):
                    STEPS = 7

                    def hidden(g, f):
                        n = g * 2 + f
                        one = bass.ds(n, 1)
                        link = Link(dve, sem("mlp_step"), n * STEPS)
                        dve.tensor_scalar(Us[:, :, 0:2].unsqueeze(3), fst[:, :, :, one], 1.0, None, ALU.mult) \
                            .then_inc(sem("history"), 1)
                        link(dve.tensor_scalar(fw[:, :].unsqueeze(2), fcw[:, :, one], 1.0, None, ALU.mult))
                        dve.wait_ge(sem("history"), n + 1)
                        dve.wait_ge(sem("wup_pfree0"), n + 2)
                        dve.wait_ge(sem("ff_lo"), n)
                        conv3(dve, link, U, Us, y, [fw[:, w:w + 1] for w in range(3)])
                        dve.tensor_scalar(nfs[:, :, :, one], Us[:, :, LS:].unsqueeze(3), 1.0, None, ALU.mult) \
                            .then_inc(sem("new_history"), 1)
                        dve.tensor_scalar(nfp[:, :, one], U[:, NP_:].unsqueeze(2), 1.0, None, ALU.mult) \
                            .then_inc(sem("conv_read"), 1)
                        ws.arrived(dve, n, 1)
                        dve.wait_ge(sem("gate_silu"), n + 1)
                        dve.tensor_tensor(by_group(y[:, :]), by_group(y[:, :]), groups(ps[1]), ALU.mult) \
                            .then_inc(sem("ff_full"), 1)
                        dve.wait_ge(sem("ff_full"), n + 1)
                        dve.sem_inc(sem("wup_pfree1"), 1)

                    def low(g, f):
                        dve.wait_ge(sem("ff_hi"), g * 2 + f + 1)
                        dve.tensor_tensor(ff[:, 1, f, :], y[:, :], f32(ff[:, 0, f, :]), ALU.subtract).then_inc(sem("ff_lo"), 1)

                    def add_down(g):
                        for n in range(DOWNS):
                            part = out_sum[:, n // 2, n % 2, :]
                            dve.wait_ge(sem("down_mm"), g * DOWNS + (n + 1))
                            dve.wait_ge(sem("down_free"), g * DOWNS + 2)
                            dve.tensor_tensor(part, part, pdn[:, n % 2, :], ALU.add).then_inc(sem("down_free"), 1)

                    dve.memset(U[:, 0:2], 0.0).then_inc(sem("u_zero"), 1)
                    dve.wait_ge(sem("u_zero"), 1)
                    dve.wait_ge(sem("sum_zero"), 1)
                    hidden(0, 0)
                    low(0, 0)
                    hidden(0, 1)
                    low(0, 1)
                    with dve.Fori(1, TURNS, 1) as g:
                        hidden(g, 0)
                        add_down(g - 1)
                        low(g, 0)
                        hidden(g, 1)
                        low(g, 1)
                    add_down(TURNS - 1)

        new_semaphores()
        y_rows, y_sample_rows = token_rows("y_prompt", "y_sample")
        ctx = ExitStack()
        with ctx:
            X = sb(ctx, "x1_tile", [P, 2, D])
            gate = sb(ctx, "gate_mlp", [P, 2, D])
            scratch = sb(ctx, "squares_out", [P, 2, D])
            stat = sb(ctx, "stat_out", [P, 2, 4])
            rows = sb(ctx, "history_rows", [P, 6, P])
            prow = pb(ctx, "p_history", [P, 2, 512])
            n_s = 2 * NB * KB
            ffn_s = io["ffn_sample"].rearrange("a b w (k p) -> (a b w k) p", p=P)
            HISTORY = [(new_ffn[:, 0:P], ffn_s[0:P, :]), (new_ffn[:, P:2 * P], ffn_s[P:2 * P, :]),
                       (new_ffn[:, 2 * P:n_fst], ffn_s[2 * P:, :]),
                       (new_ffn[:, n_fst:], io["ffn_prompt"].rearrange("a b w (k p) -> (a b w k) p", p=P)),
                       (new_conv[:, 0:n_s], io["conv_sample"].rearrange("a b w (k p) -> (a b w k) p", p=P)),
                       (new_conv[:, n_s:], io["conv_prompt"].rearrange("a b w (k p) -> (a b w k) p", p=P))]

            with nc.Block() as block:
                @block.sync
                def _(sp):
                    load_gate(sp, gate[:, 0, :], 1, False, "gate_in")
                    load_gate(sp, gate[:, 1, :], 1, True, "gate_in")

                    def load(u, s, src):
                        hold(sp, f"y_out{s}", u * 16)
                        sp.dma_start(X[:, s, :], src).then_inc(sem(f"x1_in{s}"), 16)

                    def store(u, s, dst):
                        hold(sp, "y", u * 2 + s + 1)
                        sp.dma_start(dst, X[:, s, :]).then_inc(sem(f"y_out{s}"), 16)

                    load(0, 0, x1_scratch[0:P, :])
                    load(0, 1, x1_scratch[P:2 * P, :])
                    for n, (src, dst) in enumerate(HISTORY):
                        sp.wait_ge(sem("history_rows"), n + 1)
                        sp.dma_start(dst, rows[0:src.shape[1], n, :]).then_inc(sem("history_out"), 16)
                    with sp.Fori(0, NPT // 2 - 1, 1) as i:
                        for s in range(2):
                            store(i, s, y_rows(i * 2 + s))
                            load(i + 1, s, x1_scratch[bass.ds((i * 2 + s + 2) * P, P), :])
                    store(NPT // 2 - 1, 0, y_rows(NPT - 2))
                    load(NPT // 2, 0, x1_scratch[NPT * P:, :])
                    store(NPT // 2 - 1, 1, y_rows(NPT - 1))
                    store(NPT // 2, 0, y_sample_rows)
                    sp.wait_ge(sem("y_out0"), 16 * (NPT // 2 + 1))
                    sp.wait_ge(sem("y_out1"), 16 * (NPT // 2))
                    sp.wait_ge(sem("history_out"), 16 * len(HISTORY))

                @block.tensor
                def _(pe):
                    for n, (src, _) in enumerate(HISTORY):
                        last = pe.transpose(prow[0:src.shape[1], n // 4, (n % 4) * P:(n % 4 + 1) * P], src, ident[:, :])
                    last.then_inc(sem("history_T"), 1)

                @block.scalar
                def _(act):
                    def norm(u, s):
                        t = u * 2 + s
                        link = Link(act, sem("out_norm"), t * 2)
                        flat = lambda ap: ap.rearrange("p (a n) -> p a n", n=HALF)
                        act.wait_ge(sem("y"), u * 2)
                        tile = M[:, :, :].rearrange("p k t -> p (k t)")[:, bass.ds(t * D, D)]
                        link(act.activation(scratch[:, 1, :], tile, ACT.Square, accum_out=stat[:, s, 0:1]))
                        link(act.activation(stat[:, s, 1:2], stat[:, s, 0:1], ACT.Ln, scale=1.0 / D, bias=eps[:, :]))
                        act.activation(stat[:, s, 2:3], stat[:, s, 1:2], ACT.Exp, scale=-0.5).then_inc(sem("out_rstd"), 1)

                    pairs(act, NPT, norm)
                    norm(NPT // 2, 0)

                @block.vector
                def _(dve):
                    dve.wait_ge(sem("history_T"), 1)
                    for n, (src, _) in enumerate(HISTORY):
                        r = src.shape[1]
                        dve.tensor_copy(rows[0:r, n, :], prow[0:r, n // 4, (n % 4) * P:(n % 4 + 1) * P]) \
                            .then_inc(sem("history_rows"), 1)
                    dve.wait_ge(sem("gate_in"), 16 * (1 + NB))

                    def combine(u, s, which):
                        t = u * 2 + s
                        tile = M[:, :, :].rearrange("p k t -> p (k t)")[:, bass.ds(t * D, D)]
                        dve.wait_ge(sem("out_rstd"), t + 1)
                        dve.wait_ge(sem("y"), t)
                        dve.scalar_tensor_tensor(scratch[:, 0, :], tile, stat[:, s, 2:3], gate[:, which, :], ALU.mult, ALU.mult) \
                            .then_inc(sem("out_scaled"), 1)
                        dve.wait_ge(sem("out_scaled"), t + 1)
                        dve.wait_ge(sem(f"x1_in{s}"), u * 16 + 16)
                        dve.tensor_tensor(X[:, s, :], X[:, s, :], scratch[:, 0, :], ALU.add).then_inc(sem("y"), 1)

                    pairs(dve, NPT, lambda u, s: combine(u, s, 0))
                    combine(NPT // 2, 0, 1)


_ORDER = ["x_prompt", "x_sample", "state_hgrn", "state_conv", "state_ffn_conv", "c_prompt", "c_sample", "w_ada",
          "b_ada", "g_pre_mix", "g_post_mix", "g_pre_ffn", "g_post_ffn", "w_in", "hgrn_lb_logits", "hgrn_norm",
          "w_pa", "conv_w", "w_pb", "w_bgate", "w_o", "w_up", "ffn_conv_w", "w_down"]


def output_shapes(shape):
    depth, batch, heads, dk, dv = shape["state_hgrn"]
    return {
        "y_prompt": shape["x_prompt"],
        "y_sample": shape["x_sample"],
        "hgrn_prompt": (depth, shape["x_prompt"][0], heads, dk, dv),
        "conv_prompt": (depth, shape["x_prompt"][0], *shape["state_conv"][2:]),
        "ffn_prompt": (depth, shape["x_prompt"][0], *shape["state_ffn_conv"][2:]),
        "hgrn_sample": shape["state_hgrn"],
        "conv_sample": shape["state_conv"],
        "ffn_sample": shape["state_ffn_conv"],
    }


def kernel(**inputs):
    import numpy as np
    import concourse.bacc as bacc
    from concourse.bass_utils import run_bass_kernel_spmd

    nc = bacc.Bacc("TRN2", target_bir_lowering=False, num_devices=1)
    arrays = {name: np.ascontiguousarray(inputs[name]) for name in _ORDER}
    io = {name: nc.dram_tensor(name, a.shape, F32, kind="ExternalInput").ap() for name, a in arrays.items()}
    outs = output_shapes({name: tuple(a.shape) for name, a in arrays.items()})
    for name, shape in outs.items():
        io[name] = nc.dram_tensor(name, tuple(shape), F32, kind="ExternalOutput").ap()
    build_trunk(nc, io)
    result = run_bass_kernel_spmd(nc, [arrays], core_ids=[0])
    return tuple(result.results[0][name] for name in outs)
```

```python
from contextlib import ExitStack

import concourse.bass as bass
from concourse import mybir

P = 128
F32 = mybir.dt.float32
F32R = mybir.dt.float32r
U32 = mybir.dt.uint32
ALU = mybir.AluOpType
ACT = mybir.ActivationFunctionType
NEG_HUGE = -3.0e38
LN_FLOOR = 2.0 ** -63
EPS = 1e-6


class Link:

    def __init__(self, eng, sem, base=0):
        self.eng, self.sem, self.base, self.n = eng, sem, base, 0

    def __call__(self, ins):
        self.n += 1
        ins.then_inc(self.sem, 1)
        self.eng.wait_ge(self.sem, self.base + self.n)


def build_trunk(nc, io):
    NP_, D = io["x_prompt"].shape[1:]
    NB, LS = io["x_sample"].shape[:2]
    DFF = io["w_down"].shape[1]
    AW = io["w_pa"].shape[1]
    BW = io["w_pb"].shape[1]
    H = AW // P
    T = NP_ + NB * LS
    KD = D // P
    KF = DFF // P
    KB = BW // P
    NT = T // P
    NPT = NP_ // P
    NG, G = 3, T // 3
    C = NB + 1
    HALF = D // 2
    assert NB * LS == P and G <= 512 and io["state_hgrn"].shape[0] == 1 and KF % 2 == 0
    assert NG * G == T and 2 * G <= NP_ < 3 * G and H == KB == 4 and H * P == 512
    REST = NP_ - 2 * G

    w_in, w_bgate, w_up = io["w_in"][0], io["w_bgate"][0], io["w_up"][0]

    gate_scratch = nc.dram_tensor("gate_rows_scratch", (2, C, D), F32, kind="Internal").ap()
    kfv_scratch = nc.dram_tensor("k_logf_v_scratch", (3, P, H, T), F32, kind="Internal").ap()
    x1_scratch = nc.dram_tensor("x_after_mixer_scratch", (T, D), F32, kind="Internal").ap()

    top = ExitStack()
    sems, kept, parts = {}, {}, [1]

    def sem(name):
        if name.startswith("ws_"):
            if name not in kept:
                kept[name] = nc.alloc_semaphore(name)
            return kept[name]
        if name not in sems:
            sems[name] = nc.alloc_semaphore(f"{name}_part{parts[0]}")
        return sems[name]

    def new_semaphores():
        nc.clear_and_free_semaphores(list(sems.values()))
        sems.clear()
        parts[0] += 1
        nc.all_engine_barrier()

    def hold(sp, name, value):
        sp.wait_ge(sem(name), value)
        sp.sem_inc(sem("sp_passed"), 1)

    def sb(ctx, name, shape, dt=F32):
        return ctx.enter_context(nc.sbuf_tensor(name, shape, dt))

    def pb(ctx, name, shape):
        return ctx.enter_context(nc.psum_tensor(name, shape, F32))

    def f32(ap):
        return ap.bitcast(F32)

    PASSES = ((0, 0), (0, 1), (1, 0))
    SLOTS = 2

    def give_slots(eng, names):
        for name in names:
            eng.sem_inc(sem(name), SLOTS)

    def pairs(eng, count, body):
        with eng.Fori(0, count // 2, 1) as i:
            for s in range(2):
                body(i, s)

    def start_at_one(eng, names):
        for name in names:
            eng.sem_inc(sem(name), 1)

    class WeightStream:

        def __init__(self, ctx, name):
            self.name = name
            self.raw = sb(ctx, name + "_raw", [P, 2, KD * P])
            self.halves = sb(ctx, name + "_halves", [P, 2, 2, KD * P], F32R)

        def start(self, eng):
            eng.sem_inc(sem(self.name + "_lo"), SLOTS)
            eng.sem_inc(sem(self.name + "_mm"), SLOTS * NG)

        def load(self, sp, u, s, src):
            k = src.shape[0] // P
            hold(sp, self.name + "_lo", u * 2 + (s + 1))
            sp.dma_start(self.raw[:, s, 0:k * P].rearrange("p (k m) -> p k m", m=P),
                         src.rearrange("(k p) m -> p k m", p=P)).then_inc(sem(f"{self.name}_in{s}"), 16)

        def split(self, pool, u, s, k):
            raw, hi, lo = self.raw[:, s, :k * P], self.halves[:, s, 0, :k * P], self.halves[:, s, 1, :k * P]
            pool.wait_ge(sem(f"{self.name}_in{s}"), u * 16 + 16)
            pool.wait_ge(sem(self.name + "_mm"), u * (2 * NG) + (s + 1) * NG)
            pool.tensor_tensor(hi, raw, ones[:, 0:1].to_broadcast([P, k * P]), ALU.mult).then_inc(sem(self.name + "_hi"), 1)
            pool.wait_ge(sem(self.name + "_hi"), u * 2 + (s + 1))
            pool.tensor_tensor(lo, raw, f32(hi), ALU.subtract).then_inc(sem(self.name + "_lo"), 1)

        def product(self, pe, u, s, k, moving, bank, between=None):
            pe.wait_ge(sem(self.name + "_lo"), u * 2 + (s + 3))
            for g in range(NG):
                out, free, value = bank(g)
                pe.wait_ge(sem(free), value)
                for j, (a, b) in enumerate(PASSES):
                    for kt in range(k):
                        last = pe.matmul(out[:, 0:G], self.halves[:, s, a, kt * P:(kt + 1) * P],
                                         moving[:, b, kt, g * G:(g + 1) * G],
                                         start=(j == 0 and kt == 0), stop=(j == 2 and kt == k - 1))
                    if j == 2:
                        last.then_inc(sem(self.name + "_mm"), 1)
                    if between is not None:
                        between(g * 3 + j)

        def arrived(self, eng, u, s, g=NG - 1):
            eng.wait_ge(sem(self.name + "_mm"), u * (2 * NG) + (s * NG + SLOTS * NG + g + 1))

    def groups(ps):
        return ps[:, :, 0:G]

    def by_group(ap):
        return ap.rearrange("p (g t) -> p g t", t=G)

    with top:
        ident = sb(top, "ident", [P, P])
        ones = sb(top, "ones", [P, P])
        eps = sb(top, "eps", [P, 1])
        cs = sb(top, "silu_c", [P, C * KD])
        cols = sb(top, "param_cols", [P, 6 * P])
        scale1 = sb(top, "scale1", [P, KD, C])
        shift1 = sb(top, "shift1", [P, KD, C])
        scale2 = sb(top, "scale2", [P, KD, C])
        shift2 = sb(top, "shift2", [P, KD, C])
        log_lb = sb(top, "log_lower_bound", [P, H])
        log_1mlb = sb(top, "log_one_minus_lb", [P, H])
        new_conv = sb(top, "new_conv", [P, 2 * NB * KB + 2 * KB])
        new_ffn = sb(top, "new_ffn", [P, 2 * NB * KF + 2 * KF])
        h = sb(top, "h", [P, 2, KD, T], F32R)
        M = sb(top, "middle", [P, KD, T])

        def two_slots(ps, name, u, s):
            return lambda g: (ps[s][:, g, :], f"{name}_pfree{s}", u + 1)

        def modulate(dve, name, u, s, pT, full, scale, shift, sample=False):
            t = u * 2 + s
            buf = full[:, s % full.shape[1], :].rearrange("p (k t) -> p k t", t=P)
            src = pT[:, s].rearrange("p a (k t) -> p (a k) t", t=P)
            if sample:
                view = lambda ap: ap.rearrange("p k (b l) -> p k b l", l=LS)
                sc, sh = (m[:, :, 1:C].unsqueeze(3).to_broadcast([P, KD, NB, LS]) for m in (scale, shift))
            else:
                view = lambda ap: ap
                sc, sh = (m[:, :, 0:1].to_broadcast([P, KD, P]) for m in (scale, shift))
            dve.wait_ge(sem(name + "_xT"), t + 3)
            dve.wait_ge(sem(name + "_lo"), t + (2 if full.shape[1] == 1 else 1))
            dve.tensor_tensor(view(buf), view(src), sc, ALU.mult).then_inc(sem(name + "_pT"), 1)
            dve.wait_ge(sem(name + "_pT"), t + 3)
            dve.tensor_tensor(view(buf), view(buf), sh, ALU.add).then_inc(sem(name + "_h"), 1)

        def halves_of_h(pool, name, u, s, full):
            t = u * 2 + s
            tok = bass.ds(t * P, P)
            buf = full[:, s % full.shape[1], :].rearrange("p (k t) -> p k t", t=P)
            pool.wait_ge(sem(name + "_h"), t + 1)
            pool.tensor_tensor(h[:, 0, :, tok], buf, ones[:, 0:1].unsqueeze(1).to_broadcast([P, KD, P]), ALU.mult) \
                .then_inc(sem(name + "_hi"), 1)
            pool.wait_ge(sem(name + "_hi"), t + 1)
            pool.tensor_tensor(h[:, 1, :, tok], buf, f32(h[:, 0, :, tok]), ALU.subtract).then_inc(sem(name + "_lo"), 1)

        def conv3(dve, link, U, Us, y, w):
            ys = y[:, NP_:].rearrange("p (b t) -> p b t", t=LS)
            for out, u, n in ((y[:, 0:NP_], U[:, :], NP_), (ys, Us[:, :, :], LS)):
                tap = lambda d: u[..., d:d + n]
                link(dve.tensor_scalar(out, tap(0), w[0], None, ALU.mult))
                link(dve.scalar_tensor_tensor(out, tap(1), w[1], out, ALU.mult, ALU.add))
                link(dve.scalar_tensor_tensor(out, tap(2), w[2], out, ALU.mult, ALU.add))

        def transposes(pe, name, u, s, xn, pT):
            t = u * 2 + s
            pe.wait_ge(sem(name + "_xn"), t + 2)
            pe.wait_ge(sem(name + "_pT"), t + 1)
            for k in range(KD):
                last = pe.transpose(pT[:, s, k // 4, (k % 4) * P:(k % 4 + 1) * P], xn[:, s % xn.shape[1], k * P:(k + 1) * P],
                                    ident[:, :])
            last.then_inc(sem(name + "_xT"), 1)

        o_bada, o_fcw, o_gmix = 0, 6 * KD, 6 * KD + 3 * KF
        o_gffn = P
        o_cw = o_gffn + KD
        o_an = o_cw + 3 * KB
        o_lb = o_an + 1
        o_gpost = o_lb + H
        o_c = o_gpost + 2 * KD
        o_fst = 2 * P
        n_fst = 2 * NB * KF
        o_cst = 5 * P
        n_cst = 2 * NB * KB
        stack_rows = [o_gmix + KD, o_c + C * KD - P, P, P, n_fst - 2 * P, n_cst]
        assert max(stack_rows) <= P

        def state_ffn_cols(f):
            return cols[:, o_fst:o_fst + n_fst].rearrange("p (bw f) -> p f bw", f=KF)[:, f]

        mixer = ExitStack()
        ws = WeightStream(mixer, "ws")
        bada = cols[:, o_bada:o_bada + 6 * KD].rearrange("p (s k) -> p s k", k=KD)
        cs_k = cs[:, :].rearrange("p (c k) -> p k c", k=KD)

        def ada_tile(pe, out, w):
            for k in range(KD):
                last = pe.matmul(out, w[:, k, :], cs_k[:, k, :], start=(k == 0), stop=(k == KD - 1))
            return last

        ctx = ExitStack()
        with ctx:
            rows = sb(ctx, "param_rows", [P, 6, P])
            wada = (sb(ctx, "w_ada_section", [P, KD, D])[:, :, :], M[:, :, 0:D])
            tiny = sb(ctx, "lb_steps", [P, 8, H])
            xt = sb(ctx, "x_tile", [P, 2, D])
            xn = sb(ctx, "x_normed", [P, 2, D])
            junk = sb(ctx, "squares", [P, D])
            stat = sb(ctx, "stat", [P, 2, 4])
            hf = sb(ctx, "h_full", [P, 2, D])
            pcol = pb(ctx, "p_cols", [P, 2, 512])
            pada = pb(ctx, "p_ada", [P, 2, 512])
            pT = pb(ctx, "p_xT", [P, 2, 2, 512])
            xp_dram = io["x_prompt"][0]
            xs_dram = io["x_sample"].rearrange("b l d -> (b l) d")
            N_ROWS_IN = 15

            with nc.Block() as block:
                @block.sync
                def _(sp):
                    ws.start(sp)
                    give_slots(sp, ["in_xT", "in_pT", "in_lo"])
                    start_at_one(sp, ["in_xn"])

                    def rows_in(stack, r, src):
                        sp.dma_start(rows[r:r + src.shape[0], stack, :], src).then_inc(sem("rows_in"), 16)

                    rows_in(1, o_c - P, io["c_prompt"].rearrange("b (k p) -> (b k) p", p=P))
                    rows_in(1, o_c - P + KD, io["c_sample"].rearrange("b (k p) -> (b k) p", p=P))
                    rows_in(1, 0, io["g_pre_ffn"].rearrange("a (k p) -> (a k) p", p=P))
                    rows_in(1, o_cw - P, io["conv_w"].rearrange("a w (k p) -> (a w k) p", p=P))
                    rows_in(1, o_an - P, io["hgrn_norm"])
                    rows_in(1, o_lb - P, io["hgrn_lb_logits"].rearrange("a (k p) -> (a k) p", p=P))
                    rows_in(1, o_gpost - P, io["g_post_mix"].rearrange("a (k p) -> (a k) p", p=P))
                    rows_in(1, o_gpost - P + KD, io["g_post_ffn"].rearrange("a (k p) -> (a k) p", p=P))
                    rows_in(0, o_bada, io["b_ada"].rearrange("a (k p) -> (a k) p", p=P))
                    rows_in(0, o_fcw, io["ffn_conv_w"].rearrange("a w (k p) -> (a w k) p", p=P))
                    rows_in(0, o_gmix, io["g_pre_mix"].rearrange("a (k p) -> (a k) p", p=P))
                    fst = io["state_ffn_conv"].rearrange("a b w (k p) -> (a b w k) p", p=P)
                    for n in range(3):
                        rows_in(2 + n, 0, fst[n * P:min((n + 1) * P, n_fst), :])
                    rows_in(5, 0, io["state_conv"].rearrange("a b w (k p) -> (a b w k) p", p=P))
                    for n, s in enumerate((1, 0)):
                        sp.dma_start(wada[n], io["w_ada"][0, :, s * D:(s + 1) * D]
                                     .rearrange("(k p) n -> p k n", p=P)).then_inc(sem(f"wada_in{n}"), 16)
                    for s in range(2):
                        ws.load(sp, 0, s, w_in[:, s * P:(s + 1) * P])

                @block.gpsimd
                def _(pool):
                    pool.memset(ident[:, :], 0.0).then_inc(sem("ident_zero"), 1)
                    pool.memset(ones[:, :], 1.0).then_inc(sem("consts"), 1)
                    pool.memset(eps[:, :], EPS).then_inc(sem("consts"), 1)
                    pool.wait_ge(sem("ident_zero"), 1)
                    pool.affine_select(out=ident[:, :], in_=ident[:, :], compare_op=ALU.not_equal, fill=1.0,
                                       base=0, pattern=[[-1, P]], channel_multiplier=1).then_inc(sem("ident"), 1)
                    pairs(pool, NPT, lambda u, s: halves_of_h(pool, "in", u, s, hf))
                    halves_of_h(pool, "in", NPT // 2, 0, hf)
                    for s in range(2):
                        ws.split(pool, 0, s, KD)

                @block.scalar
                def _(act):
                    act.dma_start(xt[:, 0], xp_dram[0:P, :]).then_inc(sem("x_in0"), 16)
                    act.wait_ge(sem("cols"), 6)
                    act.activation(cs[:, :], cols[:, o_c:o_c + C * KD], ACT.Silu).then_inc(sem("cs"), 1)
                    act.preload_act_table_set("natural_log_exp_and_others")
                    act.wait_ge(sem("lb_shifted"), 1)
                    act.activation(tiny[:, 1], tiny[:, 0], ACT.Exp).then_inc(sem("lb_exp"), 1)
                    act.wait_ge(sem("lb_ready"), 1)
                    act.activation(log_1mlb[:, :], tiny[:, 5], ACT.Ln).then_inc(sem("lb_logs"), 1)
                    act.activation(tiny[:, 7], tiny[:, 6], ACT.Ln).then_inc(sem("lb_logs"), 1)
                    act.wait_ge(sem("consts"), 2)

                    def norm(u, s, following):
                        t = u * 2 + s
                        if following is not None:
                            act.wait_ge(sem("in_xn"), t + 1)
                            act.dma_start(xt[:, 1 - s], following).then_inc(sem(f"x_in{1 - s}"), 16)
                        act.wait_ge(sem(f"x_in{s}"), u * 16 + 16)
                        link = Link(act, sem("in_norm"), t * 3)
                        link(act.activation(junk[:, :], xt[:, s], ACT.Square, accum_out=stat[:, s, 0:1]))
                        link(act.activation(stat[:, s, 1:2], stat[:, s, 0:1], ACT.Ln, scale=1.0 / D, bias=eps[:, :]))
                        link(act.activation(stat[:, s, 2:3], stat[:, s, 1:2], ACT.Exp, scale=-0.5))
                        act.wait_ge(sem("in_xT"), t + 1)
                        act.activation(xn[:, s], xt[:, s], ACT.Copy, scale=stat[:, s, 2:3]).then_inc(sem("in_xn"), 1)

                    with act.Fori(0, NPT // 2 - 1, 1) as i:
                        for s in range(2):
                            norm(i, s, xp_dram[bass.ds((i * 2 + s + 1) * P, P), :])
                    norm(NPT // 2 - 1, 0, xp_dram[(NPT - 1) * P:, :])
                    norm(NPT // 2 - 1, 1, xs_dram)
                    norm(NPT // 2, 0, None)

                @block.vector
                def _(dve):
                    dve.wait_ge(sem("rows_T"), 1)
                    for n, r in enumerate(stack_rows):
                        dve.tensor_copy(cols[:, n * P:n * P + r], pcol[:, n // 4, (n % 4) * P:(n % 4) * P + r]) \
                            .then_inc(sem("cols"), 1)
                    dve.wait_ge(sem("cols"), 6)
                    lg = cols[:, o_lb:o_lb + H]
                    link = Link(dve, sem("lb_step"))
                    dve.tensor_tensor(tiny[:, 0], lg, lg, ALU.subtract).then_inc(sem("lb_shifted"), 1)
                    dve.wait_ge(sem("lb_exp"), 1)
                    link(dve.reciprocal(tiny[:, 2], tiny[:, 1]))
                    link(dve.tensor_tensor(tiny[:, 3], tiny[:, 1], tiny[:, 2], ALU.mult))
                    link(dve.tensor_tensor(tiny[:, 4], tiny[:, 3], tiny[:, 3], ALU.subtract))
                    link(dve.tensor_scalar(tiny[:, 5], tiny[:, 4], -1.0, 1.0, ALU.mult, ALU.add))
                    link(dve.tensor_scalar(tiny[:, 6], tiny[:, 4], LN_FLOOR, None, ALU.max))
                    dve.tensor_scalar(log_lb[:, :], tiny[:, 4], 0.0, NEG_HUGE, ALU.is_le, ALU.mult) \
                        .then_inc(sem("lb_ready"), 1)
                    dve.wait_ge(sem("lb_ready"), 1)
                    dve.wait_ge(sem("lb_logs"), 2)
                    dve.tensor_tensor(log_lb[:, :], log_lb[:, :], tiny[:, 7], ALU.add).then_inc(sem("lb_ready"), 1)

                    def ada(n, dst):
                        dve.wait_ge(sem("ada_mm"), n + 1)
                        dve.tensor_tensor(dst[:, :, :], pada[:, n, 0:KD * C].rearrange("p (k c) -> p k c", c=C),
                                          bada[:, 1 - n, :].unsqueeze(2).to_broadcast([P, KD, C]), ALU.add) \
                            .then_inc(sem("ada_sum"), 1)
                        dve.wait_ge(sem("ada_sum"), n + 1)

                    ada(0, scale1)
                    dve.scalar_tensor_tensor(scale1[:, :, :], scale1[:, :, :], 1.0,
                                             cols[:, o_gmix:o_gmix + KD].unsqueeze(2).to_broadcast([P, KD, C]),
                                             ALU.add, ALU.mult).then_inc(sem("ada_gain"), 1)
                    dve.wait_ge(sem("ada_gain"), 1)
                    ada(1, shift1)
                    pairs(dve, NPT, lambda u, s: modulate(dve, "in", u, s, pT, hf, scale1, shift1))
                    modulate(dve, "in", NPT // 2, 0, pT, hf, scale1, shift1, sample=True)

                @block.tensor
                def _(pe):
                    pe.wait_ge(sem("ident"), 1)
                    pe.wait_ge(sem("rows_in"), 16 * N_ROWS_IN)
                    for n, r in enumerate(stack_rows):
                        last = pe.transpose(pcol[:, n // 4, (n % 4) * P:(n % 4) * P + r], rows[0:r, n, :],
                                            ident[0:r, 0:r])
                    last.then_inc(sem("rows_T"), 1)
                    pe.wait_ge(sem("cs"), 1)

                    for n in range(2):
                        pe.wait_ge(sem(f"wada_in{n}"), 16)
                        for j in range(KD):
                            ada_tile(pe, pada[:, n, j * C:(j + 1) * C], wada[n][:, :, j * P:(j + 1) * P]) \
                                .then_inc(sem("ada_tiles"), 1)
                        pe.wait_ge(sem("ada_tiles"), (n + 1) * KD)
                        pe.sem_inc(sem("ada_mm"), 1)
                    pairs(pe, NPT, lambda u, s: transposes(pe, "in", u, s, xn, pT))
                    transposes(pe, "in", NPT // 2, 0, xn, pT)

        Q = sb(mixer, "q", [P, H, T])
        N_QFI = 3 * H
        ctx = ExitStack()
        with ctx:
            ps = [pb(ctx, f"p_proj{s}", [P, NG, 512]) for s in range(2)]
            pada = pb(ctx, "p_ada_rest", [P, 512])
            prow = pb(ctx, "p_gate_rows", [P, 512])
            ft = [M[:, n, :] for n in range(4)]
            kst, lst, vst = (M[:, 4 + n, :] for n in range(3))
            wada = sb(ctx, "w_ada_chunk", [P, 2, KD, 2 * P])
            ada = sb(ctx, "ada_rest", [P, 4, KD, C])
            gr = sb(ctx, "gate_rows", [C, 2, KD, P])
            AFTER = (2, 1, 2, 1, 1, 1)
            A_TURN = sum(AFTER)
            A_SECTION = KD // 2
            assert 2 * A_TURN == 4 * A_SECTION and H == 4
            ada_w = io["w_ada"][0]

            with nc.Block() as block:
                @block.sync
                def _(sp):
                    for s in range(2):
                        sp.sem_inc(sem(f"qfi_pfree{s}"), 1)
                    give_slots(sp, ["ada_done"])

                    def turn(i, ahead):
                        m = 0
                        for n in range(6):
                            for _ in range(AFTER[n]):
                                hold(sp, "ada_done", i * A_TURN + (m + 1))
                                sp.dma_start(wada[:, m % 2], ada_w[:, bass.ds(i * (2 * D) + 2 * D + m * 2 * P, 2 * P)]
                                             .rearrange("(k p) n -> p k n", p=P)).then_inc(sem(f"wada_chunk{m % 2}"), 16)
                                m += 1
                            ahead(i, n + 2)

                    def qfi(i, n):
                        if n < 6:
                            ws.load(sp, i * 3 + n // 2, n % 2, w_in[:, bass.ds(i * (2 * P) + (n // 2 * AW + n % 2 * P), P)])
                        else:
                            qfi(i + 1, n - 6)

                    turn(0, qfi)
                    turn(1, lambda i, n: qfi(i, n) if n < 6 else
                         ws.load(sp, 6, n % 2, w_in[:, (4 * AW + (1 + n % 2) * BW):(4 * AW + (1 + n % 2) * BW + P)]))
                    sp.wait_ge(sem("gate_rows"), 4)
                    sp.dma_start(gate_scratch.rearrange("n c (k p) -> c n k p", p=P), gr[:, :, :, :]).then_inc(sem("gate_out"), 16)
                    sp.wait_ge(sem("gate_out"), 16)

                @block.gpsimd
                def _(pool):
                    with pool.Fori(0, 2, 1) as i:
                        for n in range(2, 8):
                            ws.split(pool, i * 3 + n // 2, n % 2, KD)

                @block.tensor
                def _(pe):
                    with pe.Fori(0, 2, 1) as i:
                        m = 0
                        for n in range(6):
                            ws.product(pe, i * 3 + n // 2, n % 2, KD, h, two_slots(ps, "qfi", i * 3 + n // 2, n % 2))
                            for _ in range(AFTER[n]):
                                pe.wait_ge(sem(f"wada_chunk{m % 2}"), i * (A_TURN // 2 * 16) + (m // 2 + 1) * 16)
                                for t in range(2):
                                    at = bass.ds(i * (2 * A_TURN * C) + (2 * m + t) * C, C)
                                    last = ada_tile(pe, pada[:, at], wada[:, m % 2, :, t * P:(t + 1) * P])
                                last.then_inc(sem("ada_done"), 1)
                                m += 1
                    pe.wait_ge(sem("ada_ready"), 1)
                    for n in range(4):
                        if n:
                            pe.wait_ge(sem("gate_rows"), n)
                        for k in range(4):
                            src = ada[:, (0, 3)[n // 2], n % 2 * 4 + k, :]
                            last = pe.transpose(prow[0:C, k * P:(k + 1) * P], src, ident[:, :])
                        last.then_inc(sem("gate_T"), 1)

                @block.scalar
                def _(act):
                    link = Link(act, sem("f_act"))
                    for i in range(2):
                        for n in range(2):
                            u, s, hd = i * 3, n, i * 2 + n
                            ws.arrived(act, u, s)
                            act.activation(by_group(Q[:, hd, :]), groups(ps[s]), ACT.Silu).then_inc(sem(f"qfi_pfree{s}"), 1)
                        act.preload_act_table_set("natural_log_exp_and_others")
                        for n in range(2):
                            u, s, hd = i * 3 + 1, n, i * 2 + n
                            ws.arrived(act, u, s)
                            if hd:
                                act.wait_ge(sem("f_kexp"), hd)
                                act.wait_ge(sem("f_done"), hd)
                            link(act.activation(by_group(ft[1][:, :]), groups(ps[s]), ACT.Abs))
                            link(act.activation(ft[1][:, :], ft[1][:, :], ACT.Exp, scale=-1.0))
                            act.activation(ft[1][:, :], ft[1][:, :], ACT.Ln, bias=1.0).then_inc(sem("f_softplus"), 1)
                            act.wait_ge(sem("f_kexp"), hd + 1)
                            if hd:
                                act.wait_ge(sem("k_out"), 16 * hd)
                            act.activation(kst[:, :], ft[2][:, :], ACT.Exp, scale=-1.0, bias=log_1mlb[:, hd:hd + 1]) \
                                .then_inc(sem("f_k"), 1)
                            act.wait_ge(sem("f_c"), hd + 1)
                            link(act.activation(ft[3][:, :], ft[0][:, :], ACT.Abs, scale=-1.0, bias=log_lb[:, hd:hd + 1]))
                            link(act.activation(ft[3][:, :], ft[3][:, :], ACT.Exp, scale=-1.0))
                            act.activation(ft[3][:, :], ft[3][:, :], ACT.Ln, bias=1.0).then_inc(sem("f_lse"), 1)
                            act.wait_ge(sem("f_k"), hd + 1)
                            act.dma_start(kfv_scratch[0, :, hd, :], kst[:, :]).then_inc(sem("k_out"), 16)
                            act.wait_ge(sem("f_done"), hd + 1)
                            act.dma_start(kfv_scratch[1, :, hd, :], lst[:, :]).then_inc(sem("f_out"), 16)
                        for n in range(2):
                            u, s, hd = i * 3 + 2, n, i * 2 + n
                            ws.arrived(act, u, s)
                            if hd:
                                act.wait_ge(sem("v_out"), 16 * hd)
                            act.activation(by_group(vst[:, :]), groups(ps[s]), ACT.Copy).then_inc(sem(f"qfi_pfree{s}"), 1)
                            act.wait_ge(sem(f"qfi_pfree{s}"), 3 * i + 4)
                            act.dma_start(kfv_scratch[2, :, hd, :], vst[:, :]).then_inc(sem("v_out"), 16)
                    for name in ("k_out", "f_out", "v_out"):
                        act.wait_ge(sem(name), 16 * H)

                @block.vector
                def _(dve):
                    link = Link(dve, sem("f_dve"))
                    for hd in range(H):
                        i, s = hd // 2, hd % 2
                        z, step = groups(ps[s]), [by_group(f[:, :]) for f in ft]
                        lb = log_lb[:, hd:hd + 1]
                        ws.arrived(dve, i * 3 + 1, s)
                        dve.wait_ge(sem("f_softplus"), hd + 1)
                        link(dve.scalar_tensor_tensor(step[0], z, 0.0, step[1], ALU.min, ALU.subtract))
                        if hd:
                            dve.wait_ge(sem("f_k"), hd)
                        dve.scalar_tensor_tensor(step[2], z, 0.0, step[1], ALU.max, ALU.add).then_inc(sem("f_kexp"), 1)
                        dve.wait_ge(sem("f_kexp"), hd + 1)
                        dve.sem_inc(sem(f"qfi_pfree{s}"), 1)
                        dve.tensor_scalar(ft[0][:, :], ft[0][:, :], log_1mlb[:, hd:hd + 1], None, ALU.add) \
                            .then_inc(sem("f_c"), 1)
                        dve.wait_ge(sem("f_lse"), hd + 1)
                        if hd:
                            dve.wait_ge(sem("f_out"), 16 * hd)
                        dve.scalar_tensor_tensor(lst[:, :], ft[0][:, :], lb, ft[3][:, :], ALU.max, ALU.add) \
                            .then_inc(sem("f_done"), 1)
                        dve.wait_ge(sem("f_done"), hd + 1)
                    dve.wait_ge(sem("ada_done"), 2 * A_TURN + SLOTS)
                    link(dve.tensor_tensor(ada[:, :, :, :], pada[:, 0:4 * KD * C].rearrange("p (s k c) -> p s k c", s=4, c=C),
                                           bada[:, 2:6, :].unsqueeze(3).to_broadcast([P, 4, KD, C]), ALU.add))
                    gain = lambda at: cols[:, at:at + KD].unsqueeze(2).to_broadcast([P, KD, C])
                    for n in range(2):
                        link(dve.tensor_tensor(ada[:, 3 * n], ada[:, 3 * n], gain(o_gpost + n * KD), ALU.mult))
                    dve.sem_inc(sem("ada_ready"), 1)
                    link(dve.tensor_copy(shift2[:, :, :], ada[:, 1]))
                    link(dve.scalar_tensor_tensor(scale2[:, :, :], ada[:, 2], 1.0, gain(o_gffn), ALU.add, ALU.mult))
                    for n in range(4):
                        dve.wait_ge(sem("gate_T"), n + 1)
                        dve.tensor_copy(gr[:, n // 2, n % 2 * 4:n % 2 * 4 + 4, :],
                                        prow[0:C, :].rearrange("p (k t) -> p k t", t=P)).then_inc(sem("gate_rows"), 1)

        rec = ExitStack()
        HW = H * P
        R = sb(rec, "decay_in", [P, 2, HW])
        Kc = sb(rec, "k_chunk", [P, 2, HW])
        Vc = sb(rec, "v_chunk", [P, 2, HW])
        L = sb(rec, "decay_out", [P, HW])
        Er = sb(rec, "exp_in", [P, 2, HW // 2])
        El = sb(rec, "exp_out", [P, 2, HW // 2])
        Ql = sb(rec, "q_level", [P, 2, HW // 2])
        Kl = sb(rec, "k_level", [P, 2, HW])
        Qb = sb(rec, "q_decayed", [P, HW])
        Kd = sb(rec, "k_decayed", [P, HW])
        vt = sb(rec, "v_tokens", [P, HW])
        kdt = sb(rec, "kd_tokens", [P, HW])
        A = sb(rec, "attention", [P, HW])
        S = sb(rec, "state", [P, HW])
        LEVELS = P.bit_length() - 1
        SLEVELS = LS.bit_length() - 1
        masks = sb(rec, "level_masks", [P, LEVELS, P // 2])
        pl = pb(rec, "p_levels", [P, 2, HW // 2])
        pt = pb(rec, "p_tokens", [P, 512])
        po = pb(rec, "p_readout", [P, 512])
        px = pb(rec, "p_shared", [P, 512])
        a_norm = cols[:, o_an:o_an + 1]
        CHUNK_STARTS = ("on", "state", "kdt", "fin", "taken", "lnms")

        def heads(ap):
            return ap.rearrange("p (h t) -> p h t", h=H)

        def head(ap, hd):
            return ap[:, hd * P:(hd + 1) * P]

        def blocks(ap, l):
            return ap.rearrange("p (n two t) -> p n two t", two=2, t=1 << l)

        def load_chunk(sp, x, u, s, tok, tile):
            if tile is not None:
                hold(sp, x + "on", tile + 1)
                hold(sp, x + "state", tile * H + 1)
            for dst, n in ((Kc, 0), (R, 1), (Vc, 2)):
                sp.dma_start(heads(dst[:, s, :]), kfv_scratch[n, :, :, tok]).then_inc(sem(f"{x}in{s}"), 16)

        def chunk_in(eng, x, u, s):
            eng.wait_ge(sem(f"{x}in{s}"), u * 48 + 48)

        def chunk_act(act, x, u, s, levels, at_level):
            c = u * 2 + s
            r = R[:, s, :]
            chunk_in(act, x, u, s)
            for l in range(levels):
                if l == 0:
                    act.wait_ge(sem(x + "L0"), c + 1)
                else:
                    act.wait_ge(sem(x + "upd"), c * (2 * levels) + 2 * l)
                if l >= 2:
                    act.wait_ge(sem(x + "prod"), c * (2 * levels) + 2 * (l - 1))
                act.activation(Er[:, l % 2, :].rearrange("p (n t) -> p n t", t=1 << l),
                               blocks(r, l)[:, :, 1, :], ACT.Exp).then_inc(sem(x + "ex"), 1)
                act.activation(El[:, l % 2, :].rearrange("p (n t) -> p n t", t=1 << l),
                               blocks(L[:, :], l)[:, :, 0, :], ACT.Exp).then_inc(sem(x + "ex"), 1)
                if l == 1:
                    act.wait_ge(sem(x + "vT"), c + 1)
                    act.activation(vt[:, :], pt[:, :], ACT.Copy).then_inc(sem(x + "vt"), 1)
                at_level(l)
            act.wait_ge(sem(x + "upd"), c * (2 * levels) + 2 * levels)
            act.activation(L[:, :], L[:, :], ACT.Exp).then_inc(sem(x + "exf"), 1)
            act.activation(r, r, ACT.Exp).then_inc(sem(x + "exf"), 1)
            act.wait_ge(sem(x + "kdT"), c + 1)
            act.activation(kdt[:, :], pt[:, :], ACT.Copy).then_inc(sem(x + "kdt"), 1)
            act.wait_ge(sem(x + "o"), c + 1)
            act.activation(Qb[:, :], po[:, :], ACT.Square).then_inc(sem(x + "sq"), 1)
            act.wait_ge(sem(x + "ms"), c + 1)
            act.activation(Kd[:, :], px[:, :], ACT.Ln, scale=1.0 / P, bias=eps[:, :]).then_inc(sem(x + "lnms"), 1)
            act.wait_ge(sem(x + "lnms"), c + 2)
            act.activation(Kd[:, :], Kd[:, :], ACT.Exp, scale=-0.5).then_inc(sem(x + "rs"), 1)

        def chunk_dve(dve, x, u, s, tok, levels, state_update, at_level):
            c = u * 2 + s
            L2, T1 = 2 * levels, levels + 1
            R_, K_, Q_ = R[:, s, :], Kc[:, s, :], Q[:, :, tok]
            dve.wait_ge(sem(x + "fin"), c * 2 + 1)
            dve.memset(L[:, :], 0.0).then_inc(sem(x + "L0"), 1)
            dve.wait_ge(sem(x + "L0"), c + 1)
            chunk_in(dve, x, u, s)

            def take_diagonal():
                dve.wait_ge(sem(x + "diag"), c + 1)
                dve.wait_ge(sem(x + "taken"), c * T1 + 1)
                dve.sem_inc(sem("dve_passed"), 1)
                dve.copy_predicated(heads(A[:, :]), ident[:, :].bitcast(U32).unsqueeze(1).to_broadcast([P, H, P]),
                                    heads(px[:, :])).then_inc(sem(x + "taken"), 1)

            def take(l):
                dve.wait_ge(sem(x + "lev"), c * levels + (l + 1))
                dve.wait_ge(sem(x + "taken"), c * T1 + (l + 2))
                dve.sem_inc(sem("dve_passed"), 1)
                nb, hh = P >> (l + 1), 1 << l
                out = blocks(A[:, :], l)[:, :, 1, :].rearrange("p (h n) t -> p h n t", h=H)
                mask = masks[:, l, :].bitcast(U32).rearrange("p (n t) -> p n t", t=hh) \
                    .unsqueeze(1).to_broadcast([P, H, nb, hh])
                dve.copy_predicated(out, mask, pl[:, l % 2, :].rearrange("p (h n t) -> p h n t", h=H, t=hh)) \
                    .then_inc(sem(x + "taken"), 1)

            for l in range(levels):
                r, k, lo = blocks(R_, l), blocks(K_, l), blocks(L[:, :], l)
                q = Q_.rearrange("p h (n two t) -> p h n two t", two=2, t=1 << l)
                n, hh = HW >> (l + 1), 1 << l
                half = lambda ap: ap.rearrange("p (n t) -> p n t", t=hh)
                quad = lambda ap: ap.rearrange("p (h n t) -> p h n t", h=H, t=hh)
                dve.wait_ge(sem(x + "ex"), c * L2 + 2 * l + 2)
                dve.tensor_tensor(lo[:, :, 0, :], lo[:, :, 0, :], r[:, :, 1, hh - 1:hh].to_broadcast([P, n, hh]),
                                  ALU.add).then_inc(sem(x + "upd"), 1)
                dve.wait_ge(sem(x + "upd"), c * L2 + 2 * l + 1)
                dve.tensor_tensor(r[:, :, 1, :], r[:, :, 1, :], r[:, :, 0, hh - 1:hh].to_broadcast([P, n, hh]),
                                  ALU.add).then_inc(sem(x + "upd"), 1)
                if l >= 2:
                    dve.wait_ge(sem(x + "lev"), c * levels + (l - 1))
                dve.tensor_tensor(quad(Ql[:, l % 2, :]), quad(Er[:, l % 2, :]), q[:, :, :, 1, :], ALU.mult) \
                    .then_inc(sem(x + "prod"), 1)
                dve.tensor_tensor(blocks(Kl[:, l % 2, :], l)[:, :, 0, :], half(El[:, l % 2, :]), k[:, :, 0, :],
                                  ALU.mult).then_inc(sem(x + "prod"), 1)
                dve.wait_ge(sem(x + "upd"), c * L2 + 2 * l + 2)
                if l == 0:
                    take_diagonal()
                else:
                    take(l - 1)
                at_level(l)
            dve.wait_ge(sem(x + "exf"), c * 2 + 1)
            dve.tensor_tensor(Kd[:, :], L[:, :], K_, ALU.mult).then_inc(sem(x + "fin"), 1)
            dve.wait_ge(sem(x + "exf"), c * 2 + 2)
            dve.tensor_tensor(heads(Qb[:, :]), heads(R_), Q_, ALU.mult).then_inc(sem(x + "fin"), 1)
            take(levels - 1)
            state_update()
            dve.wait_ge(sem(x + "rs"), c + 1)
            dve.scalar_tensor_tensor(Q_, heads(po[:, :]), a_norm, heads(Kd[:, :]), ALU.mult, ALU.mult) \
                .then_inc(sem(x + "on"), 1)

        def chunk_step(pe, x, u, s, tok, levels, step, inter, state_product):
            c = u * 2 + s
            T1 = levels + 1
            if step == "in":
                chunk_in(pe, x, u, s)
                pe.wait_ge(sem(x + "kdt"), c + 1)
                for hd in range(H):
                    last = pe.transpose(head(pt, hd), head(Vc[:, s, :], hd), ident[:, :])
                last.then_inc(sem(x + "vT"), 1)
                pe.wait_ge(sem(x + "lnms"), c + 1)
                for hd in range(H):
                    last = pe.matmul(head(px, hd), head(Kc[:, s, :], hd), Q[:, hd, tok], start=True, stop=True)
                last.then_inc(sem(x + "diag"), 1)
            elif step == "kd":
                pe.wait_ge(sem(x + "fin"), c * 2 + 2)
                pe.wait_ge(sem(x + "vt"), c + 1)
                for hd in range(H):
                    last = pe.transpose(head(pt, hd), head(Kd, hd), ident[:, :])
                last.then_inc(sem(x + "kdT"), 1)
            elif step == "o":
                pe.wait_ge(sem(x + "fin"), c * 2 + 3)
                pe.wait_ge(sem(x + "taken"), c * T1 + (T1 + 1))
                pe.wait_ge(sem(x + "state"), c * H + 1)
                pe.wait_ge(sem(x + "on"), c + 1)
                for hd in range(H):
                    pe.matmul(head(po, hd), head(vt, hd), head(A, hd), start=True, stop=x == "s_")
                    last = inter(hd)
                last.then_inc(sem(x + "o"), 1)
            elif step == "state":
                pe.wait_ge(sem(x + "kdt"), c + 2)
                state_product(c)
            elif step == "ms":
                pe.wait_ge(sem(x + "sq"), c + 1)
                pe.wait_ge(sem(x + "state"), c * H + (H + 1))
                pe.matmul(px[:, :], ones[:, :], Qb[:, :], start=True, stop=True).then_inc(sem(x + "ms"), 1)
            else:
                l = step
                pe.wait_ge(sem(x + "prod"), c * (2 * levels) + 2 * l + 2)
                if l >= 1:
                    pe.wait_ge(sem(x + "taken"), c * T1 + (l + 2))
                for hd in range(H):
                    last = pe.matmul(pl[:, l % 2, hd * P // 2:(hd + 1) * P // 2], head(Kl[:, l % 2, :], hd),
                                     Ql[:, l % 2, hd * P // 2:(hd + 1) * P // 2], start=True, stop=True)
                last.then_inc(sem(x + "lev"), 1)

        new_semaphores()
        nothing = lambda l: None
        sctx = ExitStack()
        with sctx:
            S0 = [M[:, b // 2, b % 2 * HW:(b % 2 + 1) * HW] for b in range(NB)]
            kdm = sb(sctx, "kd_of_stream", [P, HW])
            in_stream = sb(sctx, "in_stream", [P, NB])
            pst = [pt, px]
            with nc.Block() as block:
                @block.sync
                def _(sp):
                    start_at_one(sp, ["s_" + n for n in CHUNK_STARTS])
                    load_chunk(sp, "s_", 0, 0, slice(NP_, T), None)
                    for b in range(NB):
                        sp.dma_start(heads(S0[b]), io["state_hgrn"][0, b].rearrange("h k v -> k h v")) \
                            .then_inc(sem("s_S0"), 16)
                    for b in range(NB):
                        sp.wait_ge(sem("s_new"), b + 1)
                        sp.dma_start(io["hgrn_sample"][0, b].rearrange("h k v -> k h v"), heads(S0[b])) \
                            .then_inc(sem("s_state_out"), 16)
                    sp.wait_ge(sem("s_state_out"), 16 * NB)

                @block.gpsimd
                def _(pool):
                    for ap in (masks[:, :, :], in_stream[:, :]):
                        pool.memset(ap, 1.0).then_inc(sem("mask"), 1)
                    for ap in (Kl[:, :, :], A[:, :], S[:, :]):
                        pool.memset(ap, 0.0).then_inc(sem("mask"), 1)
                    pool.wait_ge(sem("mask"), 5)

                    def keep(ap, base, pattern, channel):
                        pool.affine_select(out=ap, in_=ap, compare_op=ALU.is_ge, fill=0.0, base=base, pattern=pattern,
                                           channel_multiplier=channel).then_inc(sem("mask"), 1)

                    for l in range(LEVELS):
                        nb, hh = P >> (l + 1), 1 << l
                        keep(masks[:, l, :].rearrange("p (n t) -> p n t", t=hh), 0, [[-2 * hh, nb], [0, hh]], 1)
                    keep(in_stream[:, :], 0, [[-LS, NB]], 1)
                    pool.wait_ge(sem("mask"), 5 + LEVELS + 1)
                    for l in range(LEVELS):
                        nb, hh = P >> (l + 1), 1 << l
                        keep(masks[:, l, :].rearrange("p (n t) -> p n t", t=hh), hh - 1, [[2 * hh, nb], [0, hh]], -1)
                    keep(in_stream[:, :], LS - 1, [[LS, NB]], -1)
                    pool.wait_ge(sem("mask"), 5 + 2 * (LEVELS + 1))
                    pool.sem_inc(sem("masks_ready"), 1)

                @block.scalar
                def _(act):
                    act.preload_act_table_set("natural_log_exp_and_others")
                    chunk_act(act, "s_", 0, 0, SLEVELS, nothing)

                @block.vector
                def _(dve):
                    def states():
                        dve.wait_ge(sem("s_kdt"), 2)
                        dve.wait_ge(sem("s_S0"), 16 * NB)
                        dve.wait_ge(sem("s_o"), 1)
                        ends = R[:, 0, :].rearrange("p (h b t) -> p b h t", h=H, t=LS)[:, :, :, LS - 1:LS]
                        for b in range(NB):
                            if b:
                                dve.wait_ge(sem("s_mm"), b)
                            dve.tensor_scalar(kdm[:, :], kdt[:, :], in_stream[:, b:b + 1], None, ALU.mult) \
                                .then_inc(sem("s_kdm"), 1)
                            s0 = heads(S0[b])
                            dve.tensor_tensor(s0, s0, ends[:, b].to_broadcast([P, H, P]), ALU.mult) \
                                .then_inc(sem("s_dec"), 1)
                            dve.wait_ge(sem("s_dec"), b + 1)
                            dve.wait_ge(sem("s_mm"), b + 1)
                            dve.tensor_tensor(S0[b], S0[b], pst[b % 2][:, :], ALU.add) \
                                .then_inc(sem("s_new"), 1)
                        dve.wait_ge(sem("s_new"), NB)
                        dve.sem_inc(sem("s_state"), H)

                    dve.wait_ge(sem("masks_ready"), 1)
                    chunk_dve(dve, "s_", 0, 0, slice(NP_, T), SLEVELS, states, nothing)

                @block.tensor
                def _(pe):
                    def inter(hd):
                        for b in range(NB):
                            at = slice(hd * P + b * LS, hd * P + (b + 1) * LS)
                            last = pe.matmul(po[:, at], head(S0[b], hd), Qb[:, at], start=False,
                                             stop=(b == NB - 1), skip_group_check=True)
                        return last

                    def state_product(c):
                        for b in range(NB):
                            pe.wait_ge(sem("s_kdm"), b + 1)
                            if b >= 2:
                                pe.wait_ge(sem("s_new"), b - 1)
                            for hd in range(H):
                                last = pe.matmul(head(pst[b % 2], hd), head(kdm, hd), head(vt, hd), start=True, stop=True)
                            last.then_inc(sem("s_mm"), 1)

                    pe.wait_ge(sem("s_S0"), 16 * NB)
                    for step in ("in", *range(SLEVELS), "kd", "o", "state", "ms"):
                        chunk_step(pe, "s_", 0, 0, slice(NP_, T), SLEVELS, step, inter, state_product)

        TM, SG = M[:, 0:KB, :], M[:, KB:KB + H, :]
        ctx = ExitStack()
        with ctx:
            ring = pb(ctx, "p_ring", [P, 4, 512])
            U = sb(ctx, "conv_in", [P, 2 + NP_])
            Us = sb(ctx, "conv_in_samples", [P, NB, 2 + LS])
            y = sb(ctx, "conv_out", [P, T])
            taps = sb(ctx, "conv_taps", [P, 3])
            FIRST_COL = (4 * AW + BW, 4 * AW + 2 * BW, 4 * AW, 3 * AW)
            cw = cols[:, o_cw:o_cw + 3 * KB].rearrange("p (w j) -> p w j", j=KB)
            cst = cols[:, o_cst:o_cst + n_cst].rearrange("p (b w j) -> p b w j", w=2, j=KB)
            n_s = 2 * NB * KB
            ncs = new_conv[:, 0:n_s].rearrange("p (b w j) -> p b w j", w=2, j=KB)
            ncp = new_conv[:, n_s:].rearrange("p (w j) -> p w j", j=KB)
            U0 = N_QFI // 2
            TURNS = KB
            assert NPT == 2 * TURNS

            def bank_free(j, m):
                return f"ring{m % 4}", j * 3 + (m // 4 + 1)

            with nc.Block() as block:
                @block.sync
                def _(sp):
                    start_at_one(sp, ["p_" + n for n in CHUNK_STARTS] + ["b_done"] + [f"ring{b}" for b in range(4)])
                    load_chunk(sp, "p_", 0, 0, slice(0, P), None)

                    def tile(j, n):
                        ws.load(sp, j * 2 + (U0 + n // 2), n % 2, w_in[:, bass.ds(j * P + FIRST_COL[n], P)])

                    with sp.Fori(0, TURNS - 1, 1) as j:
                        load_chunk(sp, "p_", j, 1, bass.ds(j * (2 * P) + P, P), j * 2)
                        tile(j, 2)
                        tile(j, 3)
                        load_chunk(sp, "p_", j + 1, 0, bass.ds(j * (2 * P) + 2 * P, P), j * 2 + 1)
                        tile(j + 1, 0)
                        tile(j + 1, 1)
                    load_chunk(sp, "p_", TURNS - 1, 1, slice((NPT - 1) * P, NP_), NPT - 2)
                    tile(TURNS - 1, 2)
                    tile(TURNS - 1, 3)
                    ws.load(sp, U0 + 2 * TURNS, 0, w_bgate[:, D:D + P])
                    ws.load(sp, U0 + 2 * TURNS, 1, io["w_pb"][0][:, 0:P])
                    sp.wait_ge(sem("p_state"), H * NPT + 1)
                    sp.dma_start(io["hgrn_prompt"][0, 0].rearrange("h k v -> k h v"), heads(S[:, :])) \
                        .then_inc(sem("p_state_out"), 16)
                    sp.wait_ge(sem("p_state_out"), 16)

                @block.gpsimd
                def _(pool):
                    with pool.Fori(0, TURNS, 1) as j:
                        for n in (2, 3, 4, 5):
                            ws.split(pool, j * 2 + (U0 + n // 2), n % 2, KD)

                @block.scalar
                def _(act):
                    act.preload_act_table_set("natural_log_exp_and_others")

                    def copy_out(j, n, dst):
                        for g in range(NG):
                            ws.arrived(act, j * 2 + (U0 + n // 2), n % 2, g)
                            act.activation(dst(g), ring[:, (3 * n + g) % 4, 0:G], ACT.Copy) \
                                .then_inc(sem(f"ring{(3 * n + g) % 4}"), 1)

                    with act.Fori(0, TURNS, 1) as j:
                        def c_out(l):
                            if l == LEVELS - 2:
                                act.wait_ge(sem("b_done"), j * 3 + 1)
                                copy_out(j, 0, lambda g: y[:, g * G:(g + 1) * G])
                                act.wait_ge(sem("ring2"), j * 3 + 2)
                                act.sem_inc(sem("c_done"), 1)

                        chunk_act(act, "p_", j, 0, LEVELS, c_out)
                        chunk_act(act, "p_", j, 1, LEVELS, nothing)
                        copy_out(j, 3, lambda g: SG[:, bass.ds(j, 1), g * G:(g + 1) * G].rearrange("p a t -> p (a t)"))

                @block.vector
                def _(dve):
                    dve.memset(U[:, 0:2], 0.0).then_inc(sem("u_zero"), 1)
                    dve.wait_ge(sem("u_zero"), 1)

                    with dve.Fori(0, TURNS, 1) as j:
                        one = bass.ds(j, 1)
                        link = Link(dve, sem("conv_step"), j * 11)

                        def state(c, s):
                            def update():
                                dve.wait_ge(sem("p_st"), c + 1)
                                for hd in range(H):
                                    dve.scalar_tensor_tensor(head(S, hd), head(S, hd), R[:, s, (hd + 1) * P - 1:(hd + 1) * P],
                                                             head(px, hd), ALU.mult, ALU.add).then_inc(sem("p_state"), 1)
                            return update

                        def conv_in():
                            link(dve.tensor_scalar(Us[:, :, 0:2].unsqueeze(3), cst[:, :, :, one], 1.0, None, ALU.mult))
                            link(dve.tensor_scalar(taps[:, :].unsqueeze(2), cw[:, :, one], 1.0, None, ALU.mult))
                            dve.wait_ge(sem("c_done"), j + 1)
                            for g in range(NG):
                                bank = (3 + g) % 4
                                ws.arrived(dve, j * 2 + U0, 1, g)
                                if g < 2:
                                    dve.tensor_tensor(U[:, 2 + g * G:2 + (g + 1) * G], ring[:, bank, 0:G], y[:, g * G:(g + 1) * G],
                                                      ALU.mult).then_inc(sem(f"ring{bank}"), 1)
                                else:
                                    link(dve.tensor_tensor(U[:, 2 + 2 * G:], ring[:, bank, 0:REST], y[:, 2 * G:NP_], ALU.mult))
                                    dve.tensor_tensor(Us[:, :, 2:], ring[:, bank, REST:G].rearrange("p (b t) -> p b t", t=LS),
                                                      y[:, NP_:].rearrange("p (b t) -> p b t", t=LS), ALU.mult) \
                                        .then_inc(sem(f"ring{bank}"), 1)
                                    dve.wait_ge(sem(f"ring{bank}"), j * 3 + 3)
                            conv3(dve, link, U, Us, y, [taps[:, w:w + 1] for w in range(3)])
                            link(dve.tensor_scalar(ncs[:, :, :, one], Us[:, :, LS:].unsqueeze(3), 1.0, None, ALU.mult))
                            link(dve.tensor_scalar(ncp[:, :, one], U[:, NP_:].unsqueeze(2), 1.0, None, ALU.mult))

                        def b_out(l):
                            if l == LEVELS - 2:
                                for g in range(NG):
                                    bank = (6 + g) % 4
                                    ws.arrived(dve, j * 2 + (U0 + 1), 0, g)
                                    dve.tensor_tensor(TM[:, one, g * G:(g + 1) * G].rearrange("p a t -> p (a t)"),
                                                      ring[:, bank, 0:G], y[:, g * G:(g + 1) * G], ALU.mult) \
                                        .then_inc(sem("b_done"), 1)
                                    dve.wait_ge(sem("b_done"), j * 3 + (g + 2))
                                    dve.sem_inc(sem(f"ring{bank}"), 1)

                        chunk_dve(dve, "p_", j, 0, bass.ds(j * (2 * P), P), LEVELS, state(j * 2, 0), nothing)
                        conv_in()
                        chunk_dve(dve, "p_", j, 1, bass.ds(j * (2 * P) + P, P), LEVELS, state(j * 2 + 1, 1), b_out)

                @block.tensor
                def _(pe):
                    STEP_AT = {0: "in", 2: 0, 3: 1, 5: 2, 6: 3, 8: 4, 9: 5, 11: 6, 12: "kd", 13: "o", 14: "state", 16: "ms"}

                    def inter(hd):
                        return pe.matmul(head(po, hd), head(S, hd), head(Qb, hd), start=False, stop=True)

                    def state_product(c):
                        for hd in range(H):
                            last = pe.matmul(head(px, hd), head(kdt, hd), head(vt, hd), start=True, stop=True)
                        last.then_inc(sem("p_st"), 1)

                    with pe.Fori(0, TURNS, 1) as j:
                        for n in range(4):
                            tok = bass.ds(j * (2 * P) + n // 2 * P, P)

                            def between(run):
                                step = STEP_AT.get(n % 2 * 9 + run)
                                if step is not None:
                                    chunk_step(pe, "p_", j, n // 2, tok, LEVELS, step, inter, state_product)

                            ws.product(pe, j * 2 + (U0 + n // 2), n % 2, KD, h,
                                       lambda g: (ring[:, (3 * n + g) % 4, :], *bank_free(j, 3 * n + g)), between)
        rec.close()

        new_semaphores()
        ctx = ExitStack()
        with ctx:
            branch = sb(ctx, "branch", [P, 2, H, T], F32R)
            ps = [pb(ctx, f"p_mix{s}", [P, NG, 512]) for s in range(2)]
            sg = sb(ctx, "gate_sigmoid", [P, T])
            gated = sb(ctx, "gated", [P, T])
            U0 = (N_QFI + 4 * KB) // 2
            HALVES = ((D, io["w_pb"][0], U0), (0, io["w_pa"][0], U0 + KD))

            with nc.Block() as block:
                @block.sync
                def _(sp):
                    start_at_one(sp, ["mix_pfree0", "mix_pfree1", "mix_z"])
                    for n, (col, w_proj, u0) in enumerate(HALVES):
                        with sp.Fori(1, KD, 1) as j:
                            ws.load(sp, j + u0, 0, w_bgate[:, bass.ds(j * P + col, P)])
                            ws.load(sp, j + u0, 1, w_proj[:, bass.ds(j * P, P)])
                        if n == 0:
                            ws.load(sp, HALVES[1][2], 0, w_bgate[:, 0:P])
                            ws.load(sp, HALVES[1][2], 1, HALVES[1][1][:, 0:P])

                @block.gpsimd
                def _(pool):
                    with pool.Fori(1, 2 * KD, 1) as j:
                        ws.split(pool, j + U0, 0, KD)
                        ws.split(pool, j + U0, 1, H)

                @block.tensor
                def _(pe):
                    for n, (_, _, u0) in enumerate(HALVES):
                        def turn(j):
                            local = j + n * KD
                            ws.product(pe, j + u0, 0, KD, h, two_slots(ps, "mix", local, 0))
                            if isinstance(j, int):
                                pe.wait_ge(sem("branch_lo"), (n + 1) * H)
                            ws.product(pe, j + u0, 1, H, branch, two_slots(ps, "mix", local, 1))
                        turn(0)
                        with pe.Fori(1, KD, 1) as j:
                            turn(j)

                @block.scalar
                def _(act):
                    for k in range(H):
                        act.activation(branch[:, 0, k, :], TM[:, k, :], ACT.Copy).then_inc(sem("branch_hi"), 1)
                    act.activation(SG, SG, ACT.Silu).then_inc(sem("silu_g"), 1)
                    for n, (_, _, u0) in enumerate(HALVES):
                        if n == 1:
                            ws.arrived(act, u0 - 1, 1)
                            for k in range(H):
                                act.activation(branch[:, 0, k, :], Q[:, k, :], ACT.Copy).then_inc(sem("branch_hi"), 1)
                        with act.Fori(0, KD, 1) as j:
                            ws.arrived(act, j + u0, 0)
                            act.wait_ge(sem("mix_pfree1"), j + (n * KD + 1))
                            act.activation(by_group(sg[:, :]), groups(ps[0]), ACT.Sigmoid).then_inc(sem("mix_pfree0"), 1)

                @block.vector
                def _(dve):
                    for k in range(H):
                        dve.wait_ge(sem("branch_hi"), k + 1)
                        dve.tensor_tensor(branch[:, 1, k, :], TM[:, k, :], f32(branch[:, 0, k, :]), ALU.subtract) \
                            .then_inc(sem("branch_lo"), 1)
                    dve.wait_ge(sem("silu_g"), 1)
                    dve.tensor_tensor(Q[:, :, :], Q[:, :, :], SG, ALU.mult).then_inc(sem("readout_gated"), 1)
                    dve.wait_ge(sem("branch_lo"), H)
                    dve.wait_ge(sem("readout_gated"), 1)
                    for n, (_, _, u0) in enumerate(HALVES):
                        if n == 1:
                            for k in range(H):
                                dve.wait_ge(sem("branch_hi"), H + k + 1)
                                dve.tensor_tensor(branch[:, 1, k, :], Q[:, k, :], f32(branch[:, 0, k, :]), ALU.subtract) \
                                    .then_inc(sem("branch_lo"), 1)
                        with dve.Fori(0, KD, 1) as j:
                            z = M[:, bass.ds(j, 1), :]
                            ws.arrived(dve, j + u0, 1)
                            dve.wait_ge(sem("mix_pfree0"), j + (n * KD + 2))
                            if n == 0:
                                dve.tensor_tensor(z.rearrange("p a (g t) -> p (a g) t", t=G), by_group(sg[:, :]),
                                                  groups(ps[1]), ALU.mult).then_inc(sem("mix_pfree1"), 1)
                            else:
                                dve.wait_ge(sem("mix_z"), j + 1)
                                dve.tensor_tensor(by_group(gated[:, :]), by_group(sg[:, :]), groups(ps[1]), ALU.mult) \
                                    .then_inc(sem("mix_pfree1"), 1)
                                dve.wait_ge(sem("mix_pfree1"), j + (KD + 2))
                                dve.tensor_tensor(z, z, gated[:, :].unsqueeze(1), ALU.add).then_inc(sem("mix_z"), 1)
        mixer.close()

        def token_rows(name_p, name_s):
            prompt = io[name_p][0]
            return (lambda t: prompt[bass.ds(t * P, P), :]), io[name_s].rearrange("b l d -> (b l) d")

        def load_gate(sp, dst, n, sample, sem_name):
            if sample:
                for b in range(NB):
                    sp.dma_start(dst[b * LS:(b + 1) * LS, :], gate_scratch[n, b + 1:b + 2, :].to_broadcast([LS, D])) \
                        .then_inc(sem(sem_name), 16)
            else:
                sp.dma_start(dst[:, :], gate_scratch[n, 0:1, :].to_broadcast([P, D])).then_inc(sem(sem_name), 16)

        x_rows, x_sample_rows = token_rows("x_prompt", "x_sample")
        ctx = ExitStack()
        with ctx:
            wo = sb(ctx, "w_o_halves", [P, 2, KD, D], F32R)
            X = sb(ctx, "x_tile_mid", [P, 2, D])
            zh = sb(ctx, "z_tile", [P, 2, KD, P], F32R)
            xn = sb(ctx, "x1_normed", [P, 1, D])
            gate = sb(ctx, "gate_mix", [P, D])
            full = sb(ctx, "h_mid", [P, 1, D])
            stat = sb(ctx, "stat_mid", [P, 8])
            pm = pb(ctx, "p_m", [P, 2, 2, 512])
            pT = pb(ctx, "p_x1T", [P, 2, 2, 512])
            w_o = io["w_o"][0]

            with nc.Block() as block:
                @block.sync
                def _(sp):
                    give_slots(sp, ["mid_xT", "mid_pT", "mid_lo", "m_used"])
                    start_at_one(sp, ["mid_xn", "x1_out0", "x1_out1"])
                    load_gate(sp, gate, 0, False, "gate_mix_in")
                    for k in range(KD):
                        if k >= 2:
                            sp.wait_ge(sem("wo_lo"), k - 1)
                        sp.dma_start(X[:, k % 2, :], w_o[k * P:(k + 1) * P, :]).then_inc(sem(f"wo_in{k % 2}"), 16)
                    sp.wait_ge(sem("wo_lo"), KD)

                    def load_x(u, s, src, normed):
                        if normed is not None:
                            hold(sp, "mid_xn", normed + 1)
                        hold(sp, f"x1_out{s}", u * 16 + 1)
                        sp.dma_start(X[:, s, :], src).then_inc(sem(f"x_mid_in{s}"), 16)

                    def store(u, s, dst):
                        hold(sp, "x1", u * 2 + s + 1)
                        sp.dma_start(dst, X[:, s, :]).then_inc(sem(f"x1_out{s}"), 16)

                    load_x(0, 0, x_rows(0), None)
                    with sp.Fori(0, NPT // 2 - 1, 1) as i:
                        for s in range(2):
                            load_x(i + s, 1 - s, x_rows(i * 2 + s + 1), i * 2 + s)
                            store(i, s, x1_scratch[bass.ds((i * 2 + s) * P, P), :])
                    i = NPT // 2 - 1
                    load_x(i, 1, x_rows(NPT - 1), NPT - 2)
                    store(i, 0, x1_scratch[(NPT - 2) * P:(NPT - 1) * P, :])
                    load_x(NPT // 2, 0, x_sample_rows, NPT - 1)
                    store(i, 1, x1_scratch[(NPT - 1) * P:NPT * P, :])
                    sp.wait_ge(sem("x1"), NPT)
                    load_gate(sp, gate, 0, True, "gate_mix_s_in")
                    store(NPT // 2, 0, x1_scratch[NPT * P:, :])
                    sp.wait_ge(sem("x1_out0"), 16 * (NPT // 2 + 1) + 1)
                    sp.wait_ge(sem("x1_out1"), 16 * (NPT // 2) + 1)

                @block.gpsimd
                def _(pool):
                    pairs(pool, NPT, lambda u, s: halves_of_h(pool, "mid", u, s, full))
                    halves_of_h(pool, "mid", NPT // 2, 0, full)

                @block.scalar
                def _(act):
                    act.preload_act_table_set("natural_log_exp_and_others")
                    for k in range(KD):
                        act.wait_ge(sem(f"wo_in{k % 2}"), 16 * (k // 2 + 1))
                        act.activation(wo[:, 0, k, :], X[:, k % 2, :], ACT.Copy).then_inc(sem("wo_hi"), 1)

                    def z_hi(t):
                        if not isinstance(t, int):
                            act.wait_ge(sem("m_mm"), t)
                        act.activation(zh[:, 0, :, :], M[:, :, bass.ds(t * P, P)], ACT.Copy).then_inc(sem("z_hi"), 1)

                    def norms(u, s):
                        t = u * 2 + s
                        link = Link(act, sem("mid_norm"), t * 4)

                        def rstd(at):
                            link(act.activation(stat[:, at + 1:at + 2], stat[:, at:at + 1], ACT.Ln, scale=1.0 / D,
                                                bias=eps[:, :]))
                            act.activation(stat[:, at + 2:at + 3], stat[:, at + 1:at + 2], ACT.Exp, scale=-0.5) \
                                .then_inc(sem("mid_rstd"), 1)

                        act.wait_ge(sem("m_mm"), t + 1)
                        act.wait_ge(sem("mid_xT"), t + 2)
                        link(act.activation(xn[:, 0, :].rearrange("p (a n) -> p a n", a=2), pm[:, s], ACT.Square,
                                            accum_out=stat[:, 0:1]))
                        rstd(0)
                        act.wait_ge(sem("x1"), t + 1)
                        link(act.activation(xn[:, 0, :], X[:, s, :], ACT.Square, accum_out=stat[:, 4:5]))
                        rstd(4)
                        act.wait_ge(sem("mid_rstd"), t * 2 + 2)
                        act.activation(xn[:, 0, :], X[:, s, :], ACT.Copy, scale=stat[:, 6:7]).then_inc(sem("mid_xn"), 1)

                    z_hi(0)
                    with act.Fori(0, NPT // 2, 1) as i:
                        for s in range(2):
                            z_hi(i * 2 + s + 1)
                            norms(i, s)
                    norms(NPT // 2, 0)

                @block.vector
                def _(dve):
                    for k in range(KD):
                        dve.wait_ge(sem("wo_hi"), k + 1)
                        dve.tensor_tensor(wo[:, 1, k, :], X[:, k % 2, :], f32(wo[:, 0, k, :]), ALU.subtract) \
                            .then_inc(sem("wo_lo"), 1)

                    def z_lo(t):
                        dve.wait_ge(sem("z_hi"), t + 1)
                        dve.tensor_tensor(zh[:, 1, :, :], M[:, :, bass.ds(t * P, P)], f32(zh[:, 0, :, :]), ALU.subtract) \
                            .then_inc(sem("z_lo"), 1)

                    def residual(u, s, sample):
                        t = u * 2 + s
                        flat = lambda ap: ap.rearrange("p (a n) -> p a n", a=2)
                        dve.wait_ge(sem("mid_rstd"), t * 2 + 1)
                        dve.wait_ge(sem("mid_lo"), t + 2)
                        dve.wait_ge(sem("gate_mix_in"), 16)
                        if sample:
                            dve.wait_ge(sem("gate_mix_s_in"), 16 * NB)
                        dve.scalar_tensor_tensor(flat(full[:, 0, :]), pm[:, s], stat[:, 2:3], flat(gate[:, :]), ALU.mult,
                                                 ALU.mult).then_inc(sem("m_used"), 1)
                        dve.wait_ge(sem("m_used"), t + 3)
                        dve.wait_ge(sem(f"x_mid_in{s}"), u * 16 + 16)
                        dve.tensor_tensor(X[:, s, :], X[:, s, :], full[:, 0, :], ALU.add).then_inc(sem("x1"), 1)
                        dve.wait_ge(sem("x1"), t + 1)

                    z_lo(0)
                    with dve.Fori(0, NPT // 2, 1) as i:
                        for s in range(2):
                            z_lo(i * 2 + s + 1)
                            residual(i, s, False)
                            modulate(dve, "mid", i, s, pT, full, scale2, shift2)
                    residual(NPT // 2, 0, True)
                    modulate(dve, "mid", NPT // 2, 0, pT, full, scale2, shift2, sample=True)

                @block.tensor
                def _(pe):
                    def out_product(t, s):
                        pe.wait_ge(sem("z_lo"), t + 1)
                        pe.wait_ge(sem("m_used"), t + 1)
                        for half in range(2):
                            for j, (a, b) in enumerate(PASSES):
                                for k in range(KD):
                                    last = pe.matmul(pm[:, s, half, :], zh[:, a, k, :],
                                                     wo[:, b, k, half * HALF:(half + 1) * HALF],
                                                     start=(j == 0 and k == 0), stop=(j == 2 and k == KD - 1))
                        last.then_inc(sem("m_mm"), 1)

                    pe.wait_ge(sem("wo_lo"), KD)
                    out_product(0, 0)
                    with pe.Fori(0, NPT // 2, 1) as i:
                        for s in range(2):
                            out_product(i * 2 + s + 1, 1 - s)
                            transposes(pe, "mid", i, s, xn, pT)
                    transposes(pe, "mid", NPT // 2, 0, xn, pT)

        out_sum = M[:, :, :].rearrange("p k t -> p (k t)").rearrange("p (t a n) -> p t a n", a=2, n=HALF)
        ctx = ExitStack()
        with ctx:
            ps = [pb(ctx, f"p_up{s}", [P, NG, 512]) for s in range(2)]
            pdn = pb(ctx, "p_down", [P, 2, 512])
            ws = WeightStream(ctx, "wup")
            wd_raw = sb(ctx, "w_down_raw", [P, 2, D])
            wd = sb(ctx, "w_down_halves", [P, 2, 2, D], F32R)
            ff = sb(ctx, "mlp_hidden", [P, 2, 2, T], F32R)
            U = sb(ctx, "gate_in", [P, 2 + NP_])
            Us = sb(ctx, "gate_in_samples", [P, NB, 2 + LS])
            y = sb(ctx, "gate_conv", [P, T])
            fw = sb(ctx, "ffn_taps", [P, 3])
            TURNS, DOWNS = KF // 2, NT * 2
            w_gate, w_val, w_dn = w_up[:, 0:DFF], w_up[:, DFF:], io["w_down"][0]
            fcw = cols[:, o_fcw:o_fcw + 3 * KF].rearrange("p (w f) -> p w f", f=KF)
            fst = cols[:, o_fst:o_fst + n_fst].rearrange("p (b w f) -> p b w f", w=2, f=KF)
            nfs = new_ffn[:, 0:n_fst].rearrange("p (b w f) -> p b w f", w=2, f=KF)
            nfp = new_ffn[:, n_fst:].rearrange("p (w f) -> p w f", f=KF)

            with nc.Block() as block:
                @block.sync
                def _(sp):
                    ws.start(sp)
                    start_at_one(sp, ["wup_pfree0", "wup_pfree1"])
                    give_slots(sp, ["down_free"])
                    start_at_one(sp, ["wd_lo", "down_mm", "conv_read", "ff_lo"])
                    with sp.Fori(0, TURNS, 1) as g:
                        for f in range(2):
                            col = bass.ds((g * 2 + f) * P, P)
                            ws.load(sp, g * 2 + f, 0, w_gate[:, col])
                            ws.load(sp, g * 2 + f, 1, w_val[:, col])
                        hold(sp, "wd_lo", g + 1)
                        sp.dma_start(wd_raw[:, :, :], w_dn[bass.ds(g * (2 * P), 2 * P), :]
                                     .rearrange("(f p) n -> p f n", p=P)).then_inc(sem("wd_in"), 16)

                @block.gpsimd
                def _(pool):
                    pool.memset(out_sum[:, :, :, :], 0.0).then_inc(sem("sum_zero"), 1)
                    with pool.Fori(0, TURNS, 1) as g:
                        for n in range(4):
                            ws.split(pool, g * 2 + n // 2, n % 2, KD)
                        hi, lo = wd[:, 0, :, :], wd[:, 1, :, :]
                        pool.wait_ge(sem("wd_in"), g * 16 + 16)
                        pool.wait_ge(sem("down_mm"), g * DOWNS + 1)
                        pool.tensor_tensor(hi, wd_raw[:, :, :], ones[:, 0:1].unsqueeze(1).to_broadcast([P, 2, D]),
                                           ALU.mult).then_inc(sem("wd_hi"), 1)
                        pool.wait_ge(sem("wd_hi"), g + 1)
                        pool.tensor_tensor(lo, wd_raw[:, :, :], f32(hi), ALU.subtract).then_inc(sem("wd_lo"), 1)

                @block.tensor
                def _(pe):
                    def up(g, f):
                        for s in range(2):
                            ws.product(pe, g * 2 + f, s, KD, h, two_slots(ps, "wup", g * 2 + f, s))

                    def down(g):
                        pe.wait_ge(sem("ff_lo"), g * 2 + 3)
                        pe.wait_ge(sem("wd_lo"), g + 2)
                        for n in range(DOWNS):
                            t, half = n // 2, n % 2
                            pe.wait_ge(sem("down_free"), g * DOWNS + (n + 1))
                            for j, (a, b) in enumerate(PASSES):
                                for f in range(2):
                                    last = pe.matmul(pdn[:, half, :], ff[:, a, f, t * P:(t + 1) * P],
                                                     wd[:, b, f, half * HALF:(half + 1) * HALF],
                                                     start=(j == 0 and f == 0), stop=(j == 2 and f == 1))
                            last.then_inc(sem("down_mm"), 1)

                    up(0, 0)
                    up(0, 1)
                    with pe.Fori(1, TURNS, 1) as g:
                        up(g, 0)
                        down(g - 1)
                        up(g, 1)
                    down(TURNS - 1)

                @block.scalar
                def _(act):
                    def hidden(g, f):
                        n = g * 2 + f
                        gate = ps[0]
                        ws.arrived(act, n, 0)
                        act.wait_ge(sem("conv_read"), n + 1)
                        act.activation(U[:, 2:2 + 2 * G].rearrange("p (g t) -> p g t", t=G), gate[:, 0:2, 0:G], ACT.Copy) \
                            .then_inc(sem("gate_rows"), 1)
                        act.activation(U[:, 2 + 2 * G:], gate[:, 2, 0:REST], ACT.Copy).then_inc(sem("gate_rows"), 1)
                        act.activation(Us[:, :, 2:], gate[:, 2, REST:G].rearrange("p (b t) -> p b t", t=LS), ACT.Copy) \
                            .then_inc(sem("wup_pfree0"), 1)
                        act.wait_ge(sem("conv_read"), n + 2)
                        act.activation(y[:, :], y[:, :], ACT.Silu).then_inc(sem("gate_silu"), 1)
                        act.wait_ge(sem("ff_full"), n + 1)
                        act.wait_ge(sem("down_mm"), g * DOWNS + 1)
                        act.activation(ff[:, 0, f, :], y[:, :], ACT.Copy).then_inc(sem("ff_hi"), 1)

                    with act.Fori(0, TURNS, 1) as g:
                        hidden(g, 0)
                        hidden(g, 1)

                @block.vector
                def _(dve):
                    STEPS = 7

                    def hidden(g, f):
                        n = g * 2 + f
                        one = bass.ds(n, 1)
                        link = Link(dve, sem("mlp_step"), n * STEPS)
                        dve.tensor_scalar(Us[:, :, 0:2].unsqueeze(3), fst[:, :, :, one], 1.0, None, ALU.mult) \
                            .then_inc(sem("history"), 1)
                        link(dve.tensor_scalar(fw[:, :].unsqueeze(2), fcw[:, :, one], 1.0, None, ALU.mult))
                        dve.wait_ge(sem("history"), n + 1)
                        dve.wait_ge(sem("wup_pfree0"), n + 2)
                        dve.wait_ge(sem("ff_lo"), n + 1)
                        conv3(dve, link, U, Us, y, [fw[:, w:w + 1] for w in range(3)])
                        dve.tensor_scalar(nfs[:, :, :, one], Us[:, :, LS:].unsqueeze(3), 1.0, None, ALU.mult) \
                            .then_inc(sem("new_history"), 1)
                        dve.tensor_scalar(nfp[:, :, one], U[:, NP_:].unsqueeze(2), 1.0, None, ALU.mult) \
                            .then_inc(sem("conv_read"), 1)
                        ws.arrived(dve, n, 1)
                        dve.wait_ge(sem("gate_silu"), n + 1)
                        dve.tensor_tensor(by_group(y[:, :]), by_group(y[:, :]), groups(ps[1]), ALU.mult) \
                            .then_inc(sem("ff_full"), 1)
                        dve.wait_ge(sem("ff_full"), n + 1)
                        dve.sem_inc(sem("wup_pfree1"), 1)

                    def low(g, f):
                        dve.wait_ge(sem("ff_hi"), g * 2 + f + 1)
                        dve.tensor_tensor(ff[:, 1, f, :], y[:, :], f32(ff[:, 0, f, :]), ALU.subtract).then_inc(sem("ff_lo"), 1)

                    def add_down(g):
                        for n in range(DOWNS):
                            part = out_sum[:, n // 2, n % 2, :]
                            dve.wait_ge(sem("down_mm"), g * DOWNS + (n + 2))
                            dve.wait_ge(sem("down_free"), g * DOWNS + 2)
                            dve.tensor_tensor(part, part, pdn[:, n % 2, :], ALU.add).then_inc(sem("down_free"), 1)

                    dve.memset(U[:, 0:2], 0.0).then_inc(sem("u_zero"), 1)
                    dve.wait_ge(sem("u_zero"), 1)
                    dve.wait_ge(sem("sum_zero"), 1)
                    hidden(0, 0)
                    low(0, 0)
                    hidden(0, 1)
                    low(0, 1)
                    with dve.Fori(1, TURNS, 1) as g:
                        hidden(g, 0)
                        add_down(g - 1)
                        low(g, 0)
                        hidden(g, 1)
                        low(g, 1)
                    add_down(TURNS - 1)

        new_semaphores()
        y_rows, y_sample_rows = token_rows("y_prompt", "y_sample")
        ctx = ExitStack()
        with ctx:
            X = sb(ctx, "x1_tile", [P, 2, D])
            gate = sb(ctx, "gate_mlp", [P, 2, D])
            scratch = sb(ctx, "squares_out", [P, 2, D])
            stat = sb(ctx, "stat_out", [P, 2, 4])
            rows = sb(ctx, "history_rows", [P, 6, P])
            prow = pb(ctx, "p_history", [P, 2, 512])
            n_s = 2 * NB * KB
            ffn_s = io["ffn_sample"].rearrange("a b w (k p) -> (a b w k) p", p=P)
            HISTORY = [(new_ffn[:, 0:P], ffn_s[0:P, :]), (new_ffn[:, P:2 * P], ffn_s[P:2 * P, :]),
                       (new_ffn[:, 2 * P:n_fst], ffn_s[2 * P:, :]),
                       (new_ffn[:, n_fst:], io["ffn_prompt"].rearrange("a b w (k p) -> (a b w k) p", p=P)),
                       (new_conv[:, 0:n_s], io["conv_sample"].rearrange("a b w (k p) -> (a b w k) p", p=P)),
                       (new_conv[:, n_s:], io["conv_prompt"].rearrange("a b w (k p) -> (a b w k) p", p=P))]

            with nc.Block() as block:
                @block.sync
                def _(sp):
                    start_at_one(sp, ["y", "y_out0", "y_out1"])
                    load_gate(sp, gate[:, 0, :], 1, False, "gate_in")
                    load_gate(sp, gate[:, 1, :], 1, True, "gate_in")

                    def load(u, s, src):
                        hold(sp, f"y_out{s}", u * 16 + 1)
                        sp.dma_start(X[:, s, :], src).then_inc(sem(f"x1_in{s}"), 16)

                    def store(u, s, dst):
                        hold(sp, "y", u * 2 + s + 2)
                        sp.dma_start(dst, X[:, s, :]).then_inc(sem(f"y_out{s}"), 16)

                    load(0, 0, x1_scratch[0:P, :])
                    load(0, 1, x1_scratch[P:2 * P, :])
                    for n, (src, dst) in enumerate(HISTORY):
                        sp.wait_ge(sem("history_rows"), n + 1)
                        sp.dma_start(dst, rows[0:src.shape[1], n, :]).then_inc(sem("history_out"), 16)
                    with sp.Fori(0, NPT // 2 - 1, 1) as i:
                        for s in range(2):
                            store(i, s, y_rows(i * 2 + s))
                            load(i + 1, s, x1_scratch[bass.ds((i * 2 + s + 2) * P, P), :])
                    store(NPT // 2 - 1, 0, y_rows(NPT - 2))
                    load(NPT // 2, 0, x1_scratch[NPT * P:, :])
                    store(NPT // 2 - 1, 1, y_rows(NPT - 1))
                    store(NPT // 2, 0, y_sample_rows)
                    sp.wait_ge(sem("y_out0"), 16 * (NPT // 2 + 1) + 1)
                    sp.wait_ge(sem("y_out1"), 16 * (NPT // 2) + 1)
                    sp.wait_ge(sem("history_out"), 16 * len(HISTORY))

                @block.tensor
                def _(pe):
                    for n, (src, _) in enumerate(HISTORY):
                        last = pe.transpose(prow[0:src.shape[1], n // 4, (n % 4) * P:(n % 4 + 1) * P], src, ident[:, :])
                    last.then_inc(sem("history_T"), 1)

                @block.scalar
                def _(act):
                    act.preload_act_table_set("natural_log_exp_and_others")

                    def norm(u, s):
                        t = u * 2 + s
                        link = Link(act, sem("out_norm"), t * 2)
                        flat = lambda ap: ap.rearrange("p (a n) -> p a n", n=HALF)
                        act.wait_ge(sem("y"), u * 2 + 1)
                        tile = M[:, :, :].rearrange("p k t -> p (k t)")[:, bass.ds(t * D, D)]
                        link(act.activation(scratch[:, 1, :], tile, ACT.Square, accum_out=stat[:, s, 0:1]))
                        link(act.activation(stat[:, s, 1:2], stat[:, s, 0:1], ACT.Ln, scale=1.0 / D, bias=eps[:, :]))
                        act.activation(stat[:, s, 2:3], stat[:, s, 1:2], ACT.Exp, scale=-0.5).then_inc(sem("out_rstd"), 1)

                    pairs(act, NPT, norm)
                    norm(NPT // 2, 0)

                @block.vector
                def _(dve):
                    dve.wait_ge(sem("history_T"), 1)
                    for n, (src, _) in enumerate(HISTORY):
                        r = src.shape[1]
                        dve.tensor_copy(rows[0:r, n, :], prow[0:r, n // 4, (n % 4) * P:(n % 4 + 1) * P]) \
                            .then_inc(sem("history_rows"), 1)
                    dve.wait_ge(sem("gate_in"), 16 * (1 + NB))

                    def combine(u, s, which):
                        t = u * 2 + s
                        tile = M[:, :, :].rearrange("p k t -> p (k t)")[:, bass.ds(t * D, D)]
                        dve.wait_ge(sem("out_rstd"), t + 1)
                        dve.wait_ge(sem("y"), t + 1)
                        dve.scalar_tensor_tensor(scratch[:, 0, :], tile, stat[:, s, 2:3], gate[:, which, :], ALU.mult, ALU.mult) \
                            .then_inc(sem("out_scaled"), 1)
                        dve.wait_ge(sem("out_scaled"), t + 1)
                        dve.wait_ge(sem(f"x1_in{s}"), u * 16 + 16)
                        dve.tensor_tensor(X[:, s, :], X[:, s, :], scratch[:, 0, :], ALU.add).then_inc(sem("y"), 1)

                    pairs(dve, NPT, lambda u, s: combine(u, s, 0))
                    combine(NPT // 2, 0, 1)


_ORDER = ["x_prompt", "x_sample", "state_hgrn", "state_conv", "state_ffn_conv", "c_prompt", "c_sample", "w_ada",
          "b_ada", "g_pre_mix", "g_post_mix", "g_pre_ffn", "g_post_ffn", "w_in", "hgrn_lb_logits", "hgrn_norm",
          "w_pa", "conv_w", "w_pb", "w_bgate", "w_o", "w_up", "ffn_conv_w", "w_down"]


def output_shapes(shape):
    depth, batch, heads, dk, dv = shape["state_hgrn"]
    return {
        "y_prompt": shape["x_prompt"],
        "y_sample": shape["x_sample"],
        "hgrn_prompt": (depth, shape["x_prompt"][0], heads, dk, dv),
        "conv_prompt": (depth, shape["x_prompt"][0], *shape["state_conv"][2:]),
        "ffn_prompt": (depth, shape["x_prompt"][0], *shape["state_ffn_conv"][2:]),
        "hgrn_sample": shape["state_hgrn"],
        "conv_sample": shape["state_conv"],
        "ffn_sample": shape["state_ffn_conv"],
    }


def kernel(**inputs):
    import numpy as np
    import concourse.bacc as bacc
    from concourse.bass_utils import run_bass_kernel_spmd

    nc = bacc.Bacc("TRN2", target_bir_lowering=False, num_devices=1)
    arrays = {name: np.ascontiguousarray(inputs[name]) for name in _ORDER}
    io = {name: nc.dram_tensor(name, a.shape, F32, kind="ExternalInput").ap() for name, a in arrays.items()}
    outs = output_shapes({name: tuple(a.shape) for name, a in arrays.items()})
    for name, shape in outs.items():
        io[name] = nc.dram_tensor(name, tuple(shape), F32, kind="ExternalOutput").ap()
    build_trunk(nc, io)
    result = run_bass_kernel_spmd(nc, [arrays], core_ids=[0])
    return tuple(result.results[0][name] for name in outs)
```

```python
from contextlib import ExitStack

import concourse.bass as bass
from concourse import mybir

P = 128
F32 = mybir.dt.float32
F32R = mybir.dt.float32r
U32 = mybir.dt.uint32
ALU = mybir.AluOpType
ACT = mybir.ActivationFunctionType
NEG_HUGE = -3.0e38
LN_FLOOR = 2.0 ** -63
EPS = 1e-6


class Link:

    def __init__(self, eng, sem, base=0):
        self.eng, self.sem, self.base, self.n = eng, sem, base, 0

    def __call__(self, ins):
        self.n += 1
        ins.then_inc(self.sem, 1)
        self.eng.wait_ge(self.sem, self.base + self.n)


def build_trunk(nc, io):
    NP_, D = io["x_prompt"].shape[1:]
    NB, LS = io["x_sample"].shape[:2]
    DFF = io["w_down"].shape[1]
    AW = io["w_pa"].shape[1]
    BW = io["w_pb"].shape[1]
    H = AW // P
    T = NP_ + NB * LS
    KD = D // P
    KF = DFF // P
    KB = BW // P
    NT = T // P
    NPT = NP_ // P
    NG, G = 3, T // 3
    C = NB + 1
    HALF = D // 2
    assert NB * LS == P and G <= 512 and io["state_hgrn"].shape[0] == 1 and KF % 2 == 0
    assert NG * G == T and 2 * G <= NP_ < 3 * G and H == KB == 4 and H * P == 512
    REST = NP_ - 2 * G

    w_in, w_bgate, w_up = io["w_in"][0], io["w_bgate"][0], io["w_up"][0]

    gate_scratch = nc.dram_tensor("gate_rows_scratch", (2, C, D), F32, kind="Internal").ap()
    ada_scratch = nc.dram_tensor("ada_rows_scratch", (6, C, D), F32, kind="Internal").ap()
    kfv_scratch = nc.dram_tensor("k_logf_v_scratch", (3, P, H, T), F32, kind="Internal").ap()
    x1_scratch = nc.dram_tensor("x_after_mixer_scratch", (T, D), F32, kind="Internal").ap()

    top = ExitStack()
    sems, kept, parts = {}, {}, [1]

    def sem(name):
        if name.startswith(("ws_", "late_")):
            if name not in kept:
                kept[name] = nc.alloc_semaphore(name)
            return kept[name]
        if name not in sems:
            sems[name] = nc.alloc_semaphore(f"{name}_part{parts[0]}")
        return sems[name]

    def new_semaphores():
        nc.clear_and_free_semaphores(list(sems.values()))
        sems.clear()
        parts[0] += 1
        nc.all_engine_barrier()

    def hold(sp, name, value):
        sp.wait_ge(sem(name), value)
        sp.sem_inc(sem("sp_passed"), 1)

    def sb(ctx, name, shape, dt=F32, side="left"):
        return ctx.enter_context(nc.sbuf_tensor(name, shape, dt, side=side))

    def pb(ctx, name, shape):
        return ctx.enter_context(nc.psum_tensor(name, shape, F32))

    def f32(ap):
        return ap.bitcast(F32)

    PASSES = ((0, 0), (0, 1), (1, 0))
    SLOTS = 2

    def give_slots(eng, names):
        for name in names:
            eng.sem_inc(sem(name), SLOTS)

    def start_at_one(eng, names):
        for name in names:
            eng.sem_inc(sem(name), 1)

    class WeightStream:

        def __init__(self, name, raw, halves):
            self.name, self.raw, self.halves = name, raw, halves

        def start(self, eng):
            eng.sem_inc(sem(self.name + "_lo"), SLOTS)
            eng.sem_inc(sem(self.name + "_mm"), SLOTS * NG)

        def load(self, sp, u, s, src):
            k = src.shape[0] // P
            hold(sp, self.name + "_lo", u * 2 + (s + 1))
            sp.dma_start(self.raw[:, s, 0:k * P].rearrange("p (k m) -> p k m", m=P),
                         src.rearrange("(k p) m -> p k m", p=P)).then_inc(sem(f"{self.name}_in{s}"), 16)

        def split(self, pool, u, s, k):
            raw, hi, lo = self.raw[:, s, :k * P], self.halves[:, s, 0, :k * P], self.halves[:, s, 1, :k * P]
            pool.wait_ge(sem(f"{self.name}_in{s}"), u * 16 + 16)
            pool.wait_ge(sem(self.name + "_mm"), u * (2 * NG) + (s + 1) * NG)
            pool.tensor_tensor(hi, raw, ones[:, 0:1].to_broadcast([P, k * P]), ALU.mult).then_inc(sem(self.name + "_hi"), 1)
            pool.wait_ge(sem(self.name + "_hi"), u * 2 + (s + 1))
            pool.tensor_tensor(lo, raw, f32(hi), ALU.subtract).then_inc(sem(self.name + "_lo"), 1)

        def product(self, pe, u, s, k, moving, bank, between=None):
            pe.wait_ge(sem(self.name + "_lo"), u * 2 + (s + 3))
            for g in range(NG):
                out, free, value = bank(g)
                pe.wait_ge(sem(free), value)
                for j, (a, b) in enumerate(PASSES):
                    for kt in range(k):
                        last = pe.matmul(out[:, 0:G], self.halves[:, s, a, kt * P:(kt + 1) * P],
                                         moving[:, b, kt, g * G:(g + 1) * G],
                                         start=(j == 0 and kt == 0), stop=(j == 2 and kt == k - 1))
                    if j == 2:
                        last.then_inc(sem(self.name + "_mm"), 1)
                    if between is not None:
                        between(g * 3 + j)

        def arrived(self, eng, u, s, g=NG - 1):
            eng.wait_ge(sem(self.name + "_mm"), u * (2 * NG) + (s * NG + SLOTS * NG + g + 1))

    def groups(ps):
        return ps[:, :, 0:G]

    def by_group(ap):
        return ap.rearrange("p (g t) -> p g t", t=G)

    with top:
        ident = sb(top, "ident", [P, P])
        ones = sb(top, "ones", [P, P])
        eps = sb(top, "eps", [P, 1])
        cs = sb(top, "silu_c", [P, C * KD])
        cols = sb(top, "param_cols", [P, 6 * P])
        scale1 = sb(top, "scale1", [P, KD, C])
        shift1 = sb(top, "shift1", [P, KD, C])
        scale2 = sb(top, "scale2", [P, KD, C])
        shift2 = sb(top, "shift2", [P, KD, C])
        log_bounds = sb(top, "log_lower_bounds", [P, 2, H])
        log_lb, log_1mlb = log_bounds[:, 0, :], log_bounds[:, 1, :]
        new_conv = sb(top, "new_conv", [P, 2 * NB * KB + 2 * KB])
        new_ffn = sb(top, "new_ffn", [P, 2 * NB * KF + 2 * KF])
        h = sb(top, "h", [P, 2, KD, T], F32R)
        Q = sb(top, "q", [P, H, T], side="right")
        M = sb(top, "middle", [P, KD, T])

        def two_slots(ps, name, u, s):
            return lambda g: (ps[s][:, g, :], f"{name}_pfree{s}", u + 1)

        def modulate(dve, name, u, s, pT, full, scale, shift, sample=False):
            t = u * 2 + s
            buf = full[:, s % full.shape[1], :].rearrange("p (k t) -> p k t", t=P)
            src = pT[:, s].rearrange("p a (k t) -> p (a k) t", t=P)
            if sample:
                view = lambda ap: ap.rearrange("p k (b l) -> p k b l", l=LS)
                sc, sh = (m[:, :, 1:C].unsqueeze(3).to_broadcast([P, KD, NB, LS]) for m in (scale, shift))
            else:
                view = lambda ap: ap
                sc, sh = (m[:, :, 0:1].to_broadcast([P, KD, P]) for m in (scale, shift))
            dve.wait_ge(sem(name + "_xT"), t + 3)
            dve.wait_ge(sem(name + "_lo"), t + (2 if full.shape[1] == 1 else 1))
            dve.tensor_tensor(view(buf), view(src), sc, ALU.mult).then_inc(sem(name + "_pT"), 1)
            dve.wait_ge(sem(name + "_pT"), t + 3)
            dve.tensor_tensor(view(buf), view(buf), sh, ALU.add).then_inc(sem(name + "_h"), 1)

        def halves_of_h(pool, name, u, s, full):
            t = u * 2 + s
            tok = bass.ds(t * P, P)
            buf = full[:, s % full.shape[1], :].rearrange("p (k t) -> p k t", t=P)
            pool.wait_ge(sem(name + "_h"), t + 1)
            pool.tensor_tensor(h[:, 0, :, tok], buf, ones[:, 0:1].unsqueeze(1).to_broadcast([P, KD, P]), ALU.mult) \
                .then_inc(sem(name + "_hi"), 1)
            pool.wait_ge(sem(name + "_hi"), t + 1)
            pool.tensor_tensor(h[:, 1, :, tok], buf, f32(h[:, 0, :, tok]), ALU.subtract).then_inc(sem(name + "_lo"), 1)

        def conv3_steps(dve, link, U, Us, y, w):
            ys = y[:, NP_:].rearrange("p (b t) -> p b t", t=LS)

            def step(out, u, n, d):
                tap = u[..., d:d + n]
                if d == 0:
                    link(dve.tensor_scalar(out, tap, w[0], None, ALU.mult))
                else:
                    link(dve.scalar_tensor_tensor(out, tap, w[d], out, ALU.mult, ALU.add))

            return [lambda out=out, u=u, n=n, d=d: step(out, u, n, d)
                    for out, u, n in ((y[:, 0:NP_], U[:, :], NP_), (ys, Us[:, :, :], LS)) for d in range(3)]

        def conv3(dve, link, U, Us, y, w):
            for step in conv3_steps(dve, link, U, Us, y, w):
                step()

        def transposes(pe, name, u, s, xn, pT):
            t = u * 2 + s
            pe.wait_ge(sem(name + "_xn"), t + 2)
            pe.wait_ge(sem(name + "_pT"), t + 1)
            for k in range(KD):
                last = pe.transpose(pT[:, s, k // 4, (k % 4) * P:(k % 4 + 1) * P], xn[:, s % xn.shape[1], k * P:(k + 1) * P],
                                    ident[:, :])
            last.then_inc(sem(name + "_xT"), 1)

        o_bada, o_fcw, o_gmix = 0, 6 * KD, 6 * KD + 3 * KF
        o_gffn = P
        o_cw = o_gffn + KD
        o_an = o_cw + 3 * KB
        o_lb = o_an + 1
        o_gpost = o_lb + H
        o_c = o_gpost + 2 * KD
        o_fst = 2 * P
        n_fst = 2 * NB * KF
        o_cst = 5 * P
        n_cst = 2 * NB * KB
        stack_rows = [o_gmix + KD, o_c + C * KD - P, P, P, n_fst - 2 * P, n_cst]
        assert max(stack_rows) <= P

        mixer = ExitStack()
        ws = WeightStream("ws", sb(mixer, "ws_raw", [P, 2, KD * P]), sb(mixer, "ws_halves", [P, 2, 2, KD * P], F32R))
        bada = cols[:, o_bada:o_bada + 6 * KD].rearrange("p (s k) -> p s k", k=KD)
        cs_k = cs[:, :].rearrange("p (c k) -> p k c", k=KD)

        def ada_product(pe, out, w):
            for k in range(KD):
                last = pe.matmul(out, cs_k[:, k, :], w[:, k, :], start=(k == 0), stop=(k == KD - 1))
            return last

        def ada_rows(section, count):
            return ada_scratch[section:section + count].rearrange("s c (k p) -> (c k) s p", p=P)

        def by_channel(ap):
            return ap.rearrange("p (c k) -> p k c", k=KD)

        ctx = ExitStack()
        with ctx:
            rows = sb(ctx, "param_rows", [P, 6, P])
            wada = sb(ctx, "w_ada_halves", [P, 2, KD, HALF])
            arow = sb(ctx, "ada_rows", [C, 2, D])
            ack = sb(ctx, "ada_rows_by_k", [C * KD, 2, P])
            tiny = sb(ctx, "lb_steps", [P, 8, H])
            xt, xn = Q[:, 0:2, 0:D], Q[:, 2:4, 0:D]
            junk = sb(ctx, "squares", [P, D])
            stat = sb(ctx, "stat", [P, 2, 4])
            pcol = pb(ctx, "p_cols", [P, 2, 512])
            pada = pb(ctx, "p_ada", [P, 2, 512])
            pT = pb(ctx, "p_xT", [P, 2, 2, 512])
            xp_dram = io["x_prompt"][0]
            xs_dram = io["x_sample"].rearrange("b l d -> (b l) d")
            N_ROWS_IN = 15

            def low_half(eng, k):
                eng.wait_ge(sem("h_hi"), k + 1)
                eng.tensor_tensor(h[:, 1, k, :], M[:, k, :], f32(h[:, 0, k, :]), ALU.subtract).then_inc(sem("h_lo"), 1)

            with nc.Block() as block:
                @block.sync
                def _(sp):
                    ws.start(sp)
                    give_slots(sp, ["in_xT", "in_pT", "ada_row"])
                    start_at_one(sp, ["in_xn"])

                    def rows_in(stack, r, src):
                        sp.dma_start(rows[r:r + src.shape[0], stack, :], src).then_inc(sem("rows_in"), 16)

                    rows_in(1, o_c - P, io["c_prompt"].rearrange("b (k p) -> (b k) p", p=P))
                    rows_in(1, o_c - P + KD, io["c_sample"].rearrange("b (k p) -> (b k) p", p=P))
                    rows_in(1, 0, io["g_pre_ffn"].rearrange("a (k p) -> (a k) p", p=P))
                    rows_in(1, o_cw - P, io["conv_w"].rearrange("a w (k p) -> (a w k) p", p=P))
                    rows_in(1, o_an - P, io["hgrn_norm"])
                    rows_in(1, o_lb - P, io["hgrn_lb_logits"].rearrange("a (k p) -> (a k) p", p=P))
                    rows_in(1, o_gpost - P, io["g_post_mix"].rearrange("a (k p) -> (a k) p", p=P))
                    rows_in(1, o_gpost - P + KD, io["g_post_ffn"].rearrange("a (k p) -> (a k) p", p=P))
                    rows_in(0, o_bada, io["b_ada"].rearrange("a (k p) -> (a k) p", p=P))
                    rows_in(0, o_fcw, io["ffn_conv_w"].rearrange("a w (k p) -> (a w k) p", p=P))
                    rows_in(0, o_gmix, io["g_pre_mix"].rearrange("a (k p) -> (a k) p", p=P))
                    fst = io["state_ffn_conv"].rearrange("a b w (k p) -> (a b w k) p", p=P)
                    for n in range(3):
                        rows_in(2 + n, 0, fst[n * P:min((n + 1) * P, n_fst), :])
                    rows_in(5, 0, io["state_conv"].rearrange("a b w (k p) -> (a b w k) p", p=P))
                    for m in range(4):
                        if m >= 2:
                            sp.wait_ge(sem("ada_half"), m - 1)
                        col = (1 - m // 2) * D + m % 2 * HALF
                        sp.dma_start(wada[:, m % 2], io["w_ada"][0, :, col:col + HALF]
                                     .rearrange("(k p) n -> p k n", p=P)).then_inc(sem(f"wada_in{m % 2}"), 16)
                    for s in range(2):
                        ws.load(sp, 0, s, w_in[:, s * P:(s + 1) * P])
                    sp.wait_ge(sem("ada_row"), 4 + SLOTS)
                    for n in range(2):
                        sp.dma_start(ada_scratch[1 - n], arow[:, n, :]).then_inc(sem("ada_out"), 16)
                    sp.wait_ge(sem("ada_out"), 32)
                    sp.dma_start(ack[:, :, :], ada_rows(0, 2)).then_inc(sem("ada_back"), 16)

                @block.gpsimd
                def _(pool):
                    pool.memset(ident[:, :], 0.0).then_inc(sem("ident_zero"), 1)
                    pool.memset(ones[:, :], 1.0).then_inc(sem("consts"), 1)
                    pool.memset(eps[:, :], EPS).then_inc(sem("consts"), 1)
                    pool.wait_ge(sem("ident_zero"), 1)
                    pool.affine_select(out=ident[:, :], in_=ident[:, :], compare_op=ALU.not_equal, fill=1.0,
                                       base=0, pattern=[[-1, P]], channel_multiplier=1).then_inc(sem("ident"), 1)
                    for s in range(2):
                        ws.split(pool, 0, s, KD)
                    for k in range(KD // 2):
                        low_half(pool, k)

                @block.scalar
                def _(act):
                    act.dma_start(xt[:, 0], xp_dram[0:P, :]).then_inc(sem("x_in0"), 16)
                    act.wait_ge(sem("cols"), 6)
                    act.activation(cs[:, :], cols[:, o_c:o_c + C * KD], ACT.Silu).then_inc(sem("cs"), 1)
                    act.preload_act_table_set("natural_log_exp_and_others")
                    act.wait_ge(sem("lb_shifted"), 1)
                    act.activation(tiny[:, 1], tiny[:, 0], ACT.Exp).then_inc(sem("lb_exp"), 1)
                    act.wait_ge(sem("lb_ready"), 1)
                    act.activation(log_1mlb[:, :], tiny[:, 5], ACT.Ln).then_inc(sem("lb_logs"), 1)
                    act.activation(tiny[:, 7], tiny[:, 6], ACT.Ln).then_inc(sem("lb_logs"), 1)
                    act.wait_ge(sem("consts"), 2)

                    def norm(u, s, following):
                        t = u * 2 + s
                        if following is not None:
                            act.wait_ge(sem("in_xn"), t + 1)
                            act.dma_start(xt[:, 1 - s], following).then_inc(sem(f"x_in{1 - s}"), 16)
                        act.wait_ge(sem(f"x_in{s}"), u * 16 + 16)
                        link = Link(act, sem("in_norm"), t * 3)
                        link(act.activation(junk[:, :], xt[:, s], ACT.Square, accum_out=stat[:, s, 0:1]))
                        link(act.activation(stat[:, s, 1:2], stat[:, s, 0:1], ACT.Ln, scale=1.0 / D, bias=eps[:, :]))
                        link(act.activation(stat[:, s, 2:3], stat[:, s, 1:2], ACT.Exp, scale=-0.5))
                        act.wait_ge(sem("in_xT"), t + 1)
                        act.activation(xn[:, s], xt[:, s], ACT.Copy, scale=stat[:, s, 2:3]).then_inc(sem("in_xn"), 1)

                    with act.Fori(0, NPT // 2 - 1, 1) as i:
                        for s in range(2):
                            norm(i, s, xp_dram[bass.ds((i * 2 + s + 1) * P, P), :])
                    norm(NPT // 2 - 1, 0, xp_dram[(NPT - 1) * P:, :])
                    norm(NPT // 2 - 1, 1, xs_dram)
                    norm(NPT // 2, 0, None)
                    for k in range(KD):
                        act.wait_ge(sem("h_full"), k + 1)
                        act.activation(h[:, 0, k, :], M[:, k, :], ACT.Copy).then_inc(sem("h_hi"), 1)

                @block.vector
                def _(dve):
                    dve.wait_ge(sem("rows_T"), 1)
                    for n, r in enumerate(stack_rows):
                        dve.tensor_copy(cols[:, n * P:n * P + r], pcol[:, n // 4, (n % 4) * P:(n % 4) * P + r]) \
                            .then_inc(sem("cols"), 1)
                    dve.wait_ge(sem("cols"), 6)
                    lg = cols[:, o_lb:o_lb + H]
                    link = Link(dve, sem("lb_step"))
                    dve.tensor_tensor(tiny[:, 0], lg, lg, ALU.subtract).then_inc(sem("lb_shifted"), 1)
                    dve.wait_ge(sem("lb_exp"), 1)
                    link(dve.reciprocal(tiny[:, 2], tiny[:, 1]))
                    link(dve.tensor_tensor(tiny[:, 3], tiny[:, 1], tiny[:, 2], ALU.mult))
                    link(dve.tensor_tensor(tiny[:, 4], tiny[:, 3], tiny[:, 3], ALU.subtract))
                    link(dve.tensor_scalar(tiny[:, 5], tiny[:, 4], -1.0, 1.0, ALU.mult, ALU.add))
                    link(dve.tensor_scalar(tiny[:, 6], tiny[:, 4], LN_FLOOR, None, ALU.max))
                    dve.tensor_scalar(log_lb[:, :], tiny[:, 4], 0.0, NEG_HUGE, ALU.is_le, ALU.mult) \
                        .then_inc(sem("lb_ready"), 1)
                    dve.wait_ge(sem("lb_ready"), 1)
                    dve.wait_ge(sem("lb_logs"), 2)
                    dve.tensor_tensor(log_lb[:, :], log_lb[:, :], tiny[:, 7], ALU.add).then_inc(sem("lb_ready"), 1)

                    def rows_of(i, m):
                        dve.wait_ge(sem("ada_half"), i * 2 + (m + 1))
                        dve.tensor_copy(arow[:, bass.ds(i, 1), m * HALF:(m + 1) * HALF], pada[0:C, m, :].unsqueeze(1)) \
                            .then_inc(sem("ada_row"), 1)

                    def keep_tile(u, s):
                        t = u * 2 + s
                        dve.wait_ge(sem("in_xT"), t + 3)
                        dve.tensor_copy(M[:, :, bass.ds(t * P, P)], pT[:, s].rearrange("p a (k t) -> p (a k) t", t=P)) \
                            .then_inc(sem("in_pT"), 1)

                    with dve.Fori(0, 2, 1) as i:
                        for m in range(2):
                            rows_of(i, m)
                            for s in range(2):
                                keep_tile(i * 2 + m, s)
                    keep_tile(NPT // 2, 0)
                    dve.wait_ge(sem("ada_T"), 1)
                    for n, dst in ((1, scale1), (0, shift1)):
                        dve.tensor_tensor(dst[:, :, :], by_channel(pcol[:, 0, n * C * KD:(n + 1) * C * KD]),
                                          bada[:, n, :].unsqueeze(2).to_broadcast([P, KD, C]), ALU.add) \
                            .then_inc(sem("ada_sum"), 1)
                    dve.wait_ge(sem("ada_sum"), 2)
                    dve.scalar_tensor_tensor(scale1[:, :, :], scale1[:, :, :], 1.0,
                                             cols[:, o_gmix:o_gmix + KD].unsqueeze(2).to_broadcast([P, KD, C]),
                                             ALU.add, ALU.mult).then_inc(sem("ada_gain"), 1)
                    dve.wait_ge(sem("ada_gain"), 1)
                    dve.wait_ge(sem("in_pT"), NT + SLOTS)
                    sample = M[:, :, NP_:].rearrange("p k (b l) -> p k b l", l=LS)
                    for n, (op, par) in enumerate(((ALU.mult, scale1), (ALU.add, shift1))):
                        dve.tensor_tensor(sample, sample, par[:, :, 1:C].unsqueeze(3).to_broadcast([P, KD, NB, LS]), op) \
                            .then_inc(sem("h_sample"), 1)
                        dve.wait_ge(sem("h_sample"), n + 1)
                    for k in range(KD):
                        dve.tensor_scalar(M[:, k, 0:NP_], M[:, k, 0:NP_], scale1[:, k, 0:1], shift1[:, k, 0:1],
                                          ALU.mult, ALU.add).then_inc(sem("h_full"), 1)
                    for k in range(KD // 2, KD):
                        dve.wait_ge(sem("h_full"), k + 1)
                        low_half(dve, k)

                @block.tensor
                def _(pe):
                    pe.wait_ge(sem("ident"), 1)
                    pe.wait_ge(sem("rows_in"), 16 * N_ROWS_IN)
                    for n, r in enumerate(stack_rows):
                        last = pe.transpose(pcol[:, n // 4, (n % 4) * P:(n % 4) * P + r], rows[0:r, n, :],
                                            ident[0:r, 0:r])
                    last.then_inc(sem("rows_T"), 1)
                    pe.wait_ge(sem("cs"), 1)

                    pe.wait_ge(sem("cols"), len(stack_rows))
                    with pe.Fori(0, 2, 1) as i:
                        for m in range(2):
                            pe.wait_ge(sem(f"wada_in{m}"), i * 16 + 16)
                            pe.wait_ge(sem("ada_row"), i * 2 + (m + 1))
                            ada_product(pe, pada[0:C, m, :], wada[:, m]).then_inc(sem("ada_half"), 1)
                            for s in range(2):
                                transposes(pe, "in", i * 2 + m, s, xn, pT)
                    transposes(pe, "in", NPT // 2, 0, xn, pT)
                    pe.wait_ge(sem("ada_back"), 16)
                    for n in range(2):
                        last = pe.transpose(pcol[:, 0, n * C * KD:(n + 1) * C * KD], ack[:, n, :],
                                            ident[0:C * KD, 0:C * KD])
                    last.then_inc(sem("ada_T"), 1)

        N_QFI = 3 * H
        ctx = ExitStack()
        with ctx:
            ps = [pb(ctx, f"p_proj{s}", [P, NG, 512]) for s in range(2)]
            pada = pb(ctx, "p_ada_chunk", [P, 2, 512])
            ft = [M[:, n, :] for n in range(4)]
            kst, lst, vst = (M[:, 4 + n, :] for n in range(3))
            CHUNK = 2 * P
            wada = sb(ctx, "w_ada_chunk", [P, 2, KD, CHUNK])
            arow = sb(ctx, "ada_rows_rest", [C, 2 * D])
            AFTER = (2, 2, 2, 1, 1, 0)
            A_TURN = sum(AFTER)
            assert A_TURN * CHUNK == 2 * D and H == 4
            ada_w = io["w_ada"][0]

            with nc.Block() as block:
                @block.sync
                def _(sp):
                    for s in range(2):
                        sp.sem_inc(sem(f"qfi_pfree{s}"), 1)
                    give_slots(sp, ["ada_done", "ada_copied"])

                    def turn(i, ahead):
                        m = 0
                        for n in range(6):
                            for _ in range(AFTER[n]):
                                hold(sp, "ada_done", i * A_TURN + (m + 1))
                                sp.dma_start(wada[:, m % 2], ada_w[:, bass.ds(i * (2 * D) + 2 * D + m * CHUNK, CHUNK)]
                                             .rearrange("(k p) n -> p k n", p=P)).then_inc(sem(f"wada_chunk{m % 2}"), 16)
                                m += 1
                            ahead(i, n + 2)

                    def qfi(i, n):
                        if n < 6:
                            ws.load(sp, i * 3 + n // 2, n % 2, w_in[:, bass.ds(i * (2 * P) + (n // 2 * AW + n % 2 * P), P)])
                        else:
                            qfi(i + 1, n - 6)

                    turn(0, qfi)
                    turn(1, lambda i, n: qfi(i, n) if n < 6 else
                         ws.load(sp, N_QFI // 2, n % 2, w_in[:, 3 * AW + n % 2 * P:3 * AW + (n % 2 + 1) * P]))

                @block.gpsimd
                def _(pool):
                    with pool.Fori(0, 2, 1) as i:
                        for n in range(2, 8):
                            ws.split(pool, i * 3 + n // 2, n % 2, KD)

                @block.tensor
                def _(pe):
                    with pe.Fori(0, 2, 1) as i:
                        m = 0
                        for n in range(6):
                            ws.product(pe, i * 3 + n // 2, n % 2, KD, h, two_slots(ps, "qfi", i * 3 + n // 2, n % 2))
                            for _ in range(AFTER[n]):
                                pe.wait_ge(sem(f"wada_chunk{m % 2}"), i * (A_TURN // 2 * 16) + (m // 2 + 1) * 16)
                                pe.wait_ge(sem("ada_copied"), i * A_TURN + (m + 1))
                                ada_product(pe, pada[0:C, m % 2, 0:CHUNK], wada[:, m % 2]).then_inc(sem("ada_done"), 1)
                                m += 1

                @block.scalar
                def _(act):
                    link = Link(act, sem("f_act"))
                    for i in range(2):
                        for n in range(2):
                            u, s, hd = i * 3, n, i * 2 + n
                            ws.arrived(act, u, s)
                            act.activation(by_group(Q[:, hd, :]), groups(ps[s]), ACT.Silu).then_inc(sem(f"qfi_pfree{s}"), 1)
                        act.preload_act_table_set("natural_log_exp_and_others")
                        for n in range(2):
                            u, s, hd = i * 3 + 1, n, i * 2 + n
                            ws.arrived(act, u, s)
                            if hd:
                                act.wait_ge(sem("f_kexp"), hd)
                                act.wait_ge(sem("f_done"), hd)
                            link(act.activation(by_group(ft[1][:, :]), groups(ps[s]), ACT.Abs))
                            link(act.activation(ft[1][:, :], ft[1][:, :], ACT.Exp, scale=-1.0))
                            act.activation(ft[1][:, :], ft[1][:, :], ACT.Ln, bias=1.0).then_inc(sem("f_softplus"), 1)
                            act.wait_ge(sem("f_kexp"), hd + 1)
                            if hd:
                                act.wait_ge(sem("k_out"), 16 * hd)
                            act.activation(kst[:, :], ft[2][:, :], ACT.Exp, scale=-1.0, bias=log_1mlb[:, hd:hd + 1]) \
                                .then_inc(sem("f_k"), 1)
                            act.wait_ge(sem("f_c"), hd + 1)
                            link(act.activation(ft[3][:, :], ft[0][:, :], ACT.Abs, scale=-1.0, bias=log_lb[:, hd:hd + 1]))
                            link(act.activation(ft[3][:, :], ft[3][:, :], ACT.Exp, scale=-1.0))
                            act.activation(ft[3][:, :], ft[3][:, :], ACT.Ln, bias=1.0).then_inc(sem("f_lse"), 1)
                            act.wait_ge(sem("f_k"), hd + 1)
                            act.dma_start(kfv_scratch[0, :, hd, :], kst[:, :]).then_inc(sem("k_out"), 16)
                            act.wait_ge(sem("f_done"), hd + 1)
                            act.dma_start(kfv_scratch[1, :, hd, :], lst[:, :]).then_inc(sem("f_out"), 16)
                        for n in range(2):
                            u, s, hd = i * 3 + 2, n, i * 2 + n
                            ws.arrived(act, u, s)
                            if hd:
                                act.wait_ge(sem("v_out"), 16 * hd)
                            act.activation(by_group(vst[:, :]), groups(ps[s]), ACT.Copy).then_inc(sem(f"qfi_pfree{s}"), 1)
                            act.wait_ge(sem(f"qfi_pfree{s}"), 3 * i + 4)
                            act.dma_start(kfv_scratch[2, :, hd, :], vst[:, :]).then_inc(sem("v_out"), 16)
                        act.wait_ge(sem("ada_copied"), (i + 1) * A_TURN + SLOTS)
                        act.dma_start(ada_scratch[2 + 2 * i:4 + 2 * i].rearrange("s c d -> c s d"),
                                      arow[:, :].rearrange("c (s d) -> c s d", s=2)).then_inc(sem("ada_out2"), 16)
                    act.wait_ge(sem("ada_out2"), 32)
                    for name in ("k_out", "f_out", "v_out"):
                        act.wait_ge(sem(name), 16 * H)

                @block.vector
                def _(dve):
                    link = Link(dve, sem("f_dve"))

                    def keep_rows(i, chunks):
                        for m in chunks:
                            dve.wait_ge(sem("ada_done"), i * A_TURN + m + 1 + SLOTS)
                            if i:
                                dve.wait_ge(sem("ada_out2"), 16)
                            dve.tensor_copy(arow[:, m * CHUNK:(m + 1) * CHUNK], pada[0:C, m % 2, 0:CHUNK]) \
                                .then_inc(sem("ada_copied"), 1)

                    for hd in range(H):
                        i, s = hd // 2, hd % 2
                        keep_rows(i, range(4) if s == 0 else range(4, 6))
                        z, step = groups(ps[s]), [by_group(f[:, :]) for f in ft]
                        lb = log_lb[:, hd:hd + 1]
                        ws.arrived(dve, i * 3 + 1, s)
                        dve.wait_ge(sem("f_softplus"), hd + 1)
                        link(dve.scalar_tensor_tensor(step[0], z, 0.0, step[1], ALU.min, ALU.subtract))
                        if hd:
                            dve.wait_ge(sem("f_k"), hd)
                        dve.scalar_tensor_tensor(step[2], z, 0.0, step[1], ALU.max, ALU.add).then_inc(sem("f_kexp"), 1)
                        dve.wait_ge(sem("f_kexp"), hd + 1)
                        dve.sem_inc(sem(f"qfi_pfree{s}"), 1)
                        dve.tensor_scalar(ft[0][:, :], ft[0][:, :], log_1mlb[:, hd:hd + 1], None, ALU.add) \
                            .then_inc(sem("f_c"), 1)
                        dve.wait_ge(sem("f_lse"), hd + 1)
                        if hd:
                            dve.wait_ge(sem("f_out"), 16 * hd)
                        dve.scalar_tensor_tensor(lst[:, :], ft[0][:, :], lb, ft[3][:, :], ALU.max, ALU.add) \
                            .then_inc(sem("f_done"), 1)
                        dve.wait_ge(sem("f_done"), hd + 1)
                        if s == 1:
                            keep_rows(i, range(6, A_TURN))

        rec = ExitStack()
        HW = H * P
        R = sb(rec, "decay_in", [P, 2, HW])
        Kc = sb(rec, "k_chunk", [P, 2, HW])
        Vc = sb(rec, "v_chunk", [P, 2, HW])
        L = sb(rec, "decay_out", [P, HW])
        Er = sb(rec, "exp_in", [P, 2, HW // 2])
        El = sb(rec, "exp_out", [P, 2, HW // 2])
        Ql = sb(rec, "q_level", [P, 2, HW // 2])
        Kl = sb(rec, "k_level", [P, 2, HW])
        Qb = sb(rec, "q_decayed", [P, HW])
        Kd = sb(rec, "k_decayed", [P, HW])
        vt = sb(rec, "v_tokens", [P, HW])
        kdt = sb(rec, "kd_tokens", [P, HW])
        A = sb(rec, "attention", [P, HW])
        S = sb(rec, "state", [P, HW])
        LEVELS = P.bit_length() - 1
        SLEVELS = LS.bit_length() - 1
        masks = sb(rec, "level_masks", [P, LEVELS, P // 2])
        pl = pb(rec, "p_levels", [P, 2, HW // 2])
        pt = pb(rec, "p_tokens", [P, 512])
        po = pb(rec, "p_readout", [P, 512])
        px = pb(rec, "p_shared", [P, 512])
        a_norm = cols[:, o_an:o_an + 1]
        CHUNK_STARTS = ("on", "state", "kdt", "fin", "taken", "lnms")

        def heads(ap):
            return ap.rearrange("p (h t) -> p h t", h=H)

        def head(ap, hd):
            return ap[:, hd * P:(hd + 1) * P]

        def blocks(ap, l):
            return ap.rearrange("p (n two t) -> p n two t", two=2, t=1 << l)

        def load_chunk(sp, x, u, s, tok, tile):
            if tile is not None:
                hold(sp, x + "on", tile + 1)
                hold(sp, x + "state", tile * H + 1)
            for dst, n in ((Kc, 0), (R, 1), (Vc, 2)):
                sp.dma_start(heads(dst[:, s, :]), kfv_scratch[n, :, :, tok]).then_inc(sem(f"{x}in{s}"), 16)

        def chunk_in(eng, x, u, s):
            eng.wait_ge(sem(f"{x}in{s}"), u * 48 + 48)

        def chunk_act(act, x, u, s, levels, at_level):
            c = u * 2 + s
            r = R[:, s, :]
            chunk_in(act, x, u, s)
            for l in range(levels):
                if l == 0:
                    act.wait_ge(sem(x + "L0"), c + 1)
                else:
                    act.wait_ge(sem(x + "upd"), c * (2 * levels) + 2 * l)
                if l >= 2:
                    act.wait_ge(sem(x + "prod"), c * (2 * levels) + 2 * (l - 1))
                act.activation(Er[:, l % 2, :].rearrange("p (n t) -> p n t", t=1 << l),
                               blocks(r, l)[:, :, 1, :], ACT.Exp).then_inc(sem(x + "ex"), 1)
                act.activation(El[:, l % 2, :].rearrange("p (n t) -> p n t", t=1 << l),
                               blocks(L[:, :], l)[:, :, 0, :], ACT.Exp).then_inc(sem(x + "ex"), 1)
                if l == 1:
                    act.wait_ge(sem(x + "vT"), c + 1)
                    act.activation(vt[:, :], pt[:, :], ACT.Copy).then_inc(sem(x + "vt"), 1)
                at_level(l)
            act.wait_ge(sem(x + "upd"), c * (2 * levels) + 2 * levels)
            act.activation(L[:, :], L[:, :], ACT.Exp).then_inc(sem(x + "exf"), 1)
            act.activation(r, r, ACT.Exp).then_inc(sem(x + "exf"), 1)
            act.wait_ge(sem(x + "kdT"), c + 1)
            act.activation(kdt[:, :], pt[:, :], ACT.Copy).then_inc(sem(x + "kdt"), 1)
            act.wait_ge(sem(x + "o"), c + 1)
            act.activation(Qb[:, :], po[:, :], ACT.Square).then_inc(sem(x + "sq"), 1)
            at_level(levels)
            act.wait_ge(sem(x + "ms"), c + 1)
            act.activation(Kd[:, :], px[:, :], ACT.Ln, scale=1.0 / P, bias=eps[:, :]).then_inc(sem(x + "lnms"), 1)
            act.wait_ge(sem(x + "lnms"), c + 2)
            act.activation(Kd[:, :], Kd[:, :], ACT.Exp, scale=-0.5).then_inc(sem(x + "rs"), 1)

        def chunk_dve(dve, x, u, s, tok, levels, state_update, at_level):
            c = u * 2 + s
            L2, T1 = 2 * levels, levels + 1
            R_, K_, Q_ = R[:, s, :], Kc[:, s, :], Q[:, :, tok]
            dve.wait_ge(sem(x + "fin"), c * 2 + 1)
            dve.memset(L[:, :], 0.0).then_inc(sem(x + "L0"), 1)
            dve.wait_ge(sem(x + "L0"), c + 1)
            chunk_in(dve, x, u, s)

            def take_diagonal():
                dve.wait_ge(sem(x + "diag"), c + 1)
                dve.wait_ge(sem(x + "taken"), c * T1 + 1)
                dve.sem_inc(sem("dve_passed"), 1)
                dve.copy_predicated(heads(A[:, :]), ident[:, :].bitcast(U32).unsqueeze(1).to_broadcast([P, H, P]),
                                    heads(px[:, :])).then_inc(sem(x + "taken"), 1)

            def take(l):
                dve.wait_ge(sem(x + "lev"), c * levels + (l + 1))
                dve.wait_ge(sem(x + "taken"), c * T1 + (l + 2))
                dve.sem_inc(sem("dve_passed"), 1)
                nb, hh = P >> (l + 1), 1 << l
                out = blocks(A[:, :], l)[:, :, 1, :].rearrange("p (h n) t -> p h n t", h=H)
                mask = masks[:, l, :].bitcast(U32).rearrange("p (n t) -> p n t", t=hh) \
                    .unsqueeze(1).to_broadcast([P, H, nb, hh])
                dve.copy_predicated(out, mask, pl[:, l % 2, :].rearrange("p (h n t) -> p h n t", h=H, t=hh)) \
                    .then_inc(sem(x + "taken"), 1)

            for l in range(levels):
                r, k, lo = blocks(R_, l), blocks(K_, l), blocks(L[:, :], l)
                q = Q_.rearrange("p h (n two t) -> p h n two t", two=2, t=1 << l)
                n, hh = HW >> (l + 1), 1 << l
                half = lambda ap: ap.rearrange("p (n t) -> p n t", t=hh)
                quad = lambda ap: ap.rearrange("p (h n t) -> p h n t", h=H, t=hh)
                dve.wait_ge(sem(x + "ex"), c * L2 + 2 * l + 2)
                dve.tensor_tensor(lo[:, :, 0, :], lo[:, :, 0, :], r[:, :, 1, hh - 1:hh].to_broadcast([P, n, hh]),
                                  ALU.add).then_inc(sem(x + "upd"), 1)
                dve.wait_ge(sem(x + "upd"), c * L2 + 2 * l + 1)
                dve.tensor_tensor(r[:, :, 1, :], r[:, :, 1, :], r[:, :, 0, hh - 1:hh].to_broadcast([P, n, hh]),
                                  ALU.add).then_inc(sem(x + "upd"), 1)
                if l >= 2:
                    dve.wait_ge(sem(x + "lev"), c * levels + (l - 1))
                dve.tensor_tensor(quad(Ql[:, l % 2, :]), quad(Er[:, l % 2, :]), q[:, :, :, 1, :], ALU.mult) \
                    .then_inc(sem(x + "prod"), 1)
                dve.tensor_tensor(blocks(Kl[:, l % 2, :], l)[:, :, 0, :], half(El[:, l % 2, :]), k[:, :, 0, :],
                                  ALU.mult).then_inc(sem(x + "prod"), 1)
                dve.wait_ge(sem(x + "upd"), c * L2 + 2 * l + 2)
                if l == 0:
                    take_diagonal()
                else:
                    take(l - 1)
                at_level(l)
            dve.wait_ge(sem(x + "exf"), c * 2 + 1)
            dve.tensor_tensor(Kd[:, :], L[:, :], K_, ALU.mult).then_inc(sem(x + "fin"), 1)
            dve.wait_ge(sem(x + "exf"), c * 2 + 2)
            dve.tensor_tensor(heads(Qb[:, :]), heads(R_), Q_, ALU.mult).then_inc(sem(x + "fin"), 1)
            take(levels - 1)
            state_update()
            dve.wait_ge(sem(x + "rs"), c + 1)
            dve.scalar_tensor_tensor(Q_, heads(po[:, :]), a_norm, heads(Kd[:, :]), ALU.mult, ALU.mult) \
                .then_inc(sem(x + "on"), 1)

        def chunk_step(pe, x, u, s, tok, levels, step, inter, state_product):
            c = u * 2 + s
            T1 = levels + 1
            if step == "in":
                chunk_in(pe, x, u, s)
                pe.wait_ge(sem(x + "kdt"), c + 1)
                for hd in range(H):
                    last = pe.transpose(head(pt, hd), head(Vc[:, s, :], hd), ident[:, :])
                last.then_inc(sem(x + "vT"), 1)
                pe.wait_ge(sem(x + "lnms"), c + 1)
                for hd in range(H):
                    last = pe.matmul(head(px, hd), head(Kc[:, s, :], hd), Q[:, hd, tok], start=True, stop=True)
                last.then_inc(sem(x + "diag"), 1)
            elif step == "kd":
                pe.wait_ge(sem(x + "fin"), c * 2 + 2)
                pe.wait_ge(sem(x + "vt"), c + 1)
                for hd in range(H):
                    last = pe.transpose(head(pt, hd), head(Kd, hd), ident[:, :])
                last.then_inc(sem(x + "kdT"), 1)
            elif step == "o":
                pe.wait_ge(sem(x + "fin"), c * 2 + 3)
                pe.wait_ge(sem(x + "taken"), c * T1 + (T1 + 1))
                pe.wait_ge(sem(x + "state"), c * H + 1)
                pe.wait_ge(sem(x + "on"), c + 1)
                for hd in range(H):
                    pe.matmul(head(po, hd), head(vt, hd), head(A, hd), start=True, stop=x == "s_")
                    last = inter(hd)
                last.then_inc(sem(x + "o"), 1)
            elif str(step).startswith("state"):
                pe.wait_ge(sem(x + "kdt"), c + 2)
                state_product(c if step == "state" else int(step[5:]))
            elif step == "ms":
                pe.wait_ge(sem(x + "sq"), c + 1)
                pe.wait_ge(sem(x + "state"), c * H + (H + 1))
                pe.matmul(px[:, :], ones[:, :], Qb[:, :], start=True, stop=True).then_inc(sem(x + "ms"), 1)
            else:
                l = step
                pe.wait_ge(sem(x + "prod"), c * (2 * levels) + 2 * l + 2)
                if l >= 1:
                    pe.wait_ge(sem(x + "taken"), c * T1 + (l + 2))
                for hd in range(H):
                    last = pe.matmul(pl[:, l % 2, hd * P // 2:(hd + 1) * P // 2], head(Kl[:, l % 2, :], hd),
                                     Ql[:, l % 2, hd * P // 2:(hd + 1) * P // 2], start=True, stop=True)
                last.then_inc(sem(x + "lev"), 1)

        new_semaphores()
        nothing = lambda l: None
        TM, SG = M[:, 0:KB, :], M[:, KB:KB + H, :]
        U0 = N_QFI // 2
        FIRST_COL = (4 * AW + BW, 4 * AW + 2 * BW, 4 * AW)
        sctx = ExitStack()
        with sctx:
            S0 = [M[:, b // 2, b % 2 * HW:(b % 2 + 1) * HW] for b in range(NB)]
            kdm = sb(sctx, "kd_of_stream", [P, HW])
            in_stream = sb(sctx, "in_stream", [P, NB])
            pst = [pt, px]
            ack = sb(sctx, "ada_rest_by_k", [C * KD, 4, P])
            ada = sb(sctx, "ada_rest", [P, 4, C * KD])
            gk = sb(sctx, "gates_by_k", [C * KD, 2, P])
            pada = pb(sctx, "p_ada_cols", [P, 512])
            pgate = pada
            gring = pb(sctx, "p_g", [P, NG, 512])
            with nc.Block() as block:
                @block.sync
                def _(sp):
                    start_at_one(sp, ["s_" + n for n in CHUNK_STARTS] + [f"g_ring{g}" for g in range(NG)])
                    sp.dma_start(ack[:, :, :], ada_rows(2, 4)).then_inc(sem("ada_back"), 16)
                    load_chunk(sp, "s_", 0, 0, slice(NP_, T), None)
                    for b in range(NB):
                        sp.dma_start(heads(S0[b]), io["state_hgrn"][0, b].rearrange("h k v -> k h v")) \
                            .then_inc(sem("s_S0"), 16)
                    for n in (2, 3):
                        ws.load(sp, U0 + 1, n % 2, w_in[:, 3 * AW + n * P:3 * AW + (n + 1) * P])
                    sp.wait_ge(sem("gate_rows"), 1)
                    sp.dma_start(gate_scratch.rearrange("n c (k p) -> (c k) n p", p=P), gk[:, :, :]) \
                        .then_inc(sem("late_gates"), 16)
                    for n in range(2):
                        ws.load(sp, U0 + 2, n, w_in[:, FIRST_COL[n]:FIRST_COL[n] + P])
                    for b in range(NB):
                        sp.wait_ge(sem("s_new"), b + 1)
                        sp.dma_start(io["hgrn_sample"][0, b].rearrange("h k v -> k h v"), heads(S0[b])) \
                            .then_inc(sem("late_sample_states"), 16)

                @block.gpsimd
                def _(pool):
                    for ap in (masks[:, :, :], in_stream[:, :]):
                        pool.memset(ap, 1.0).then_inc(sem("mask"), 1)
                    for ap in (Kl[:, :, :], A[:, :], S[:, :]):
                        pool.memset(ap, 0.0).then_inc(sem("mask"), 1)
                    pool.wait_ge(sem("mask"), 5)

                    def keep(ap, base, pattern, channel):
                        pool.affine_select(out=ap, in_=ap, compare_op=ALU.is_ge, fill=0.0, base=base, pattern=pattern,
                                           channel_multiplier=channel).then_inc(sem("mask"), 1)

                    for l in range(LEVELS):
                        nb, hh = P >> (l + 1), 1 << l
                        keep(masks[:, l, :].rearrange("p (n t) -> p n t", t=hh), 0, [[-2 * hh, nb], [0, hh]], 1)
                    keep(in_stream[:, :], 0, [[-LS, NB]], 1)
                    pool.wait_ge(sem("mask"), 5 + LEVELS + 1)
                    for l in range(LEVELS):
                        nb, hh = P >> (l + 1), 1 << l
                        keep(masks[:, l, :].rearrange("p (n t) -> p n t", t=hh), hh - 1, [[2 * hh, nb], [0, hh]], -1)
                    keep(in_stream[:, :], LS - 1, [[LS, NB]], -1)
                    pool.wait_ge(sem("mask"), 5 + 2 * (LEVELS + 1))
                    pool.sem_inc(sem("masks_ready"), 1)
                    for n in range(2, 6):
                        ws.split(pool, U0 + n // 2, n % 2, KD)

                @block.scalar
                def _(act):
                    act.preload_act_table_set("natural_log_exp_and_others")

                    def g_out(m):
                        hd, g = m // NG, m % NG
                        ws.arrived(act, U0 + hd // 2, hd % 2, g)
                        act.activation(SG[:, hd, g * G:(g + 1) * G], gring[:, g, 0:G], ACT.Copy) \
                            .then_inc(sem(f"g_ring{g}"), 1)

                    def g_between(l):
                        for m in range(SLEVELS, 10) if l == SLEVELS else (l,):
                            g_out(m)

                    chunk_act(act, "s_", 0, 0, SLEVELS, g_between)
                    for m in range(10, NG * H):
                        g_out(m)

                @block.vector
                def _(dve):
                    def states():
                        dve.wait_ge(sem("s_kdt"), 2)
                        dve.wait_ge(sem("s_S0"), 16 * NB)
                        dve.wait_ge(sem("s_o"), 1)
                        ends = R[:, 0, :].rearrange("p (h b t) -> p b h t", h=H, t=LS)[:, :, :, LS - 1:LS]
                        for b in range(NB):
                            if b:
                                dve.wait_ge(sem("s_mm"), b)
                            dve.tensor_scalar(kdm[:, :], kdt[:, :], in_stream[:, b:b + 1], None, ALU.mult) \
                                .then_inc(sem("s_kdm"), 1)
                            s0 = heads(S0[b])
                            dve.tensor_tensor(s0, s0, ends[:, b].to_broadcast([P, H, P]), ALU.mult) \
                                .then_inc(sem("s_dec"), 1)
                            dve.wait_ge(sem("s_dec"), b + 1)
                            dve.wait_ge(sem("s_mm"), b + 1)
                            dve.tensor_tensor(S0[b], S0[b], pst[b % 2][:, :], ALU.add) \
                                .then_inc(sem("s_new"), 1)
                        dve.wait_ge(sem("s_new"), NB)
                        dve.sem_inc(sem("s_state"), H)

                    link = Link(dve, sem("ada_cols"))
                    dve.wait_ge(sem("ada_T"), 1)
                    rest = ada[:, :, :].rearrange("p s (c k) -> p s c k", k=KD)
                    link(dve.tensor_tensor(rest, pada[:, 0:4 * C * KD].rearrange("p (s c k) -> p s c k", s=4, k=KD),
                                           bada[:, 2:6, :].unsqueeze(2).to_broadcast([P, 4, C, KD]), ALU.add))
                    for n in range(2):
                        link(dve.tensor_tensor(rest[:, 3 * n], rest[:, 3 * n], cols[:, o_gpost + n * KD:o_gpost + (n + 1) * KD]
                                               .unsqueeze(1).to_broadcast([P, C, KD]), ALU.mult))
                    dve.sem_inc(sem("gates_ready"), 1)
                    link(dve.tensor_copy(shift2[:, :, :], by_channel(ada[:, 1])))
                    link(dve.scalar_tensor_tensor(scale2[:, :, :], by_channel(ada[:, 2]), 1.0,
                                                  cols[:, o_gffn:o_gffn + KD].unsqueeze(2).to_broadcast([P, KD, C]),
                                                  ALU.add, ALU.mult))
                    dve.wait_ge(sem("gates_T"), 1)
                    dve.tensor_copy(gk[:, :, :], pgate[0:C * KD, 0:2 * P].rearrange("p (n t) -> p n t", n=2)) \
                        .then_inc(sem("gate_rows"), 1)
                    dve.wait_ge(sem("masks_ready"), 1)
                    chunk_dve(dve, "s_", 0, 0, slice(NP_, T), SLEVELS, states, nothing)

                @block.tensor
                def _(pe):
                    def inter(hd):
                        if hd == 0:
                            pe.wait_ge(sem("s_S0"), 16 * NB)
                        for b in range(NB):
                            at = slice(hd * P + b * LS, hd * P + (b + 1) * LS)
                            last = pe.matmul(po[:, at], head(S0[b], hd), Qb[:, at], start=False,
                                             stop=(b == NB - 1), skip_group_check=True)
                        return last

                    def state_product(b):
                        pe.wait_ge(sem("s_kdm"), b + 1)
                        if b >= 2:
                            pe.wait_ge(sem("s_new"), b - 1)
                        for hd in range(H):
                            last = pe.matmul(head(pst[b % 2], hd), head(kdm, hd), head(vt, hd), start=True, stop=True)
                        last.then_inc(sem("s_mm"), 1)

                    def ada_columns():
                        pe.wait_ge(sem("ada_back"), 16)
                        for n in range(4):
                            last = pe.transpose(pada[:, n * C * KD:(n + 1) * C * KD], ack[:, n, :], ident[0:C * KD, 0:C * KD])
                        last.then_inc(sem("ada_T"), 1)

                    def gate_rows():
                        pe.wait_ge(sem("gates_ready"), 1)
                        for n in range(2):
                            last = pe.transpose(pgate[0:C * KD, n * P:(n + 1) * P], ada[:, 3 * n, :], ident[:, :])
                        last.then_inc(sem("gates_T"), 1)

                    steps = {2: ada_columns, 4: gate_rows, 6: "in", 7: 0, 9: 1, 10: 2, 12: 3, 14: "kd", 16: "o", 32: "ms"}
                    steps.update({18 + 3 * b // 2: f"state{b}" for b in range(NB)})
                    assert SLEVELS == 4 and len(steps) == 10 + NB

                    for n in range(H):
                        def between(run):
                            step = steps.get(n * 9 + run)
                            if callable(step):
                                step()
                            elif step is not None:
                                chunk_step(pe, "s_", 0, 0, slice(NP_, T), SLEVELS, step, inter, state_product)

                        ws.product(pe, U0 + n // 2, n % 2, KD, h, lambda g: (gring[:, g, :], f"g_ring{g}", n + 1), between)

        ctx = ExitStack()
        with ctx:
            ring = pb(ctx, "p_ring", [P, 4, 512])
            U = sb(ctx, "conv_in", [P, 2 + NP_])
            Us = sb(ctx, "conv_in_samples", [P, NB, 2 + LS])
            y = sb(ctx, "conv_out", [P, T])
            taps = sb(ctx, "conv_taps", [P, 3])
            cw = cols[:, o_cw:o_cw + 3 * KB].rearrange("p (w j) -> p w j", j=KB)
            cst = cols[:, o_cst:o_cst + n_cst].rearrange("p (b w j) -> p b w j", w=2, j=KB)
            n_s = 2 * NB * KB
            ncs = new_conv[:, 0:n_s].rearrange("p (b w j) -> p b w j", w=2, j=KB)
            ncp = new_conv[:, n_s:].rearrange("p (w j) -> p w j", j=KB)
            U1 = U0 + H // 2
            TURNS = KB
            assert NPT == 2 * TURNS and TURNS % 2 == 0
            BANK = (0, 1, 2, 3, 0, 1, 2, 3, 1)

            def slot(i, q):
                return i * 3 + (U1 + q // 2), q % 2

            def bank_free(i, jj, m):
                uses = BANK.count(BANK[m])
                return f"ring{BANK[m]}", i * (2 * uses) + (jj * uses + BANK[:m].count(BANK[m]) + 1)

            with nc.Block() as block:
                @block.sync
                def _(sp):
                    start_at_one(sp, ["p_" + n for n in CHUNK_STARTS] + ["b_done"] + [f"ring{b}" for b in range(4)])

                    def tile(q):
                        j, n = q // 3, q % 3
                        if j < TURNS:
                            ws.load(sp, *slot(0, q), w_in[:, FIRST_COL[n] + j * P:FIRST_COL[n] + (j + 1) * P])

                    load_chunk(sp, "p_", 0, 0, slice(0, P), None)
                    for j in range(TURNS):
                        load_chunk(sp, "p_", j, 1, slice((2 * j + 1) * P, (2 * j + 2) * P), 2 * j if j else None)
                        tile(3 * j + 2)
                        tile(3 * j + 3)
                        if j < TURNS - 1:
                            load_chunk(sp, "p_", j + 1, 0, slice((2 * j + 2) * P, (2 * j + 3) * P), 2 * j + 1)
                        tile(3 * j + 4)
                    ws.load(sp, *slot(2, 0), w_bgate[:, D:D + P])
                    ws.load(sp, *slot(2, 1), io["w_pb"][0][:, 0:P])
                    sp.wait_ge(sem("p_state"), H * NPT + 1)
                    sp.dma_start(io["hgrn_prompt"][0, 0].rearrange("h k v -> k h v"), heads(S[:, :])) \
                        .then_inc(sem("late_prompt_state"), 16)
                    sp.wait_ge(sem("late_gates"), 16)

                @block.gpsimd
                def _(pool):
                    with pool.Fori(0, TURNS // 2, 1) as i:
                        for q in range(2, 8):
                            ws.split(pool, *slot(i, q), KD)

                @block.scalar
                def _(act):
                    act.preload_act_table_set("natural_log_exp_and_others")

                    with act.Fori(0, TURNS // 2, 1) as i:
                        for jj in range(2):
                            def c_out(l):
                                if l == 2:
                                    act.wait_ge(sem("b_done"), i * 6 + (jj * 3 + 1))
                                if l in (2, 4, 6):
                                    g = l // 2 - 1
                                    name, free = bank_free(i, jj, g)
                                    ws.arrived(act, *slot(i, 3 * jj), g)
                                    act.activation(y[:, g * G:(g + 1) * G], ring[:, BANK[g], 0:G], ACT.Copy) \
                                        .then_inc(sem(name), 1)
                                    if g == NG - 1:
                                        act.wait_ge(sem(name), free + 1)
                                        act.sem_inc(sem("c_done"), 1)

                            u = i * 2 + jj
                            chunk_act(act, "p_", u, 0, LEVELS, c_out)
                            chunk_act(act, "p_", u, 1, LEVELS, nothing)

                @block.vector
                def _(dve):
                    dve.memset(U[:, 0:2], 0.0).then_inc(sem("u_zero"), 1)
                    dve.wait_ge(sem("u_zero"), 1)
                    dve.wait_ge(sem("late_sample_states"), 16 * NB)

                    def turn(i, jj):
                        j = i * 2 + jj
                        one = bass.ds(j, 1)
                        link = Link(dve, sem("conv_step"), i * 22 + jj * 11)

                        def state(s):
                            def update():
                                dve.wait_ge(sem("p_st"), j * 2 + (s + 1))
                                for hd in range(H):
                                    dve.scalar_tensor_tensor(head(S, hd), head(S, hd), R[:, s, (hd + 1) * P - 1:(hd + 1) * P],
                                                             head(px, hd), ALU.mult, ALU.add).then_inc(sem("p_state"), 1)
                            return update

                        def history_in():
                            link(dve.tensor_scalar(Us[:, :, 0:2].unsqueeze(3), cst[:, :, :, one], 1.0, None, ALU.mult))
                            link(dve.tensor_scalar(taps[:, :].unsqueeze(2), cw[:, :, one], 1.0, None, ALU.mult))
                            dve.wait_ge(sem("c_done"), j + 1)

                        def conv_in(g):
                            bank = BANK[NG + g]
                            name, free = bank_free(i, jj, NG + g)
                            ws.arrived(dve, *slot(i, 3 * jj + 1), g)
                            if g < 2:
                                dve.tensor_tensor(U[:, 2 + g * G:2 + (g + 1) * G], ring[:, bank, 0:G], y[:, g * G:(g + 1) * G],
                                                  ALU.mult).then_inc(sem(name), 1)
                            else:
                                link(dve.tensor_tensor(U[:, 2 + 2 * G:], ring[:, bank, 0:REST], y[:, 2 * G:NP_], ALU.mult))
                                dve.tensor_tensor(Us[:, :, 2:], ring[:, bank, REST:G].rearrange("p (b t) -> p b t", t=LS),
                                                  y[:, NP_:].rearrange("p (b t) -> p b t", t=LS), ALU.mult) \
                                    .then_inc(sem(name), 1)
                            dve.wait_ge(sem(name), free + 1)

                        def histories():
                            link(dve.tensor_scalar(ncs[:, :, :, one], Us[:, :, LS:].unsqueeze(3), 1.0, None, ALU.mult))
                            link(dve.tensor_scalar(ncp[:, :, one], U[:, NP_:].unsqueeze(2), 1.0, None, ALU.mult))

                        def b_out():
                            for g in range(NG):
                                bank = BANK[2 * NG + g]
                                ws.arrived(dve, *slot(i, 3 * jj + 2), g)
                                dve.tensor_tensor(TM[:, one, g * G:(g + 1) * G].rearrange("p a t -> p (a t)"),
                                                  ring[:, bank, 0:G], y[:, g * G:(g + 1) * G], ALU.mult) \
                                    .then_inc(sem("b_done"), 1)
                                dve.wait_ge(sem("b_done"), i * 6 + (jj * 3 + g + 2))
                                dve.sem_inc(sem(f"ring{bank}"), 1)

                        conv = conv3_steps(dve, link, U, Us, y, [taps[:, w:w + 1] for w in range(3)])

                        def conv_branch(l):
                            if l == 0:
                                history_in()
                            elif l == 1:
                                conv_in(0)
                                conv_in(1)
                            elif l == 2:
                                conv_in(2)
                            elif l < LEVELS - 1:
                                conv[l - 3]()
                            else:
                                for step in conv[3:]:
                                    step()
                                histories()

                        chunk_dve(dve, "p_", j, 0, bass.ds(j * (2 * P), P), LEVELS, state(0), nothing)
                        chunk_dve(dve, "p_", j, 1, bass.ds(j * (2 * P) + P, P), LEVELS, state(1), conv_branch)
                        b_out()

                    with dve.Fori(0, TURNS // 2, 1) as i:
                        for jj in range(2):
                            turn(i, jj)

                @block.tensor
                def _(pe):
                    FIRST = (0, 1, 2, 3, 5, 6, 7, 8, 9, 10, 11, 12)
                    SECOND = (13, 14, 15, 17, 18, 20, 21, 22, 23, 24, 25, 26)
                    names = ("in", *range(LEVELS), "kd", "o", "state", "ms")
                    steps = {run: (c, step) for c, runs in enumerate((FIRST, SECOND)) for run, step in zip(runs, names)}

                    def inter(hd):
                        return pe.matmul(head(po, hd), head(S, hd), head(Qb, hd), start=False, stop=True)

                    def state_product(c):
                        for hd in range(H):
                            last = pe.matmul(head(px, hd), head(kdt, hd), head(vt, hd), start=True, stop=True)
                        last.then_inc(sem("p_st"), 1)

                    with pe.Fori(0, TURNS // 2, 1) as i:
                        for q in range(6):
                            jj, n = q // 3, q % 3

                            def between(run):
                                c, step = steps.get(n * 9 + run, (0, None))
                                if step is not None:
                                    tok = bass.ds(i * (4 * P) + (jj * 2 + c) * P, P)
                                    chunk_step(pe, "p_", i * 2 + jj, c, tok, LEVELS, step, inter, state_product)

                            ws.product(pe, *slot(i, q), KD, h,
                                       lambda g: (ring[:, BANK[3 * n + g], :], *bank_free(i, jj, 3 * n + g)), between)
        rec.close()

        new_semaphores()
        ctx = ExitStack()
        with ctx:
            branch = sb(ctx, "branch", [P, 2, H, T], F32R)
            ps = [pb(ctx, f"p_mix{s}", [P, NG, 512]) for s in range(2)]
            sg = sb(ctx, "gate_sigmoid", [P, T])
            gated = sb(ctx, "gated", [P, T])
            U0 = (N_QFI + 4 * KB) // 2
            HALVES = ((D, io["w_pb"][0], U0), (0, io["w_pa"][0], U0 + KD))

            with nc.Block() as block:
                @block.sync
                def _(sp):
                    start_at_one(sp, ["mix_pfree0", "mix_pfree1", "mix_z"])
                    for n, (col, w_proj, u0) in enumerate(HALVES):
                        with sp.Fori(1, KD, 1) as j:
                            ws.load(sp, j + u0, 0, w_bgate[:, bass.ds(j * P + col, P)])
                            ws.load(sp, j + u0, 1, w_proj[:, bass.ds(j * P, P)])
                        if n == 0:
                            ws.load(sp, HALVES[1][2], 0, w_bgate[:, 0:P])
                            ws.load(sp, HALVES[1][2], 1, HALVES[1][1][:, 0:P])
                            sp.wait_ge(sem("branch_hi"), 2 * H)
                            sp.wait_ge(sem("branch_lo"), 2 * H)
                            for k in range(H):
                                sp.dma_start(Q[:, k, 0:D], io["w_o"][0, k * P:(k + 1) * P, :]).then_inc(sem(f"wo_in{k}"), 16)

                @block.gpsimd
                def _(pool):
                    with pool.Fori(1, 2 * KD, 1) as j:
                        ws.split(pool, j + U0, 0, KD)
                        ws.split(pool, j + U0, 1, H)

                @block.tensor
                def _(pe):
                    for n, (_, _, u0) in enumerate(HALVES):
                        def turn(j):
                            local = j + n * KD
                            ws.product(pe, j + u0, 0, KD, h, two_slots(ps, "mix", local, 0))
                            if isinstance(j, int):
                                pe.wait_ge(sem("branch_lo"), (n + 1) * H)
                            ws.product(pe, j + u0, 1, H, branch, two_slots(ps, "mix", local, 1))
                        turn(0)
                        with pe.Fori(1, KD, 1) as j:
                            turn(j)

                @block.scalar
                def _(act):
                    act.wait_ge(sem("late_prompt_state"), 16)
                    for k in range(H):
                        act.activation(branch[:, 0, k, :], TM[:, k, :], ACT.Copy).then_inc(sem("branch_hi"), 1)
                    act.activation(SG, SG, ACT.Silu).then_inc(sem("silu_g"), 1)
                    for n, (_, _, u0) in enumerate(HALVES):
                        if n == 1:
                            ws.arrived(act, u0 - 1, 1)
                            for k in range(H):
                                act.activation(branch[:, 0, k, :], Q[:, k, :], ACT.Copy).then_inc(sem("branch_hi"), 1)
                        with act.Fori(0, KD, 1) as j:
                            ws.arrived(act, j + u0, 0)
                            act.wait_ge(sem("mix_pfree1"), j + (n * KD + 1))
                            act.activation(by_group(sg[:, :]), groups(ps[0]), ACT.Sigmoid).then_inc(sem("mix_pfree0"), 1)

                @block.vector
                def _(dve):
                    dve.wait_ge(sem("late_prompt_state"), 16)
                    for k in range(H):
                        dve.wait_ge(sem("branch_hi"), k + 1)
                        dve.tensor_tensor(branch[:, 1, k, :], TM[:, k, :], f32(branch[:, 0, k, :]), ALU.subtract) \
                            .then_inc(sem("branch_lo"), 1)
                    dve.wait_ge(sem("silu_g"), 1)
                    dve.tensor_tensor(Q[:, :, :], Q[:, :, :], SG, ALU.mult).then_inc(sem("readout_gated"), 1)
                    dve.wait_ge(sem("branch_lo"), H)
                    dve.wait_ge(sem("readout_gated"), 1)
                    for n, (_, _, u0) in enumerate(HALVES):
                        if n == 1:
                            for k in range(H):
                                dve.wait_ge(sem("branch_hi"), H + k + 1)
                                dve.tensor_tensor(branch[:, 1, k, :], Q[:, k, :], f32(branch[:, 0, k, :]), ALU.subtract) \
                                    .then_inc(sem("branch_lo"), 1)
                        with dve.Fori(0, KD, 1) as j:
                            z = M[:, bass.ds(j, 1), :]
                            ws.arrived(dve, j + u0, 1)
                            dve.wait_ge(sem("mix_pfree0"), j + (n * KD + 2))
                            if n == 0:
                                dve.tensor_tensor(z.rearrange("p a (g t) -> p (a g) t", t=G), by_group(sg[:, :]),
                                                  groups(ps[1]), ALU.mult).then_inc(sem("mix_pfree1"), 1)
                            else:
                                dve.wait_ge(sem("mix_z"), j + 1)
                                dve.tensor_tensor(by_group(gated[:, :]), by_group(sg[:, :]), groups(ps[1]), ALU.mult) \
                                    .then_inc(sem("mix_pfree1"), 1)
                                dve.wait_ge(sem("mix_pfree1"), j + (KD + 2))
                                dve.tensor_tensor(z, z, gated[:, :].unsqueeze(1), ALU.add).then_inc(sem("mix_z"), 1)
        mixer.close()

        def token_rows(name_p, name_s):
            prompt = io[name_p][0]
            return (lambda t: prompt[bass.ds(t * P, P), :]), io[name_s].rearrange("b l d -> (b l) d")

        def load_gate(sp, dst, n, sample, sem_name):
            if sample:
                for b in range(NB):
                    sp.dma_start(dst[b * LS:(b + 1) * LS, :], gate_scratch[n, b + 1:b + 2, :].to_broadcast([LS, D])) \
                        .then_inc(sem(sem_name), 16)
            else:
                sp.dma_start(dst, gate_scratch[n, 0:1, :].to_broadcast([P, D])).then_inc(sem(sem_name), 16)

        x_rows, x_sample_rows = token_rows("x_prompt", "x_sample")
        late = ExitStack()
        wo = sb(late, "w_o_halves", [P, 2, KD, D], F32R, "right")
        late.close()
        wup = WeightStream("wup", sb(late, "wup_raw", [P, 2, KD * P], side="right"),
                           sb(late, "wup_halves", [P, 2, 2, KD * P], F32R, "right"))
        w_gate, w_val, w_dn = w_up[:, 0:DFF], w_up[:, DFF:], io["w_down"][0]
        ctx = ExitStack()
        with ctx:
            X = sb(ctx, "x_tile_mid", [P, 2, D])
            raw = [Q[:, 0, 0:D], Q[:, 1, 0:D], Q[:, 2, 0:D], Q[:, 3, 0:D], X[:, 0, :], X[:, 1, :], Q[:, 0, 0:D], Q[:, 1, 0:D]]
            full, gate, xn = Q[:, 0:1, 0:D], Q[:, 2, 0:D], Q[:, 3:4, 0:D]
            stat = sb(ctx, "stat_mid", [P, 8])
            pm = pb(ctx, "p_m", [P, 2, 2, 512])
            pT = pb(ctx, "p_x1T", [P, 2, 2, 512])
            w_o = io["w_o"][0]

            def z_slot(s):
                return h[:, :, :, (NPT - 1 + s) * P:(NPT + s) * P]

            last_tile = full[:, 0, :].rearrange("p (k t) -> p k t", t=P)

            with nc.Block() as block:
                @block.sync
                def _(sp):
                    give_slots(sp, ["mid_xT", "mid_pT", "mid_lo", "m_used"])
                    wup.start(sp)
                    start_at_one(sp, ["m_mm", "mid_xn", "x1_out0", "x1_out1"])
                    for k in range(H, KD):
                        if k >= H + 2:
                            sp.wait_ge(sem("wo_lo"), k - H - 1)
                        sp.dma_start(raw[k], w_o[k * P:(k + 1) * P, :]).then_inc(sem(f"wo_in{k}"), 16)
                    sp.wait_ge(sem("wo_lo"), 3)
                    load_gate(sp, gate, 0, False, "gate_mix_in")
                    sp.wait_ge(sem("wo_lo"), KD)

                    def load_x(u, s, src, normed):
                        if normed is not None:
                            hold(sp, "mid_xn", normed + 1)
                        hold(sp, f"x1_out{s}", u * 16 + 1)
                        sp.dma_start(X[:, s, :], src).then_inc(sem(f"x_mid_in{s}"), 16)

                    def store(u, s, dst):
                        hold(sp, "x1", u * 2 + s + 1)
                        sp.dma_start(dst, X[:, s, :]).then_inc(sem(f"x1_out{s}"), 16)

                    load_x(0, 0, x_rows(0), None)
                    with sp.Fori(0, NPT // 2 - 1, 1) as i:
                        for s in range(2):
                            load_x(i + s, 1 - s, x_rows(i * 2 + s + 1), i * 2 + s)
                            store(i, s, x1_scratch[bass.ds((i * 2 + s) * P, P), :])
                    i = NPT // 2 - 1
                    load_x(i, 1, x_rows(NPT - 1), NPT - 2)
                    store(i, 0, x1_scratch[(NPT - 2) * P:(NPT - 1) * P, :])
                    load_x(NPT // 2, 0, x_sample_rows, NPT - 1)
                    store(i, 1, x1_scratch[(NPT - 1) * P:NPT * P, :])
                    sp.wait_ge(sem("x1"), NPT)
                    load_gate(sp, gate, 0, True, "gate_mix_s_in")
                    sp.wait_ge(sem("m_mm"), NT + 1)
                    wup.load(sp, 0, 0, w_gate[:, 0:P])
                    wup.load(sp, 0, 1, w_val[:, 0:P])
                    store(NPT // 2, 0, x1_scratch[NPT * P:, :])
                    sp.wait_ge(sem("x1_out0"), 16 * (NPT // 2 + 1) + 1)
                    sp.wait_ge(sem("x1_out1"), 16 * (NPT // 2) + 1)

                @block.gpsimd
                def _(pool):
                    def z_lo(t, s):
                        pool.wait_ge(sem("z_hi"), t + 1)
                        z = z_slot(s)
                        pool.tensor_tensor(z[:, 1], M[:, :, bass.ds(t * P, P)], f32(z[:, 0]), ALU.subtract) \
                            .then_inc(sem("z_lo"), 1)

                    z_lo(0, 0)
                    z_lo(1, 1)
                    with pool.Fori(0, NPT // 2 - 1, 1) as i:
                        for s in range(2):
                            z_lo(i * 2 + s + 2, s)
                            halves_of_h(pool, "mid", i, s, full)
                    z_lo(NPT, 0)
                    for s in range(2):
                        halves_of_h(pool, "mid", NPT // 2 - 1, s, full)
                    for s in range(2):
                        wup.split(pool, 0, s, KD)

                @block.scalar
                def _(act):
                    act.preload_act_table_set("natural_log_exp_and_others")
                    def z_hi(t, s):
                        act.activation(z_slot(s)[:, 0], M[:, :, bass.ds(t * P, P)], ACT.Copy).then_inc(sem("z_hi"), 1)

                    for k in range(KD):
                        if k == 2:
                            z_hi(0, 0)
                        act.wait_ge(sem(f"wo_in{k}"), 16)
                        act.activation(wo[:, 0, k, :], raw[k], ACT.Copy).then_inc(sem("wo_hi"), 1)

                    def norms(u, s, following):
                        t = u * 2 + s
                        link = Link(act, sem("mid_norm"), t * 4)

                        def rstd(at):
                            link(act.activation(stat[:, at + 1:at + 2], stat[:, at:at + 1], ACT.Ln, scale=1.0 / D,
                                                bias=eps[:, :]))
                            act.activation(stat[:, at + 2:at + 3], stat[:, at + 1:at + 2], ACT.Exp, scale=-0.5) \
                                .then_inc(sem("mid_rstd"), 1)

                        act.wait_ge(sem("m_mm"), t + 2)
                        if following is not None:
                            z_hi(following, s)
                        act.wait_ge(sem("mid_xT"), t + 2)
                        link(act.activation(xn[:, 0, :].rearrange("p (a n) -> p a n", a=2), pm[:, s], ACT.Square,
                                            accum_out=stat[:, 0:1]))
                        rstd(0)
                        act.wait_ge(sem("x1"), t + 1)
                        link(act.activation(xn[:, 0, :], X[:, s, :], ACT.Square, accum_out=stat[:, 4:5]))
                        rstd(4)
                        act.wait_ge(sem("mid_rstd"), t * 2 + 2)
                        act.activation(xn[:, 0, :], X[:, s, :], ACT.Copy, scale=stat[:, 6:7]).then_inc(sem("mid_xn"), 1)

                    z_hi(1, 1)
                    with act.Fori(0, NPT // 2 - 1, 1) as i:
                        for s in range(2):
                            norms(i, s, i * 2 + s + 2)
                    norms(NPT // 2 - 1, 0, NPT)
                    norms(NPT // 2 - 1, 1, None)
                    norms(NPT // 2, 0, None)
                    act.wait_ge(sem("mid_h"), NT)
                    act.activation(h[:, 0, :, NP_:], last_tile, ACT.Copy).then_inc(sem("mid_hi"), 1)

                @block.vector
                def _(dve):
                    for k in range(KD):
                        dve.wait_ge(sem("wo_hi"), k + 1)
                        dve.tensor_tensor(wo[:, 1, k, :], raw[k], f32(wo[:, 0, k, :]), ALU.subtract) \
                            .then_inc(sem("wo_lo"), 1)

                    def residual(u, s, sample):
                        t = u * 2 + s
                        flat = lambda ap: ap.rearrange("p (a n) -> p a n", a=2)
                        dve.wait_ge(sem("mid_rstd"), t * 2 + 1)
                        dve.wait_ge(sem("mid_lo"), t + 2)
                        dve.wait_ge(sem("gate_mix_in"), 16)
                        if sample:
                            dve.wait_ge(sem("gate_mix_s_in"), 16 * NB)
                        dve.scalar_tensor_tensor(flat(full[:, 0, :]), pm[:, s], stat[:, 2:3], flat(gate), ALU.mult,
                                                 ALU.mult).then_inc(sem("m_used"), 1)
                        dve.wait_ge(sem("m_used"), t + 3)
                        dve.wait_ge(sem(f"x_mid_in{s}"), u * 16 + 16)
                        dve.tensor_tensor(X[:, s, :], X[:, s, :], full[:, 0, :], ALU.add).then_inc(sem("x1"), 1)
                        dve.wait_ge(sem("x1"), t + 1)

                    with dve.Fori(0, NPT // 2, 1) as i:
                        for s in range(2):
                            residual(i, s, False)
                            modulate(dve, "mid", i, s, pT, full, scale2, shift2)
                    residual(NPT // 2, 0, True)
                    modulate(dve, "mid", NPT // 2, 0, pT, full, scale2, shift2, sample=True)
                    dve.wait_ge(sem("mid_h"), NT)
                    dve.wait_ge(sem("mid_hi"), NT)
                    dve.tensor_tensor(h[:, 1, :, NP_:], last_tile, f32(h[:, 0, :, NP_:]), ALU.subtract).then_inc(sem("mid_lo"), 1)

                @block.tensor
                def _(pe):
                    def out_product(t, s):
                        pe.wait_ge(sem("z_lo"), t + 1)
                        pe.wait_ge(sem("m_used"), t + 1)
                        for half in range(2):
                            for j, (a, b) in enumerate(PASSES):
                                for k in range(KD):
                                    last = pe.matmul(pm[:, s, half, :], z_slot(s)[:, a, k, :],
                                                     wo[:, b, k, half * HALF:(half + 1) * HALF],
                                                     start=(j == 0 and k == 0), stop=(j == 2 and k == KD - 1))
                        last.then_inc(sem("m_mm"), 1)

                    for j, (a, b) in enumerate(((0, 0), (1, 0), (0, 1))):
                        if j == 1:
                            pe.wait_ge(sem("z_lo"), 1)
                        for k in range(KD):
                            if a == 0:
                                if k == 0 and b == 0:
                                    pe.wait_ge(sem("z_hi"), 1)
                                pe.wait_ge(sem(("wo_hi", "wo_lo")[b]), k + 1)
                            for half in range(2):
                                last = pe.matmul(pm[:, 0, half, :], z_slot(0)[:, a, k, :],
                                                 wo[:, b, k, half * HALF:(half + 1) * HALF],
                                                 start=(j == 0 and k == 0), stop=(j == 2 and k == KD - 1))
                    last.then_inc(sem("m_mm"), 1)
                    with pe.Fori(0, NPT // 2, 1) as i:
                        for s in range(2):
                            out_product(i * 2 + s + 1, 1 - s)
                            transposes(pe, "mid", i, s, xn, pT)
                    transposes(pe, "mid", NPT // 2, 0, xn, pT)

        out_sum = M[:, :, :].rearrange("p k t -> p (k t)").rearrange("p (t a n) -> p t a n", a=2, n=HALF)

        def out_tile(t):
            return M[:, :, :].rearrange("p k t -> p (k t)")[:, t * D:(t + 1) * D]

        y_rows, y_sample_rows = token_rows("y_prompt", "y_sample")
        ctx = ExitStack()
        with ctx:
            ps = [pb(ctx, f"p_up{s}", [P, NG, 512]) for s in range(2)]
            pdn = pb(ctx, "p_down", [P, 2, 512])
            wd_raw = sb(ctx, "w_down_raw", [P, 2, D], side="right")
            wd = sb(ctx, "w_down_halves", [P, 2, 2, D], F32R, "right")
            ff = sb(ctx, "mlp_hidden", [P, 2, 2, T], F32R, "right")
            room = Q[:, :, :].rearrange("p h t -> p (h t)")
            gate = [room[:, n * D:(n + 1) * D] for n in range(2)]
            small = room[:, 4 * D:]
            Us = small[:, 0:NB * (2 + LS)].rearrange("p (b t) -> p b t", t=2 + LS)
            fw, stat = small[:, 160:163], small[:, 192:192 + NT * 3].rearrange("p (t n) -> p t n", n=3)
            X = [room[:, 2 * D:3 * D], room[:, 3 * D:4 * D], wd_raw[:, 0], wd_raw[:, 1], wup.raw[:, 0], wup.raw[:, 1]]
            assert NB * (2 + LS) <= 160 and 192 + NT * 3 <= 4 * (T - D)
            U = sb(ctx, "gate_in", [P, 2 + NP_])
            y = sb(ctx, "gate_conv", [P, T])
            TURNS, DOWNS = KF // 2, NT * 2
            fcw = cols[:, o_fcw:o_fcw + 3 * KF].rearrange("p (w f) -> p w f", f=KF)
            fst = cols[:, o_fst:o_fst + n_fst].rearrange("p (b w f) -> p b w f", w=2, f=KF)
            nfs = new_ffn[:, 0:n_fst].rearrange("p (b w f) -> p b w f", w=2, f=KF)
            nfp = new_ffn[:, n_fst:].rearrange("p (w f) -> p w f", f=KF)
            rows = U[:, 0:6 * P].rearrange("p (n t) -> p n t", t=P)
            n_s = 2 * NB * KB
            ffn_s = io["ffn_sample"].rearrange("a b w (k p) -> (a b w k) p", p=P)
            HISTORY = [(new_ffn[:, 0:P], ffn_s[0:P, :]), (new_ffn[:, P:2 * P], ffn_s[P:2 * P, :]),
                       (new_ffn[:, 2 * P:n_fst], ffn_s[2 * P:, :]),
                       (new_ffn[:, n_fst:], io["ffn_prompt"].rearrange("a b w (k p) -> (a b w k) p", p=P)),
                       (new_conv[:, 0:n_s], io["conv_sample"].rearrange("a b w (k p) -> (a b w k) p", p=P)),
                       (new_conv[:, n_s:], io["conv_prompt"].rearrange("a b w (k p) -> (a b w k) p", p=P))]

            def history_psum(n):
                return ps[0][0:HISTORY[n][0].shape[1], n // 4, (n % 4) * P:(n % 4 + 1) * P]

            with nc.Block() as block:
                @block.sync
                def _(sp):
                    start_at_one(sp, ["wup_pfree0", "wup_pfree1"])
                    give_slots(sp, ["down_free"])
                    start_at_one(sp, ["wd_lo", "down_mm", "conv_read", "ff_lo"])

                    def load_x1(t):
                        sp.dma_start(X[t % len(X)], x1_scratch[t * P:(t + 1) * P, :]).then_inc(sem(f"x1_in{t}"), 16)

                    def up_tiles(u, f):
                        wup.load(sp, u + f, 0, w_gate[:, bass.ds((u + f) * P, P)])
                        wup.load(sp, u + f, 1, w_val[:, bass.ds((u + f) * P, P)])

                    def down_tile(g):
                        hold(sp, "wd_lo", g + 1)
                        sp.dma_start(wd_raw[:, :, :], w_dn[bass.ds(g * (2 * P), 2 * P), :]
                                     .rearrange("(f p) n -> p f n", p=P)).then_inc(sem("wd_in"), 16)

                    with sp.Fori(0, TURNS - 1, 1) as g:
                        up_tiles(g * 2, 1)
                        down_tile(g)
                        up_tiles(g * 2, 2)
                    up_tiles(KF - 2, 1)
                    down_tile(TURNS - 1)
                    load_gate(sp, gate[0], 1, False, "gate_in")
                    load_gate(sp, gate[1], 1, True, "gate_in")
                    load_x1(0)
                    load_x1(1)
                    sp.wait_ge(sem("wd_lo"), TURNS + 1)
                    load_x1(2)
                    load_x1(3)
                    sp.wait_ge(sem("wup_mm"), 2 * NG * (KF + 1))
                    load_x1(4)
                    load_x1(5)
                    for n, (src, dst) in enumerate(HISTORY):
                        sp.wait_ge(sem("history_rows"), n + 1)
                        sp.dma_start(dst, rows[0:src.shape[1], n, :]).then_inc(sem("history_out"), 16)
                    for t in range(NT):
                        sp.wait_ge(sem("y"), t + 1)
                        sp.dma_start(y_rows(t) if t < NPT else y_sample_rows, X[t % len(X)]).then_inc(sem(f"y_out{t}"), 16)
                        if t >= 2 and t - 2 + len(X) < NT:
                            sp.wait_ge(sem(f"y_out{t - 2}"), 16)
                            load_x1(t - 2 + len(X))
                    sp.wait_ge(sem("history_out"), 16 * len(HISTORY))
                    for t in range(NT):
                        sp.wait_ge(sem(f"y_out{t}"), 16)

                @block.gpsimd
                def _(pool):
                    def up_tiles(u, f):
                        wup.split(pool, u + f, 0, KD)
                        wup.split(pool, u + f, 1, KD)

                    def down_tile(g):
                        hi, lo = wd[:, 0, :, :], wd[:, 1, :, :]
                        pool.wait_ge(sem("wd_in"), g * 16 + 16)
                        pool.wait_ge(sem("down_mm"), g * DOWNS + 1)
                        pool.tensor_tensor(hi, wd_raw[:, :, :], ones[:, 0:1].unsqueeze(1).to_broadcast([P, 2, D]),
                                           ALU.mult).then_inc(sem("wd_hi"), 1)
                        pool.wait_ge(sem("wd_hi"), g + 1)
                        pool.tensor_tensor(lo, wd_raw[:, :, :], f32(hi), ALU.subtract).then_inc(sem("wd_lo"), 1)

                    with pool.Fori(0, TURNS - 1, 1) as g:
                        up_tiles(g * 2, 1)
                        down_tile(g)
                        up_tiles(g * 2, 2)
                    up_tiles(KF - 2, 1)
                    down_tile(TURNS - 1)
                    for t in range(NT):
                        pool.wait_ge(sem(f"x1_in{t}"), 16)
                        pool.wait_ge(sem("out_scaled"), t + 1)
                        pool.tensor_tensor(X[t % len(X)], X[t % len(X)], out_tile(t), ALU.add).then_inc(sem("y"), 1)

                @block.tensor
                def _(pe):
                    def up(g, f):
                        for s in range(2):
                            wup.product(pe, g * 2 + f, s, KD, h, two_slots(ps, "wup", g * 2 + f, s))

                    def down(g):
                        pe.wait_ge(sem("ff_lo"), g * 2 + 3)
                        pe.wait_ge(sem("wd_lo"), g + 2)
                        for n in range(DOWNS):
                            t, half = n // 2, n % 2
                            pe.wait_ge(sem("down_free"), g * DOWNS + (n + 1))
                            for j, (a, b) in enumerate(PASSES):
                                for f in range(2):
                                    last = pe.matmul(pdn[:, half, :], ff[:, a, f, t * P:(t + 1) * P],
                                                     wd[:, b, f, half * HALF:(half + 1) * HALF],
                                                     start=(j == 0 and f == 0), stop=(j == 2 and f == 1))
                            last.then_inc(sem("down_mm"), 1)

                    up(0, 0)
                    up(0, 1)
                    with pe.Fori(1, TURNS, 1) as g:
                        up(g, 0)
                        down(g - 1)
                        up(g, 1)
                    pe.wait_ge(sem("conv_read"), KF + 1)
                    pe.wait_ge(sem("wup_pfree0"), KF + 1)
                    for n, (src, _) in enumerate(HISTORY):
                        last = pe.transpose(history_psum(n), src, ident[:, :])
                    last.then_inc(sem("history_T"), 1)
                    down(TURNS - 1)

                @block.scalar
                def _(act):
                    def hidden(g, f):
                        n = g * 2 + f
                        gate = ps[0]
                        wup.arrived(act, n, 0)
                        act.wait_ge(sem("conv_read"), n + 1)
                        act.activation(U[:, 2:2 + 2 * G].rearrange("p (g t) -> p g t", t=G), gate[:, 0:2, 0:G], ACT.Copy) \
                            .then_inc(sem("gate_rows"), 1)
                        act.activation(U[:, 2 + 2 * G:], gate[:, 2, 0:REST], ACT.Copy).then_inc(sem("gate_rows"), 1)
                        act.activation(Us[:, :, 2:], gate[:, 2, REST:G].rearrange("p (b t) -> p b t", t=LS), ACT.Copy) \
                            .then_inc(sem("wup_pfree0"), 1)
                        act.wait_ge(sem("conv_read"), n + 2)
                        act.activation(y[:, :], y[:, :], ACT.Silu).then_inc(sem("gate_silu"), 1)
                        act.wait_ge(sem("ff_full"), n + 1)
                        act.wait_ge(sem("down_mm"), g * DOWNS + 1)
                        act.activation(ff[:, 0, f, :], y[:, :], ACT.Copy).then_inc(sem("ff_hi"), 1)

                    with act.Fori(0, TURNS, 1) as g:
                        hidden(g, 0)
                        hidden(g, 1)
                    act.preload_act_table_set("natural_log_exp_and_others")
                    act.wait_ge(sem("history_T"), 1)
                    for n, (src, _) in enumerate(HISTORY):
                        act.activation(rows[0:src.shape[1], n, :], history_psum(n), ACT.Copy).then_inc(sem("history_rows"), 1)
                    link = Link(act, sem("out_norm"))
                    act.wait_ge(sem("ff_lo"), KF + 1)
                    for t in range(NT):
                        act.wait_ge(sem("down_free"), (TURNS - 1) * DOWNS + 2 * t + 2 + SLOTS)
                        link(act.activation(y[:, 0:D], out_tile(t), ACT.Square, accum_out=stat[:, t, 0:1]))
                        link(act.activation(stat[:, t, 1:2], stat[:, t, 0:1], ACT.Ln, scale=1.0 / D, bias=eps[:, :]))
                        act.activation(stat[:, t, 2:3], stat[:, t, 1:2], ACT.Exp, scale=-0.5).then_inc(sem("out_rstd"), 1)

                @block.vector
                def _(dve):
                    STEPS = 7

                    def hidden(g, f):
                        n = g * 2 + f
                        one = bass.ds(n, 1)
                        link = Link(dve, sem("mlp_step"), n * STEPS)
                        dve.tensor_scalar(Us[:, :, 0:2].unsqueeze(3), fst[:, :, :, one], 1.0, None, ALU.mult) \
                            .then_inc(sem("history"), 1)
                        link(dve.tensor_scalar(fw[:, :].unsqueeze(2), fcw[:, :, one], 1.0, None, ALU.mult))
                        dve.wait_ge(sem("history"), n + 1)
                        dve.wait_ge(sem("wup_pfree0"), n + 2)
                        dve.wait_ge(sem("ff_lo"), n + 1)
                        conv3(dve, link, U, Us, y, [fw[:, w:w + 1] for w in range(3)])
                        dve.tensor_scalar(nfs[:, :, :, one], Us[:, :, LS:].unsqueeze(3), 1.0, None, ALU.mult) \
                            .then_inc(sem("new_history"), 1)
                        dve.tensor_scalar(nfp[:, :, one], U[:, NP_:].unsqueeze(2), 1.0, None, ALU.mult) \
                            .then_inc(sem("conv_read"), 1)
                        wup.arrived(dve, n, 1)
                        dve.wait_ge(sem("gate_silu"), n + 1)
                        dve.tensor_tensor(by_group(y[:, :]), by_group(y[:, :]), groups(ps[1]), ALU.mult) \
                            .then_inc(sem("ff_full"), 1)
                        dve.wait_ge(sem("ff_full"), n + 1)
                        dve.sem_inc(sem("wup_pfree1"), 1)

                    def low(g, f):
                        dve.wait_ge(sem("ff_hi"), g * 2 + f + 1)
                        dve.tensor_tensor(ff[:, 1, f, :], y[:, :], f32(ff[:, 0, f, :]), ALU.subtract).then_inc(sem("ff_lo"), 1)

                    def add_part(g, n):
                        part = out_sum[:, n // 2, n % 2, :]
                        dve.wait_ge(sem("down_mm"), g * DOWNS + (n + 2))
                        dve.wait_ge(sem("down_free"), g * DOWNS + 2)
                        dve.tensor_tensor(part, part, pdn[:, n % 2, :], ALU.add).then_inc(sem("down_free"), 1)

                    def add_down(g):
                        for n in range(DOWNS):
                            add_part(g, n)

                    dve.memset(U[:, 0:2], 0.0).then_inc(sem("u_zero"), 1)
                    dve.wait_ge(sem("u_zero"), 1)
                    dve.memset(out_sum[:, :, :, :], 0.0).then_inc(sem("sum_zero"), 1)
                    dve.wait_ge(sem("sum_zero"), 1)
                    hidden(0, 0)
                    low(0, 0)
                    hidden(0, 1)
                    low(0, 1)
                    with dve.Fori(1, TURNS, 1) as g:
                        hidden(g, 0)
                        add_down(g - 1)
                        low(g, 0)
                        hidden(g, 1)
                        low(g, 1)

                    def scale_out(t):
                        dve.wait_ge(sem("out_rstd"), t + 1)
                        dve.scalar_tensor_tensor(out_tile(t), out_tile(t), stat[:, t, 2:3], gate[t // NPT], ALU.mult,
                                                 ALU.mult).then_inc(sem("out_scaled"), 1)

                    for t in range(NT):
                        add_part(TURNS - 1, 2 * t)
                        add_part(TURNS - 1, 2 * t + 1)
                        if t == 0:
                            dve.wait_ge(sem("gate_in"), 16 * (1 + NB))
                        else:
                            scale_out(t - 1)
                    scale_out(NT - 1)
        late.close()

_ORDER = ["x_prompt", "x_sample", "state_hgrn", "state_conv", "state_ffn_conv", "c_prompt", "c_sample", "w_ada",
          "b_ada", "g_pre_mix", "g_post_mix", "g_pre_ffn", "g_post_ffn", "w_in", "hgrn_lb_logits", "hgrn_norm",
          "w_pa", "conv_w", "w_pb", "w_bgate", "w_o", "w_up", "ffn_conv_w", "w_down"]


def output_shapes(shape):
    depth, batch, heads, dk, dv = shape["state_hgrn"]
    return {
        "y_prompt": shape["x_prompt"],
        "y_sample": shape["x_sample"],
        "hgrn_prompt": (depth, shape["x_prompt"][0], heads, dk, dv),
        "conv_prompt": (depth, shape["x_prompt"][0], *shape["state_conv"][2:]),
        "ffn_prompt": (depth, shape["x_prompt"][0], *shape["state_ffn_conv"][2:]),
        "hgrn_sample": shape["state_hgrn"],
        "conv_sample": shape["state_conv"],
        "ffn_sample": shape["state_ffn_conv"],
    }


def kernel(**inputs):
    import numpy as np
    import concourse.bacc as bacc
    from concourse.bass_utils import run_bass_kernel_spmd

    nc = bacc.Bacc("TRN2", target_bir_lowering=False, num_devices=1)
    arrays = {name: np.ascontiguousarray(inputs[name]) for name in _ORDER}
    io = {name: nc.dram_tensor(name, a.shape, F32, kind="ExternalInput").ap() for name, a in arrays.items()}
    outs = output_shapes({name: tuple(a.shape) for name, a in arrays.items()})
    for name, shape in outs.items():
        io[name] = nc.dram_tensor(name, tuple(shape), F32, kind="ExternalOutput").ap()
    build_trunk(nc, io)
    result = run_bass_kernel_spmd(nc, [arrays], core_ids=[0])
    return tuple(result.results[0][name] for name in outs)
```
